# Optimizing a Trainium2 kernel written in Bass

```python
import math
import jax, jax.numpy as jnp
from jax import lax
import numpy as np

D_MODEL = 1024
BATCH = 1
SEQ = 128
DEPTH = 1
DEC_BATCH = 1
DEC_SEQ = 512
PAST_LEN = 256

GRID_W = 64
H_Q = 8
H_KV = 2
HD = 128
ROPE_F = HD // 4
ROPE_THETA = 10000.0
Q_BLOCK = 128
D_INNER = 2 * D_MODEL
SSD_P = 64
H_SSD = D_INNER // SSD_P
SSD_G = 8
SSD_N = 128
CONV_K = 5
CHUNK = 128
D_FF = 4 * D_MODEL
ALPHA = (2.0 * DEPTH) ** 0.25
BETA = (8.0 * DEPTH) ** -0.25
EPS = 1e-6
Q_DIM = H_Q * HD
KV_DIM = H_KV * HD
BC_DIM = SSD_G * SSD_N
XBC_DIM = D_INNER + 2 * BC_DIM
DT_DIM = 2 * H_SSD
GATE_DIM = 2 * D_MODEL
IN_DIM = Q_DIM + 2 * KV_DIM + D_INNER + XBC_DIM + DT_DIM + GATE_DIM
SPLIT_IDX = [Q_DIM, Q_DIM + KV_DIM, Q_DIM + 2 * KV_DIM, Q_DIM + 2 * KV_DIM + D_INNER,
             Q_DIM + 2 * KV_DIM + D_INNER + XBC_DIM, Q_DIM + 2 * KV_DIM + D_INNER + XBC_DIM + DT_DIM]

kernel_name = "hybrid_gqa_ssd_diffusion_prefix_step"

def layer_norm(x, g=None, b=None):
    xf = x.astype(jnp.float32)
    mu = jnp.mean(xf, axis=-1, keepdims=True)
    var = jnp.mean(jnp.square(xf - mu), axis=-1, keepdims=True)
    y = (xf - mu) * lax.rsqrt(var + EPS)
    if g is not None:
        y = y * g.astype(jnp.float32) + b.astype(jnp.float32)
    return y.astype(x.dtype)

def rms_norm(x, g):
    xf = x.astype(jnp.float32)
    y = xf * lax.rsqrt(jnp.mean(jnp.square(xf), axis=-1, keepdims=True) + EPS)
    return (y * g.astype(jnp.float32)).astype(x.dtype)

def rope_tables(L):
    rows = L // GRID_W
    t = jnp.arange(rows * GRID_W)
    pos = jnp.stack([t // GRID_W, t % GRID_W], axis=-1).astype(jnp.float32)
    inv = ROPE_THETA ** (-jnp.arange(ROPE_F, dtype=jnp.float32) / ROPE_F)
    ang = pos[:, :, None] * inv
    return jnp.cos(ang), jnp.sin(ang)

def apply_rope(x, cos, sin):
    b, L, H, _ = x.shape
    xr = x.astype(jnp.float32).reshape(b, L, H, 2, 2, ROPE_F)
    x1, x2 = xr[..., 0, :], xr[..., 1, :]
    c = cos[None, :, None]
    s = sin[None, :, None]
    out = jnp.stack([x1 * c - x2 * s, x1 * s + x2 * c], axis=-2)
    return out.reshape(b, L, H, HD).astype(x.dtype)

def block_attention(q, k, v):
    b, L = q.shape[0], q.shape[1]
    nb = L // Q_BLOCK
    rep = H_Q // H_KV
    qb = q.reshape(b, nb, Q_BLOCK, H_KV, rep, HD).transpose(1, 0, 2, 3, 4, 5)
    scale = HD ** -0.5

    def one_block(qi):
        s = jnp.einsum('bqgrd,btgd->bgrqt', qi, k, preferred_element_type=jnp.float32) * scale
        p = jax.nn.softmax(s, axis=-1).astype(v.dtype)
        return jnp.einsum('bgrqt,btgd->bqgrd', p, v)

    o = lax.map(one_block, qb)
    return o.transpose(1, 0, 2, 3, 4, 5).reshape(b, L, Q_DIM)

def centred_depthwise_conv(x, w, bias):
    y = lax.conv_general_dilated(x, w.astype(x.dtype)[:, None, :], window_strides=(1,),
                                 padding=[(CONV_K // 2, CONV_K // 2)],
                                 dimension_numbers=('NWC', 'WIO', 'NWC'),
                                 feature_group_count=x.shape[-1])
    return y + bias.astype(x.dtype)

def ssd_chunked(x, dt, A, Bm, Cm, h0):
    b, L, H, P = x.shape
    G, N = Bm.shape[-2], Bm.shape[-1]
    R = H // G
    nc = L // CHUNK
    x = x.reshape(b, nc, CHUNK, G, R, P)
    dt = dt.reshape(b, nc, CHUNK, G, R)
    Bm = Bm.reshape(b, nc, CHUNK, G, N)
    Cm = Cm.reshape(b, nc, CHUNK, G, N)
    acs = lax.cumsum(dt * A.reshape(G, R), axis=2)
    acs_t = jnp.moveaxis(acs, 2, -1)
    seg = acs_t[..., :, None] - acs_t[..., None, :]
    mask = jnp.tril(jnp.ones((CHUNK, CHUNK), dtype=bool))
    decay = jnp.where(mask, jnp.exp(jnp.where(mask, seg, 0.0)), 0.0)
    cb = jnp.einsum('bcign,bcjgn->bcgij', Cm, Bm)
    y_diag = jnp.einsum('bcgij,bcgrij,bcjgr,bcjgrp->bcigrp', cb, decay, dt, x)
    decay_to_end = jnp.exp(acs[:, :, -1:] - acs)
    states = jnp.einsum('bcjgn,bcjgr,bcjgrp->bcgrpn', Bm, decay_to_end * dt, x)
    chunk_decay = jnp.exp(acs[:, :, -1])

    def step(h, inp):
        s, d = inp
        return d[..., None, None] * h + s, h

    h_final, h_prev = lax.scan(step, h0.reshape(b, G, R, P, N),
                               (jnp.moveaxis(states, 1, 0), jnp.moveaxis(chunk_decay, 1, 0)))
    h_prev = jnp.moveaxis(h_prev, 0, 1)
    y_off = jnp.einsum('bcign,bcigr,bcgrpn->bcigrp', Cm, jnp.exp(acs), h_prev)
    y = (y_diag + y_off).reshape(b, L, H, P)
    return y, h_final.reshape(b, H, P, N)

def mixer(h, p, rope, ctx_k, ctx_v, h0_f, h0_b):
    b, L, _ = h.shape
    proj = h @ p['w_in']
    q, k, v, z, xbc, dt, gates = jnp.split(proj, SPLIT_IDX, axis=-1)
    q = rms_norm(q.reshape(b, L, H_Q, HD), p['q_norm'])
    k = rms_norm(k.reshape(b, L, H_KV, HD), p['k_norm'])
    v = v.reshape(b, L, H_KV, HD)
    if rope is None:
        qr, kr = q, k
    else:
        cos, sin = rope
        qr, kr = apply_rope(q, cos, sin), apply_rope(k, cos, sin)
    if ctx_k is None:
        k_all, v_all = kr, v
    else:
        k_all = jnp.concatenate([ctx_k.astype(kr.dtype), kr], axis=1)
        v_all = jnp.concatenate([ctx_v.astype(v.dtype), v], axis=1)
    attn = block_attention(qr, k_all, v_all)
    xbc = jax.nn.silu(centred_depthwise_conv(xbc, p['conv_w'], p['conv_b']))
    xs, bm, cm = jnp.split(xbc, [D_INNER, D_INNER + BC_DIM], axis=-1)
    xs = xs.reshape(b, L, H_SSD, SSD_P).astype(jnp.float32)
    bm = bm.reshape(b, L, SSD_G, SSD_N).astype(jnp.float32)
    cm = cm.reshape(b, L, SSD_G, SSD_N).astype(jnp.float32)
    dt = dt.astype(jnp.float32)
    dt_bias = p['dt_bias'].astype(jnp.float32)
    a = -jnp.exp(p['a_log'].astype(jnp.float32))
    dt_f = jax.nn.softplus(dt[..., :H_SSD] + dt_bias[0])
    dt_b = jax.nn.softplus(dt[..., H_SSD:] + dt_bias[1])
    y_f, h_f = ssd_chunked(xs, dt_f, a[0], bm, cm, h0_f)
    flip = lambda t: jnp.flip(t, axis=1)
    y_b, h_b = ssd_chunked(flip(xs), flip(dt_b), a[1], flip(bm), flip(cm), h0_b)
    y = y_f + flip(y_b) + p['d_skip'].astype(jnp.float32)[:, None] * xs
    y = y.reshape(b, L, D_INNER).astype(h.dtype)
    y = rms_norm(y * jax.nn.silu(z), p['ssd_norm'])
    g_a, g_b = jnp.split(gates, 2, axis=-1)
    merged = jax.nn.sigmoid(g_a) * (attn @ p['w_attn_o']) + jax.nn.sigmoid(g_b) * (y @ p['w_ssd_o'])
    return merged @ p['w_out'], k, v, h_f, h_b

def trunk_layer(x, mod, p, rope, ctx_k, ctx_v, h0_f, h0_b):
    sh1, sc1, g1, sh2, sc2, g2 = [mod[:, i][:, None, :] for i in range(6)]
    h = layer_norm(x) * (1 + sc1) + sh1
    mix, k, v, h_f, h_b = mixer(h, p, rope, ctx_k, ctx_v, h0_f, h0_b)
    x = layer_norm(ALPHA * x + g1 * mix, p['ln1_g'], p['ln1_b'])
    h = layer_norm(x) * (1 + sc2) + sh2
    ff = jnp.square(jax.nn.relu(h @ p['w_mlp1'] + p['b_mlp1'])) @ p['w_mlp2'] + p['b_mlp2']
    x = layer_norm(ALPHA * x + g2 * ff, p['ln2_g'], p['ln2_b'])
    return x, k, v, h_f, h_b

def setup_inputs(seed: int = 0) -> dict:
    key = jax.random.key(seed)
    ks = jax.random.split(key, 32)
    f32 = jnp.float32
    nrm = lambda k, shape, s: jax.random.normal(k, shape, f32) * s
    dt0 = jnp.exp(jax.random.uniform(ks[11], (DEPTH, 2, H_SSD), f32, math.log(1e-3), math.log(1e-1)))
    return {
        "x_prompt": nrm(ks[0], (BATCH, SEQ, D_MODEL), 1.0),
        "x_sample": nrm(ks[1], (DEC_BATCH, DEC_SEQ, D_MODEL), 1.0),
        "cache_k": nrm(ks[2], (DEC_BATCH, DEPTH, PAST_LEN, H_KV, HD), 1.0),
        "cache_v": nrm(ks[3], (DEC_BATCH, DEPTH, PAST_LEN, H_KV, HD), 1.0),
        "state_ssd": nrm(ks[4], (DEC_BATCH, DEPTH, 2, H_SSD, SSD_P, SSD_N), 0.1),
        "c": nrm(ks[5], (DEC_BATCH, D_MODEL), 1.0),
        "c_ctx": nrm(ks[6], (D_MODEL,), 1.0),
        "w_mod": nrm(ks[7], (DEPTH, D_MODEL, 6 * D_MODEL), 0.5 * D_MODEL ** -0.5),
        "b_mod": nrm(ks[8], (DEPTH, 6 * D_MODEL), 0.01),
        "w_in": nrm(ks[9], (DEPTH, D_MODEL, IN_DIM), D_MODEL ** -0.5),
        "q_norm": 1.0 + nrm(ks[10], (DEPTH, HD), 0.05),
        "k_norm": 1.0 + nrm(ks[12], (DEPTH, HD), 0.05),
        "conv_w": nrm(ks[13], (DEPTH, CONV_K, XBC_DIM), CONV_K ** -0.5),
        "conv_b": nrm(ks[14], (DEPTH, XBC_DIM), 0.01),
        "a_log": jnp.log(jax.random.uniform(ks[15], (DEPTH, 2, H_SSD), f32, 1.0, 16.0)),
        "dt_bias": dt0 + jnp.log(-jnp.expm1(-dt0)),
        "d_skip": 1.0 + nrm(ks[16], (DEPTH, H_SSD), 0.05),
        "ssd_norm": 1.0 + nrm(ks[17], (DEPTH, D_INNER), 0.05),
        "w_attn_o": nrm(ks[18], (DEPTH, Q_DIM, D_MODEL), Q_DIM ** -0.5),
        "w_ssd_o": nrm(ks[19], (DEPTH, D_INNER, D_MODEL), D_INNER ** -0.5),
        "w_out": nrm(ks[20], (DEPTH, D_MODEL, D_MODEL), BETA * D_MODEL ** -0.5),
        "ln1_g": 1.0 + nrm(ks[21], (DEPTH, D_MODEL), 0.05),
        "ln1_b": nrm(ks[22], (DEPTH, D_MODEL), 0.01),
        "w_mlp1": nrm(ks[23], (DEPTH, D_MODEL, D_FF), D_MODEL ** -0.5),
        "b_mlp1": nrm(ks[24], (DEPTH, D_FF), 0.01),
        "w_mlp2": nrm(ks[25], (DEPTH, D_FF, D_MODEL), BETA * D_FF ** -0.5),
        "b_mlp2": nrm(ks[26], (DEPTH, D_MODEL), 0.01),
        "ln2_g": 1.0 + nrm(ks[27], (DEPTH, D_MODEL), 0.05),
        "ln2_b": nrm(ks[28], (DEPTH, D_MODEL), 0.01),
    }

def reference(x_prompt, x_sample, cache_k, cache_v, state_ssd, c, c_ctx, w_mod, b_mod, w_in,
              q_norm, k_norm, conv_w, conv_b, a_log, dt_bias, d_skip, ssd_norm, w_attn_o, w_ssd_o,
              w_out, ln1_g, ln1_b, w_mlp1, b_mlp1, w_mlp2, b_mlp2, ln2_g, ln2_b):
    rope = rope_tables(x_sample.shape[1])
    y_p = x_prompt
    y_s = x_sample
    ks_l, vs_l, ss_l = [], [], []
    for l in range(DEPTH):
        p = dict(w_in=w_in[l], q_norm=q_norm[l], k_norm=k_norm[l], conv_w=conv_w[l], conv_b=conv_b[l],
                 a_log=a_log[l], dt_bias=dt_bias[l], d_skip=d_skip[l], ssd_norm=ssd_norm[l],
                 w_attn_o=w_attn_o[l], w_ssd_o=w_ssd_o[l], w_out=w_out[l], ln1_g=ln1_g[l], ln1_b=ln1_b[l],
                 w_mlp1=w_mlp1[l], b_mlp1=b_mlp1[l], w_mlp2=w_mlp2[l], b_mlp2=b_mlp2[l],
                 ln2_g=ln2_g[l], ln2_b=ln2_b[l])
        mod_ctx = (jax.nn.silu(c_ctx) @ w_mod[l] + b_mod[l]).reshape(1, 6, D_MODEL)
        mod_lat = (jax.nn.silu(c) @ w_mod[l] + b_mod[l]).reshape(c.shape[0], 6, D_MODEL)
        zeros = jnp.zeros((y_p.shape[0], H_SSD, SSD_P, SSD_N), jnp.float32)
        y_p, k_l, v_l, hf, hb = trunk_layer(y_p, mod_ctx, p, None, None, None, zeros, zeros)
        ks_l.append(k_l)
        vs_l.append(v_l)
        ss_l.append(jnp.stack([hf, hb], axis=1).astype(x_prompt.dtype))
        y_s, _, _, _, _ = trunk_layer(y_s, mod_lat, p, rope, cache_k[:, l], cache_v[:, l],
                                      state_ssd[:, l, 0].astype(jnp.float32),
                                      state_ssd[:, l, 1].astype(jnp.float32))
    new_cache_k = jnp.stack(ks_l, axis=1)
    new_cache_v = jnp.stack(vs_l, axis=1)
    new_state_ssd = jnp.stack(ss_l, axis=1)
    return (y_p, y_s, new_cache_k, new_cache_v, new_state_ssd)


_drawn_inputs = setup_inputs


def setup_inputs(seed=0):
    import zlib

    import numpy as np

    out = dict(_drawn_inputs(seed))
    spreads = {}
    factors = {'cache_k': 8.0,
     'cache_v': 8.0,
     'state_ssd': 5.745,
     'q_norm': 8.0,
     'conv_b': 3.717,
     'd_skip': 8.0,
     'ssd_norm': 8.0,
     'w_attn_o': 2.683,
     'ln1_b': 5.608,
     'b_mlp1': 23.764,
     'b_mlp2': 21.62,
     'ln2_b': 5.483}
    for name, (base, spread) in spreads.items():
        noise = np.random.default_rng([zlib.crc32(name.encode()), seed]).standard_normal(out[name].shape)
        drawn = base * np.exp(spread * noise) if base else spread * noise
        out[name] = __import__('jax').numpy.asarray(drawn.astype(out[name].dtype))
    for name, factor in factors.items():
        out[name] = (out[name] * factor).astype(out[name].dtype)
    return out
```

```python
import math
from contextlib import ExitStack, contextmanager

import concourse.bass as bass
from concourse import mybir

F32 = mybir.dt.float32
F32R = mybir.dt.float32r
ACT = mybir.ActivationFunctionType
ALU = mybir.AluOpType
AX = mybir.AxisListType

P = 128
D = 1024
KT = D // P
CTX, LAT, PAST = 128, 512, 256
NT = (CTX + LAT) // P
HQ, HKV, HD = 8, 2, 128
DI = 2 * D
NH, SP_ = 32, 64
NG, NS = 8, 128
R = NH // NG
BC = NG * NS
XBC = DI + 2 * BC
DFF = 4 * D
TAPS = 5
ALPHA = 2.0 ** 0.25
EPS = 1e-6
SCALE = HD ** -0.5
C_Q = 0
C_Z = HQ * HD + 2 * HKV * HD
C_XBC = C_Z + DI
C_DT = C_XBC + XBC
C_G = C_DT + 2 * NH
TP = CTX + 2 + LAT + 2
HALF = TP // 2
NCONV = CTX + 2 + LAT
BW = 256
K_ID, K_LE, K_GE, K_GT, K_LT, K_ONE, K_COS, K_SIN = (P * n for n in (0, 1, 2, 3, 4, 5, 6, 10))
K_ALL = 14 * P
GRID_W, ROPE_THETA = 64, 10000.0
Q_CONV, Q_CB, Q_SN, Q_B1, Q_BM, Q_C = 0, 160, 192, 208, 240, 288
Q_ALL = 304


def tok(t):
    return 0 if t == 0 else 2 + t * P


def count(sem, step=1, start=0):
    return {"sem": sem, "step": step, "base": start, "k": 0, "round": None, "per": 0}


def value(c, back=0):
    v = c["step"] * (c["base"] + c["k"] - back)
    assert v > 0, "a wait stands where there is something to wait for"
    return v if c["round"] is None else c["round"] * (c["per"] * c["step"]) + v


def step(c, n=1):
    c["k"] += n
    return c["step"]


def due(c, back=0):
    step(c)
    return value(c, back)


def some(c, back=0):
    n = c["base"] + c["k"] - back
    assert c["round"] is None or n > 0, "in a loop every round waits"
    return n > 0


def jump(c, n):
    c["base"], c["k"] = n, 0


@contextmanager
def rounds(eng, n, *counts):
    with eng.Fori(0, n) as i:
        for c, per in counts:
            c["base"], c["k"], c["round"], c["per"] = c["base"] + c["k"], 0, i, per
        yield i
        for c, per in counts:
            assert c["k"] == per, f"{c['sem']}: {c['k']} signals in a round, not {per}"
    for c, per in counts:
        c["base"], c["k"], c["round"] = c["base"] + n * per, 0, None


def build(nc, a, outs):
    y_p, y_s, out_k, out_v, out_st = outs
    scratch = lambda n, shape: nc.dram_tensor(n, shape, F32, kind="Internal").ap()
    xs_d = scratch("xs_nat", (NT, P, DI))
    bn_d = scratch("b_nat", (NT, P, BC))
    bct_d = scratch("bc_t", (NT, P, 2 * NG, P))
    z_d = scratch("z_silu", (NT, P, DI))
    g_d = scratch("gates_t", (2 * KT, P, TP))
    hb_d = scratch("h_back", (NT, P, DI))
    m1_d = scratch("attention_branch", (KT, P, TP))
    gr_d = scratch("gate_rows", (2, KT, 2, P))

    with ExitStack() as ctx:
        def sb(n, shape, dt=F32):
            return ctx.enter_context(nc.sbuf_tensor(n, shape, dt))

        def sem(n):
            return ctx.enter_context(nc.semaphore(n))

        raw = sb("raw", [P, 2, KT, BW])
        whi = sb("whi", [P, 2, KT, BW], F32R)
        yctx = nc.alloc_sbuf_tensor_at("y_context", [P, DI], F32, offset=nc.sbuf_base - 4 * KT * BW)
        wlo = sb("wlo", [P, 2, KT, BW], F32R)
        hh = sb("hh", [P, KT, TP], F32R)
        y13 = nc.alloc_sbuf_tensor_at("y_tiles_1_3", [P, 2 * DI], F32, offset=nc.sbuf_base - 4 * KT * TP)
        hl = sb("hl", [P, KT, TP], F32R)
        y24 = nc.alloc_sbuf_tensor_at("y_tiles_2_4", [P, 2 * DI], F32, offset=nc.sbuf_base - 4 * KT * TP)
        cst = sb("cst", [P, K_ALL])
        colp = sb("colp", [P, Q_ALL])
        siluc = sb("siluc", [P, 2 * KT])
        modc = sb("modc", [P, 6 * KT, 2])
        dts = sb("dts", [P, NT, 2 * NH])
        dta = sb("dta", [P, NT, 2 * NH])
        dec = sb("dec", [P, NT, 3, 2 * NH])
        sdt = sb("sdt", [P, NT, 2 * NH])
        wdh = sb("wdh", [P, KT, 2 * NH], F32R)
        wdl = sb("wdl", [P, KT, 2 * NH], F32R)
        st6 = sb("st6", [P, 2, 6])
        mv = sb("mv", [P, NT, 4])
        dsk = sb("dsk", [P, NH])
        opened = sb("opened", [1, 8])
        grow = sb("grow", [2 * KT, 2, P])
        A0 = -(-nc.sbuf_base // 64) * 64
        AR = (nc.sbuf_top - A0) // 4
        arena = nc.alloc_sbuf_tensor_at("arena", [P, AR], F32, offset=A0)
        ident = cst[:, K_ID:K_ID + P]
        mask = lambda k: cst[:, k:k + P]

        class Carve:

            def __init__(self, at=0):
                self.at = at

            def __call__(self, *shape):
                n = math.prod(shape)
                v = arena[:, self.at:self.at + n]
                self.at += n
                assert self.at <= AR, (self.at, AR)
                if len(shape) == 1:
                    return v
                names = "abcd"[:len(shape)]
                return v.rearrange(f"p ({' '.join(names)}) -> p {' '.join(names)}",
                                   **{x: y for x, y in zip(names[1:], shape[1:])})

        c0 = Carve()
        xin = c0(NT, D)
        prow = c0(4, P)
        hf = c0(2, TP)
        c1 = Carve()
        mraw = c1(2, KT, BW)
        xpad = c1(2, TP + 2)
        cvo = c1(2, NCONV)
        cvs = c1(2, NCONV)
        nst = c1(2, NT, P)
        wdt = c1(KT, 2 * NH)
        dtb = c1(2 * NH)
        alg = c1(2 * NH)
        dtu = c1(3, NT, 2 * NH)
        base = Carve()
        rq = base(NT, (HQ + HKV) * HD)
        vn = base(NT, HKV * HD)
        vc = base(PAST // P, HKV * HD)
        kcr = base(PAST // P, HKV * HD)
        c2 = Carve(base.at)
        q5 = c2(2, NT, BW)
        t5 = c2(NT, BW)
        u5 = c2(NT, BW)
        nrow = c2(2, HD)
        ms = c2(NT, 2)
        c3 = Carve(base.at)
        zst = c3(2, NT, BW)
        gst = c3(2, TP)
        c4 = Carve(base.at)
        qT = c4(HQ + HKV, NT * P)
        kcT = c4(HKV, PAST)
        pr = c4(2, LAT + PAST)
        pT = c4(2, (LAT + PAST) // P, LAT)
        sm = c4(2, 16)
        c4b = Carve(base.at)
        gat = c4b(2, TP)
        ast = c4b(2, TP)
        c5 = Carve()
        xs0, bn0, bc0 = c5(NH, SP_), c5(NG, NS), c5(2 * NG, P)
        rawf = raw[:].rearrange("p s k n -> p (s k n)")
        xs1 = rawf[:, 0:DI].rearrange("p (h q) -> p h q", q=SP_)
        bc1 = rawf[:, DI:2 * DI].rearrange("p (g t) -> p g t", t=P)
        bn1 = c5(NG, NS)
        xs_s, bn_s, bc_s = (xs0, xs1), (bn0, bn1), (bc0, bc1)
        zc = c5(DI)
        ysb = (y13, y24)
        xdf, xdb, xwf = (c5(2, 8, SP_) for _ in range(3))
        xwb = cst[:, K_COS:K_COS + 8 * P].rearrange("p (s h q) -> p s h q", h=8, q=SP_)
        rr = c5(2, 2, R, P)
        ee = c5(2, R, P)
        mm = c5(2, 2, R, P)
        cbm = c5(2, NG, P)
        yy = c5(NH, SP_)
        hF = c5(NH, SP_)
        hB = c5(NH, SP_)
        tq = c5(8, SP_)
        YW = 2 * KT * TP
        yh = nc.alloc_sbuf_tensor_at("yh", [P, 2 * KT, TP], F32R, offset=A0)
        yl = nc.alloc_sbuf_tensor_at("yl", [P, 2 * KT, TP], F32R, offset=A0 + 4 * YW)
        c6 = Carve(2 * YW)
        gbt = c6(TP)
        m1t = c6(TP)
        mrg = c6(TP)
        c7 = Carve()
        fh = nc.alloc_sbuf_tensor_at("fh", [P, KT, TP], F32R, offset=A0)
        fl = nc.alloc_sbuf_tensor_at("fl", [P, KT, TP], F32R, offset=A0 + 2 * YW)
        c8 = Carve(YW)
        x1 = c8(NT, D)
        xo = c8(NT, D)
        g1r = c8(2, D)
        row = c8(D)
        hf2 = c8(2, TP)
        lnr = c7(2, D)
        kout = c2(HKV * HD)
        xq = c7(NT, D)
        acc = ctx.enter_context(nc.psum_tensor("acc", [P, 4, 512], F32))
        tp = ctx.enter_context(nc.psum_tensor("tp", [P, 4, 512], F32))
        modp = tp[:, 2, 0:4 * KT].rearrange("p (b c) -> p b c", c=2)
        names = """rows_in rows_turned colp_ok silu_ok x_in xn_ok hi_of_h h_ok modc_ok mod_used mraw_used
            raw_in0 raw_in1 mraw_in0 mraw_in1 hi_done lo_done w_half acc_ready acc_free
            dve_step act_step xpad_zero conv_ok conv_silu turned turned_free
            nat_out0 nat_out1 conv_out0 conv_out1 dt_in dt_split dt_hi dt_mm dt_abs dt_soft dt_sums dt_exp dt_ok
            qkv_in rot_ok out_kv zst_out0 zst_out1 gst_out0 gst_out1
            score_ready max_ok exp_ok prob_ok pv_ready att_hi att_ok gat_in0 gat_in1 ast_out0 ast_out1
            chunk_in0 chunk_in1 z_in hb_in dsk_in h0_in h0_turned h0_ok cb_ready cb_ok rise_ok seg_ready e_ok m_ok
            xd_ok group_ready states_ready carried_ok quad_ok sq_in sq_ok chunk_ok hb_out st_copied st_out
            kout_ok qk_turned qk_copied p_turned p_copied back_ready back_ok xwb_ok mod_copied pad_ok dt_summed var_ok dev_ok
            y_turned y_hi y_ok gm_in merge_free merge_sum merge_hi merge_ok
            gate_turned gate_copied gate_out rows2_in x1_ok h2_hi h2_ok relu_ok square_ok ff_ok final_ok out_done
            bcopy""".split()
        s = {n: ctx.enter_context(nc.semaphore(n)) for n in names}
        OPEN = ("nat_out", "conv_out", "zst_out", "gst_out")
        pair = lambda n: [count(s[n + b], 16, 1 if n in OPEN else 0) for b in "01"]
        W = lambda ap: ap.rearrange("(k p) n -> p k n", p=P)
        w_mod, w_in = W(a["w_mod"][0]), W(a["w_in"][0])
        w_ao, w_so, w_out = W(a["w_attn_o"][0]), W(a["w_ssd_o"][0]), W(a["w_out"][0])
        w_1, w_2 = W(a["w_mlp1"][0]), W(a["w_mlp2"][0])
        block = ctx.enter_context(nc.Block())
        U_XBC = KT
        U_QKV = U_XBC + 2 * XBC // BW
        U_Z = U_QKV + 6 * NT
        U_G = U_Z + DI // BW * NT
        U_AO = U_G + 2 * 2 * D // BW
        U_SO = U_AO + KT
        U_OUT = U_SO + KT
        U_H2 = U_OUT + 4 * NT
        U_MLP = U_H2 + KT
        B_QKV = XBC // BW
        B_AO = B_QKV + 6 + DI // BW + 2 * D // BW
        B_SO = B_AO + 4
        B_OUT = B_SO + 8
        B_MLP = B_OUT + 4
        N_SCORE = LAT // P * HQ
        ORDER_ = [0, 4, 3, 2, 1, 2, 3, 4]

        RX, RB, RC = DI // P // 4, BC // P // 4, BC // P // 4
        NKC = PAST // P

        @block.sync
        def _(sp):
            sp.dma_start(cst[:], a["consts"]).then_inc(s["rows_in"], 16)
            cw = a["conv_w"][0].rearrange("t (c p) -> (t c) p", p=P)
            rows = lambda ap: ap.rearrange("o (c p) -> (o c) p", p=P)
            sp.dma_start(prow[:, 0], cw[0:P]).then_inc(s["rows_in"], 16)
            sp.dma_start(prow[0:32, 1], cw[P:160]).then_inc(s["rows_in"], 16)
            sp.dma_start(prow[32:64, 1], rows(a["conv_b"])).then_inc(s["rows_in"], 16)
            sp.dma_start(prow[64:80, 1], rows(a["ssd_norm"])).then_inc(s["rows_in"], 16)
            sp.dma_start(prow[80:112, 1], rows(a["b_mlp1"])).then_inc(s["rows_in"], 16)
            sp.dma_start(prow[0:48, 2], rows(a["b_mod"])).then_inc(s["rows_in"], 16)
            sp.dma_start(prow[0:8, 3], a["c_ctx"].rearrange("(c p) -> c p", p=P)).then_inc(s["rows_in"], 16)
            sp.dma_start(prow[8:16, 3], rows(a["c"])).then_inc(s["rows_in"], 16)
            raws, mraws = pair("raw_in"), pair("mraw_in")
            mod_used, lo, mru = count(s["mod_used"]), count(s["lo_done"]), count(s["mraw_used"])

            def load(slot, src):
                sp.dma_start(raw[:, slot], src).then_inc(raws[slot]["sem"], step(raws[slot]))

            for r in range(8):
                step(mod_used)
                if some(mod_used, 2):
                    sp.wait_ge(mod_used["sem"], value(mod_used, 2))
                load(r % 2, w_mod[:, :, r * BW:(r + 1) * BW])
                if r == 1:
                    sp.dma_start(xin[:, 0], a["x_prompt"][0]).then_inc(s["x_in"], 16)
                    sp.dma_start(xin[:, 1:NT], a["x_sample"][0].rearrange("(t p) d -> p t d", p=P)).then_inc(s["x_in"], 16)
            for b in range(2):
                step(mod_used)
                if some(mod_used, 2):
                    sp.wait_ge(mod_used["sem"], value(mod_used, 2))
                load(b, w_in[:, :, C_XBC + b * BW:C_XBC + (b + 1) * BW])
                step(lo)
            sp.wait_ge(s["h_ok"], KT)
            for b in range(2):
                sp.dma_start(mraw[:, b], w_mod[:, :, (8 + b) * BW:(9 + b) * BW]).then_inc(mraws[b]["sem"], step(mraws[b]))
                step(mru)
            sp.dma_start(wdt, w_in[:, :, C_DT:C_DT + 2 * NH]).then_inc(s["dt_in"], 16)
            sp.dma_start(dtb, a["dt_bias"].rearrange("o a h -> o (a h)")[0].partition_broadcast(P)).then_inc(s["dt_in"], 16)
            sp.dma_start(alg, a["a_log"].rearrange("o a h -> o (a h)")[0].partition_broadcast(P)).then_inc(s["dt_in"], 16)
            with rounds(sp, RX + RB + RC - 1, (raws[0], 1), (raws[1], 1), (mraws[0], 1), (mraws[1], 1),
                        (lo, 2), (mru, 2)) as i:
                for b in range(2):
                    step(lo)
                    if some(lo, 2):
                        sp.wait_ge(lo["sem"], value(lo, 2))
                    load(b, w_in[:, :, bass.ds(i * (2 * BW) + (C_XBC + (b + 2) * BW), BW)])
                for b in range(2):
                    step(mru)
                    if some(mru, 2):
                        sp.wait_ge(mru["sem"], value(mru, 2))
                    sp.dma_start(mraw[:, b], w_mod[:, :, bass.ds(i * (2 * BW) + (10 + b) * BW, BW)]).then_inc(mraws[b]["sem"], step(mraws[b]))

            def stream(n, src, col, wait=True):
                with rounds(sp, n, (raws[0], 1), (raws[1], 1), (lo, 2)) as i:
                    for b in range(2):
                        step(lo)
                        if some(lo, 2):
                            sp.wait_ge(lo["sem"], value(lo, 2))
                        load(b, src[:, :, bass.ds(i * (2 * BW) + (col + b * BW), BW)])

            for b in range(2):
                step(lo)
                if some(lo, 2):
                    sp.wait_ge(lo["sem"], value(lo, 2))
                load(b, w_in[:, :, b * BW:(b + 1) * BW])
            sp.wait_ge(s["dt_ok"], 1)
            for c in pair("nat_out"):
                step(c, 2 * (RX + RB))
                sp.wait_ge(c["sem"], value(c))
            for c in pair("conv_out"):
                step(c, 2 * 2 * (RB + RC))
                sp.wait_ge(c["sem"], value(c))
            hk = lambda ap: ap[0, 0].rearrange("(t p) h d -> p t (h d)", p=P)
            sp.dma_start(kcr, hk(a["cache_k"])).then_inc(s["qkv_in"], 16)
            sp.dma_start(vc, hk(a["cache_v"])).then_inc(s["qkv_in"], 16)
            sp.dma_start(nrow[:, 0], a["q_norm"][0].partition_broadcast(P)).then_inc(s["qkv_in"], 16)
            sp.dma_start(nrow[:, 1], a["k_norm"][0].partition_broadcast(P)).then_inc(s["qkv_in"], 16)
            stream(2, w_in, 2 * BW)
            stream(4, w_in, C_Z)
            stream(4, w_in, C_G)
            stream(2, w_ao, 0)
            sp.wait_ge(s["att_ok"], HQ + HKV)
            gat_in = pair("gat_in")
            for k in range(KT):
                if k >= 2:
                    sp.wait_ge(s["acc_free"], U_AO + k - 1)
                sp.dma_start(gat[:, k % 2], g_d[k]).then_inc(gat_in[k % 2]["sem"], step(gat_in[k % 2]))

            flat = lambda t: t.rearrange("p h q -> p (h q)")
            cin = pair("chunk_in")
            ORDER = [0, 4, 3, 2, 1, 2, 3, 4]

            def chunk_in(j):
                slot, c = j % 2, ORDER[j]
                if j >= 2:
                    sp.wait_ge(s["chunk_ok"], j - 1)
                sp.dma_start(flat(xs_s[slot]), xs_d[c]).then_inc(cin[slot]["sem"], step(cin[slot]))
                sp.dma_start(flat(bn_s[slot]), bn_d[c]).then_inc(cin[slot]["sem"], step(cin[slot]))
                sp.dma_start(flat(bc_s[slot]), bct_d[c].rearrange("p g t -> p (g t)")).then_inc(cin[slot]["sem"], step(cin[slot]))

            sp.wait_ge(s["acc_free"], U_SO)
            for c in pair("ast_out"):
                step(c, KT // 2)
                sp.wait_ge(c["sem"], value(c))
            sp.wait_ge(s["lo_done"], B_SO)
            sp.dma_start(dsk[:], a["d_skip"][0].partition_broadcast(P)).then_inc(s["dsk_in"], 16)
            chunk_in(0)
            sp.dma_start(zc, z_d[0]).then_inc(s["z_in"], 16)
            chunk_in(1)
            sp.wait_ge(s["chunk_ok"], 1)
            for d, buf in ((0, flat(yy)), (1, zc)):
                h0 = a["state_ssd"][0, 0, d].rearrange("(j h) q n -> (h q) j n", h=2)
                sp.dma_start(buf.rearrange("p (j n) -> p j n", n=NS), h0).then_inc(s["h0_in"], 16)
            for j in range(2, 5):
                chunk_in(j)
            sp.wait_ge(s["h0_turned"], 8)
            for j in range(4, 8):
                sp.wait_ge(s["chunk_ok"], j)
                if j == 4:
                    sp.wait_ge(s["hb_out"], 16 * 4)
                sp.dma_start(flat(hB), hb_d[j - 3]).then_inc(s["hb_in"], 16)
                sp.dma_start(zc, z_d[j - 3]).then_inc(s["z_in"], 16)
                if j < 7:
                    chunk_in(j + 1)

            sp.wait_ge(s["chunk_ok"], 8)
            jump(lo, B_SO)

            def load_so(c, wait):
                for b in range(2):
                    if wait:
                        step(lo)
                        if some(lo, 2):
                            sp.wait_ge(lo["sem"], value(lo, 2))
                    else:
                        step(lo)
                    load(b, w_so[:, b * KT:(b + 1) * KT,
                                 bass.ds(c * BW, BW)])

            load_so(0, False)
            with rounds(sp, 3, (raws[0], 1), (raws[1], 1), (lo, 2)) as i:
                for b in range(2):
                    step(lo)
                    if some(lo, 2):
                        sp.wait_ge(lo["sem"], value(lo, 2))
                    load(b, w_so[:, b * KT:(b + 1) * KT, bass.ds(i * BW + BW, BW)])
            stream(2, w_out, 0)
            sp.wait_ge(s["merge_ok"], KT)
            sp.wait_ge(s["acc_ready"], U_OUT)
            sp.wait_ge(s["gate_out"], 32)
            for n in range(2):
                sp.dma_start(g1r[:, n].rearrange("p (k c) -> p k c", c=P), gr_d[0, :, n].partition_broadcast(P)).then_inc(s["rows2_in"], 16)
            sp.dma_start(xo[:, 0], a["x_prompt"][0]).then_inc(s["rows2_in"], 16)
            sp.dma_start(xo[:, 1:NT], a["x_sample"][0].rearrange("(t p) d -> p t d", p=P)).then_inc(s["rows2_in"], 16)
            sp.dma_start(lnr[:, 0], a["ln1_g"][0].partition_broadcast(P)).then_inc(s["rows2_in"], 16)
            sp.dma_start(lnr[:, 1], a["ln1_b"][0].partition_broadcast(P)).then_inc(s["rows2_in"], 16)
            sp.dma_start(row, a["b_mlp2"][0].partition_broadcast(P)).then_inc(s["rows2_in"], 16)

            for b in range(2):
                step(lo)
                if some(lo, 2):
                    sp.wait_ge(lo["sem"], value(lo, 2))
                load(b, w_1[:, :, b * BW:(b + 1) * BW])
            with rounds(sp, 3, (raws[0], 4), (raws[1], 4), (lo, 8)) as i:
                for b in range(2, 4):
                    step(lo)
                    if some(lo, 2):
                        sp.wait_ge(lo["sem"], value(lo, 2))
                    load(b % 2, w_1[:, :, bass.ds(i * D + b * BW, BW)])
                for b in range(4):
                    step(lo)
                    if some(lo, 2):
                        sp.wait_ge(lo["sem"], value(lo, 2))
                    load(b % 2, w_2[:, bass.ds(i * KT, KT), b * BW:(b + 1) * BW])
                for b in range(2):
                    step(lo)
                    if some(lo, 2):
                        sp.wait_ge(lo["sem"], value(lo, 2))
                    load(b, w_1[:, :, bass.ds(i * D + (D + b * BW), BW)])
            for b in range(2, 4):
                step(lo)
                if some(lo, 2):
                    sp.wait_ge(lo["sem"], value(lo, 2))
                load(b % 2, w_1[:, :, 3 * D + b * BW:3 * D + (b + 1) * BW])
            for b in range(4):
                step(lo)
                if some(lo, 2):
                    sp.wait_ge(lo["sem"], value(lo, 2))
                load(b % 2, w_2[:, 3 * KT:4 * KT, b * BW:(b + 1) * BW])
            sp.wait_ge(s["h2_ok"], KT)
            for n in range(2):
                sp.dma_start(g1r[:, n].rearrange("p (k c) -> p k c", c=P), gr_d[1, :, n].partition_broadcast(P)).then_inc(s["rows2_in"], 16)
            sp.wait_ge(s["acc_free"], U_MLP + 4 * (KT + 4 * NT))
            sp.dma_start(lnr[:, 0], a["ln2_g"][0].partition_broadcast(P)).then_inc(s["rows2_in"], 16)
            sp.dma_start(lnr[:, 1], a["ln2_b"][0].partition_broadcast(P)).then_inc(s["rows2_in"], 16)
            for t in range(NT):
                sp.wait_ge(s["final_ok"], t + 1)
                dst = y_p[0] if t == 0 else y_s[0, (t - 1) * P:t * P]
                sp.dma_start(dst, xo[:, t]).then_inc(s["out_done"], 16)
            sp.wait_ge(s["out_done"], 16 * NT)

        @block.gpsimd
        def _(po):
            for j, n in enumerate(n + b for n in OPEN for b in "01"):
                po.dma_start(opened[0:1, j:j + 1], a["d_skip"][0:1, 0:1]).then_inc(s[n], 16)
            nat_out, conv_out = pair("nat_out"), pair("conv_out")
            turned, silu = count(s["turned_free"]), count(s["conv_silu"])
            step(turned)

            def store_turned(u, dst):
                po.wait_ge(turned["sem"], due(turned))
                po.dma_start(dst, nst[:, u]).then_inc(nat_out[u]["sem"], step(nat_out[u]))

            def store_conv(u, g):
                po.wait_ge(silu["sem"], due(silu))
                to = bct_d[:, :, g]
                po.dma_start(to[0], cvs[:, u, 0:P]).then_inc(conv_out[u]["sem"], step(conv_out[u]))
                po.dma_start(to[1:NT].rearrange("c p o t -> p c (o t)"),
                                                cvs[:, u, 2 + P:NCONV].rearrange("p (c t) -> p c t", t=P)).then_inc(conv_out[u]["sem"], step(conv_out[u]))

            nat = lambda t, col: t.rearrange("t p c -> p t c")[:, :, bass.ds(col, P)]
            with rounds(po, RX, (turned, 4), (silu, 4), (nat_out[0], 2), (nat_out[1], 2)) as i:
                for n in range(4):
                    step(silu)
                    store_turned(n % 2, nat(xs_d, i * (4 * P) + n * P))
            with rounds(po, RB, (turned, 4), (silu, 4), (nat_out[0], 2), (nat_out[1], 2), (conv_out[0], 4), (conv_out[1], 4)) as i:
                for n in range(4):
                    store_conv(n % 2, bass.ds(i * 4 + n, 1))
                    store_turned(n % 2, nat(bn_d, i * (4 * P) + n * P))
            with rounds(po, RC, (silu, 4), (conv_out[0], 4), (conv_out[1], 4)) as i:
                for n in range(4):
                    store_conv(n % 2, bass.ds(i * 4 + (NG + n), 1))
            po.wait_ge(s["kout_ok"], 1)
            po.dma_start(out_k[0, 0].rearrange("t h d -> t (h d)"), kout).then_inc(s["out_kv"], 16)
            free = count(s["acc_free"])
            jump(free, U_Z)
            po.wait_ge(free["sem"], value(free))
            po.dma_start(out_v[0, 0].rearrange("t h d -> t (h d)"), vn[:, 0]).then_inc(s["out_kv"], 16)
            zo, go = pair("zst_out"), pair("gst_out")
            with rounds(po, 4, (free, 2 * NT), (zo[0], 1), (zo[1], 1)) as i:
                for b in range(2):
                    step(free, NT)
                    po.wait_ge(free["sem"], value(free))
                    po.dma_start(z_d.rearrange("t p c -> p t c")[:, :, bass.ds(i * (2 * BW) + b * BW, BW)], zst[:, b]).then_inc(zo[b]["sem"], step(zo[b]))
            with rounds(po, 4, (free, 4), (go[0], 2), (go[1], 2)) as i:
                for n in range(4):
                    po.wait_ge(free["sem"], due(free))
                    po.dma_start(g_d[bass.ds(i * 4 + n, 1)].rearrange("o p t -> p (o t)"), gst[:, n % 2]).then_inc(go[n % 2]["sem"], step(go[n % 2]))
            ao = pair("ast_out")
            with rounds(po, 2, (free, 4), (ao[0], 2), (ao[1], 2)) as i:
                for n in range(4):
                    po.wait_ge(free["sem"], due(free))
                    po.dma_start(m1_d[bass.ds(i * 4 + n, 1)].rearrange("o p t -> p (o t)"), ast[:, n % 2]).then_inc(ao[n % 2]["sem"], step(ao[n % 2]))
            flat = lambda t: t.rearrange("p h q -> p (h q)")
            po.wait_ge(s["st_copied"], 8)
            for d, buf in ((0, hF), (1, hB)):
                dst = out_st[0, 0, d].rearrange("(j h) q n -> (h q) j n", h=2)
                po.dma_start(dst, flat(buf).rearrange("p (j n) -> p j n", n=NS)).then_inc(s["st_out"], 16)
            po.wait_ge(s["h0_ok"], 8)
            po.dma_start(hb_d[NT - 1], flat(hB)).then_inc(s["hb_out"], 16)
            for j in range(1, 4):
                po.wait_ge(s["chunk_ok"], j + 1)
                po.dma_start(hb_d[NT - 1 - j], flat(hB)).then_inc(s["hb_out"], 16)
            po.wait_ge(s["chunk_ok"], 8)
            for k in range(KT):
                if k:
                    po.wait_ge(s["merge_sum"], k)
                po.dma_start(gbt, g_d[KT + k]).then_inc(s["gm_in"], 16)
                po.dma_start(m1t, m1_d[k]).then_inc(s["gm_in"], 16)
            for n in range(2):
                po.wait_ge(s["gate_copied"], n + 1)
                po.dma_start(gr_d[n].rearrange("k c p -> (k c) p"), grow[:, n]).then_inc(s["gate_out"], 16)
            po.wait_ge(s["out_kv"], 32)
            po.wait_ge(s["gate_out"], 32)

        @block.tensor
        def _(pe):
            lo, ready, free = count(s["lo_done"]), count(s["acc_ready"]), count(s["acc_free"])
            raws, mraws = pair("raw_in"), pair("mraw_in")
            mod_used, mru = count(s["mod_used"]), count(s["mraw_used"])
            turned, tfree, silu = count(s["turned"]), count(s["turned_free"]), count(s["conv_silu"])
            mcopied = count(s["mod_copied"])

            def mul(out, l, r, first=True, last=True):
                return pe.matmul(out, l, r, start=first, stop=last)

            pe.wait_ge(s["rows_in"], 16 * 9)
            for j, n, q in ((0, P, Q_CONV), (1, 112, P), (2, 48, Q_BM), (3, 16, Q_C)):
                last = pe.transpose(tp[:, 0, q:q + n], prow[0:n, j], ident[0:n, 0:n])
            last.then_inc(s["rows_turned"], 1)

            def mod_block(w, out):
                for sub in range(2):
                    for k in range(KT):
                        last = mul(out[:, sub], w[:, k, sub * P:(sub + 1) * P], siluc[:, k:2 * KT:KT],
                                   k == 0, k == KT - 1)
                return last

            pe.wait_ge(s["silu_ok"], 1)
            for r in range(8):
                pe.wait_ge(raws[r % 2]["sem"], due(raws[r % 2]))
                mod_block(raw[:, r % 2], modp[:, 2 * r:2 * r + 2]).then_inc(mod_used["sem"], step(mod_used))

            def turn_x(src, ok, n):
                pe.wait_ge(s[ok], n)
                for k in range(KT):
                    step(free)
                    if some(free, 2):
                        pe.wait_ge(free["sem"], value(free, 2))
                    u = k % 2
                    for t in range(NT):
                        dst = acc[:, 2 * u + 1, 0:P] if t == 0 else acc[:, 2 * u, (t - 1) * P:t * P]
                        last = pe.transpose(dst, src[:, t, k * P:(k + 1) * P], ident)
                    last.then_inc(ready["sem"], step(ready))

            turn_x(xin, "xn_ok", NT)

            def t_pass(slot, sub, u, mh, ml, k0=0, first=True, end=True):
                for k in range(KT):
                    for w, m in ((whi, mh), (whi, ml), (wlo, mh)):
                        for half in range(2):
                            last = mul(acc[:, 2 * u + half, 0:HALF], w[:, slot, k, sub * P:(sub + 1) * P],
                                       m[:, k0 + k, half * HALF:(half + 1) * HALF],
                                       first and k == 0 and w is whi and m is mh, end and k == KT - 1 and w is wlo)
                return last

            def t_unit(slot, sub, u, mh, ml):
                step(free)
                if some(free, 2):
                    pe.wait_ge(free["sem"], value(free, 2))
                t_pass(slot, sub, u, mh, ml).then_inc(ready["sem"], step(ready))

            def n_block(slot, mh, ml):
                for t in range(NT):
                    u = (NT * slot + t) % 2
                    step(free)
                    if some(free, 2):
                        pe.wait_ge(free["sem"], value(free, 2))
                    for k in range(KT):
                        for m, w in ((mh, whi), (mh, wlo), (ml, whi)):
                            last = mul(acc[:, 2 * u, 0:BW], m[:, k, tok(t):tok(t) + P], w[:, slot, k],
                                       k == 0 and w is whi and m is mh, k == KT - 1 and m is ml)
                    last.then_inc(ready["sem"], step(ready))

            def turn_tile(n):
                pe.wait_ge(silu["sem"], due(silu))
                step(tfree)
                if some(tfree, 1):
                    pe.wait_ge(tfree["sem"], value(tfree, 1))
                for t in range(NT):
                    dst = tp[:, 1, 0:P] if t == 0 else tp[:, 0, (t - 1) * P:t * P]
                    last = pe.transpose(dst, cvs[:, n % 2, tok(t):tok(t) + P], ident)
                last.then_inc(turned["sem"], step(turned))

            def xbc_round(turning):
                for n in range(4):
                    if n % 2 == 0:
                        pe.wait_ge(lo["sem"], due(lo))
                    t_unit(n // 2, n % 2, n % 2, hh, hl)
                    if turning and n:
                        turn_tile(n - 1)
                for b in range(2):
                    pe.wait_ge(mraws[b]["sem"], due(mraws[b]))
                    if b == 0:
                        step(mcopied)
                        if some(mcopied, 1):
                            pe.wait_ge(mcopied["sem"], value(mcopied, 1))
                    mod_block(mraw[:, b], tp[:, 2 + b, 0:4].rearrange("p (b c) -> p b c", c=2)).then_inc(mru["sem"], step(mru))
                if turning:
                    turn_tile(3)

            pe.wait_ge(s["h_ok"], KT)
            step(tfree)
            step(mcopied)
            every = [(lo, 2), (ready, 4), (free, 4), (mraws[0], 1), (mraws[1], 1), (mru, 2), (mcopied, 1)]
            with rounds(pe, RX + RB, *every, (turned, 4), (tfree, 4), (silu, 4)):
                xbc_round(True)
            with rounds(pe, RC, *every):
                xbc_round(False)

            pe.wait_ge(s["dt_split"], 1)
            pe.wait_ge(mcopied["sem"], value(mcopied))
            pe.wait_ge(tfree["sem"], value(tfree))
            for t in range(NT):
                for k in range(KT):
                    for m, w in ((hh, wdh), (hh, wdl), (hl, wdh)):
                        last = mul(tp[:, 0, t * 2 * NH:(t + 1) * 2 * NH], m[:, k, tok(t):tok(t) + P], w[:, k],
                                   k == 0 and w is wdh and m is hh, k == KT - 1 and m is hl)
            last.then_inc(s["dt_mm"], 1)
            pe.wait_ge(s["dt_sums"], 1)
            for j, (f, b) in enumerate(((K_LE, K_GE), (K_GT, K_LT), (K_ONE, K_ONE))):
                o = tp[:, 1 + j, 0:NT * 2 * NH].rearrange("p (t h) -> p t h", t=NT)
                mul(o[:, :, 0:NH], mask(f), dta[:, :, 0:NH])
                last = mul(o[:, :, NH:], mask(b), dta[:, :, NH:])
            last.then_inc(s["dt_summed"], 1)

            n_each = [(lo, 2), (ready, 2 * NT), (free, 2 * NT)]
            t_each = [(lo, 2), (ready, 4), (free, 4)]

            def n_stream(n, mh, ml):
                with rounds(pe, n, *n_each):
                    for b in range(2):
                        pe.wait_ge(lo["sem"], due(lo))
                        n_block(b, mh, ml)

            def t_stream(n, mh, ml):
                with rounds(pe, n, *t_each):
                    for u in range(4):
                        if u % 2 == 0:
                            pe.wait_ge(lo["sem"], due(lo))
                        t_unit(u // 2, u % 2, u % 2, mh, ml)

            n_stream(3, hh, hl)
            n_stream(4, hh, hl)
            t_stream(4, hh, hl)

            pe.wait_ge(s["dt_ok"], 1)
            pe.wait_ge(s["rot_ok"], 5)
            pe.wait_ge(s["qkv_in"], 64)
            turned = count(s["qk_turned"])
            tfree = count(s["qk_copied"])

            def turn_qk(src, n):
                step(tfree)
                if some(tfree, 1):
                    pe.wait_ge(tfree["sem"], value(tfree, 1))
                src().then_inc(turned["sem"], step(turned))

            def q_tiles(h):
                for t in range(NT):
                    dst = tp[:, 1, 0:P] if t == 0 else tp[:, 0, (t - 1) * P:t * P]
                    last = pe.transpose(dst, rq[:, t, h * HD:(h + 1) * HD], ident)
                return last

            def cached_tiles():
                for h in range(HKV):
                    for t in range(NKC):
                        j = h * NKC + t
                        last = pe.transpose(tp[:, 0, j * P:(j + 1) * P], kcr[:, t, h * HD:(h + 1) * HD], ident)
                return last

            for h in range(HQ + HKV):
                turn_qk(lambda: q_tiles(h), h)
            turn_qk(cached_tiles, HQ + HKV)
            pe.wait_ge(free["sem"], value(free))
            score, prob = count(s["score_ready"]), count(s["prob_ok"])
            expd, pv, pvf = count(s["exp_ok"]), count(s["pv_ready"]), count(s["att_ok"])
            pt_turned, pt_free = count(s["p_turned"]), count(s["p_copied"])
            pe.wait_ge(tfree["sem"], value(tfree))

            def scores(n):
                u = n % 2
                if n < N_SCORE:
                    h, t = n // 4, n % 4
                    step(expd)
                    if some(expd, 2):
                        pe.wait_ge(expd["sem"], value(expd, 2))
                    q = qT[:, h, t * P:(t + 1) * P]
                    mul(acc[:, 2 * u, 0:LAT], q, qT[:, HQ + h // R, 0:LAT])
                    last = mul(acc[:, 2 * u + 1, 0:PAST], q, kcT[:, h // R])
                else:
                    g = n - N_SCORE
                    step(expd)
                    if some(expd, 2):
                        pe.wait_ge(expd["sem"], value(expd, 2))
                    for r in range(R):
                        last = mul(acc[:, 2 * u, r * P:(r + 1) * P], qT[:, R * g + r, LAT:], qT[:, HQ + g, LAT:])
                last.then_inc(score["sem"], step(score))

            def turn_p(n):
                u = n % 2
                pe.wait_ge(prob["sem"], due(prob))
                step(pt_free)
                if some(pt_free, 1):
                    pe.wait_ge(pt_free["sem"], value(pt_free, 1))
                for j in range(6 if n < N_SCORE else R):
                    last = pe.transpose(tp[:, j // 4, (j % 4) * P:(j % 4 + 1) * P], pr[:, u, j * P:(j + 1) * P], ident)
                last.then_inc(pt_turned["sem"], step(pt_turned))

            def values(h):
                step(pvf)
                if some(pvf, 2):
                    pe.wait_ge(pvf["sem"], value(pvf, 2))
                o = tp[:, 2 + h % 2]
                if h < HQ:
                    pe.wait_ge(s["p_copied"], 4 * (h + 1))
                    for j in range(6):
                        v = (vn[:, 1 + j] if j < 4 else vc[:, j - 4])[:, (h // R) * HD:(h // R + 1) * HD]
                        last = mul(o, v, pT[:, h % 2, j], j == 0, j == 5)
                else:
                    g = h - HQ
                    pe.wait_ge(s["p_copied"], N_SCORE + g + 1)
                    last = mul(o, vn[:, 0, g * HD:(g + 1) * HD], pT[:, h % 2, 0])
                last.then_inc(pv["sem"], step(pv))

            scores(0)
            scores(1)
            for n in range(N_SCORE + HKV):
                if n + 2 < N_SCORE + HKV:
                    scores(n + 2)
                turn_p(n)
                if n % 4 == 1 and 4 < n < N_SCORE:
                    values(n // 4 - 1)
            values(HQ - 1)
            values(HQ)
            values(HQ + 1)

            pe.wait_ge(pvf["sem"], value(pvf))
            t_stream(2, hh, hl)

            cin = pair("chunk_in")
            cbr, cbo, rise, seg, e_ok = (count(s[n]) for n in ("cb_ready", "cb_ok", "rise_ok", "seg_ready", "e_ok"))
            m_ok, xd, grp, quad, qok = (count(s[n]) for n in ("m_ok", "xd_ok", "group_ready", "states_ready", "quad_ok"))
            car = count(s["carried_ok"])
            hbin, stc = count(s["hb_in"], 16), count(s["st_copied"])

            def seg_group(slot, g):
                pe.wait_ge(rise["sem"], due(rise))
                step(e_ok)
                if some(e_ok, 2):
                    pe.wait_ge(e_ok["sem"], value(e_ok, 2))
                mul(acc[:, g % 2], mask(K_GT), rr[:, g % 2, 0].rearrange("p r t -> p (r t)"), True, False)
                mul(acc[:, g % 2], mask(K_LT), rr[:, g % 2, 1].rearrange("p r t -> p (r t)"), False, True).then_inc(seg["sem"], step(seg))

            def scan_chunk(slot, latent):
                x, b, bc = xs_s[slot], bn_s[slot], bc_s[slot]
                step(cin[slot], 3)
                pe.wait_ge(cin[slot]["sem"], value(cin[slot]))
                if latent:
                    pe.wait_ge(qok["sem"], value(qok))
                for g in range(NG):
                    last = mul(tp[:, g // 4, (g % 4) * P:(g % 4 + 1) * P], bc[:, g], bc[:, NG + g])
                last.then_inc(cbr["sem"], step(cbr))
                seg_group(slot, 0)
                seg_group(slot, 1)
                if latent:
                    pe.wait_ge(hbin["sem"], due(hbin))
                for g in range(NG):
                    q, gg = g // 2, g % 2
                    if g + 2 < NG:
                        seg_group(slot, g + 2)
                    yb, sbk = (acc[:, 2], acc[:, 3]) if q % 2 == 0 else (tp[:, 0], tp[:, 1])
                    if gg == 0:
                        pe.wait_ge(xd["sem"], due(xd))
                        states(q, sbk, b, bc, latent)
                    pe.wait_ge(m_ok["sem"], due(m_ok))
                    if gg == 0:
                        step(qok)
                        if some(qok, 2):
                            pe.wait_ge(qok["sem"], value(qok, 2))
                    for r in range(R):
                        j = gg * R + r
                        mul(yb[:, j * SP_:(j + 1) * SP_], mm[:, g % 2, 0, r], xdf[:, q % 2, j], True, False)
                        last = mul(yb[:, j * SP_:(j + 1) * SP_], mm[:, g % 2, 1, r], xdb[:, q % 2, j], False, True)
                    last.then_inc(grp["sem"], step(grp))

            def states(q, sbk, b, bc, latent):
                if latent:
                    step(car)
                    if some(car, 1):
                        pe.wait_ge(car["sem"], value(car, 1))
                else:
                    if some(stc):
                        pe.wait_ge(stc["sem"], value(stc))
                    step(stc, 2)
                for k in (0, 1):
                    w = slice(k * R * SP_, (k + 1) * R * SP_)
                    gk = 2 * q + k
                    heads = slice(gk * R, (gk + 1) * R)
                    if latent:
                        mul(tp[:, 2, w], bc[:, NG + gk], hF[:, heads])
                        mul(tp[:, 3, w], bc[:, NG + gk], hB[:, heads])
                        last = mul(sbk[:, w], b[:, gk], xwf[:, q % 2, k * R:(k + 1) * R])
                    else:
                        for h in (0, 2):
                            j = k * R + h
                            mul(sbk[:, j * SP_:j * SP_ + P], xwf[:, q % 2, j:j + 2], b[:, gk])
                            last = mul(tp[:, 2, j * SP_:j * SP_ + P], xwb[:, q % 2, j:j + 2], b[:, gk])
                last.then_inc(quad["sem"], step(quad))

            pe.wait_ge(s["acc_free"], U_SO)
            scan_chunk(0, False)
            step(car, 4)
            pe.wait_ge(s["h0_in"], 32)
            pe.wait_ge(qok["sem"], value(qok))
            pe.wait_ge(stc["sem"], value(stc))
            h0t, h0c = count(s["h0_turned"]), count(s["h0_ok"])
            for d, buf in ((0, yy.rearrange("p h q -> p (h q)")), (1, zc)):
                for j in range(4):
                    u = (4 * d + j) % 2
                    step(h0c)
                    if some(h0c, 2):
                        pe.wait_ge(h0c["sem"], value(h0c, 2))
                    for n in range(4):
                        c = 4 * j + n
                        last = pe.transpose(tp[:, u, n * P:(n + 1) * P], buf[:, c * P:(c + 1) * P], ident)
                    last.then_inc(h0t["sem"], step(h0t))
            bst, bfree, xwo = count(s["back_ready"]), count(s["back_ok"]), count(s["xwb_ok"])
            for j in range(1, 4):
                step(cin[j % 2], 3)
                pe.wait_ge(cin[j % 2]["sem"], value(cin[j % 2]))
                for q in range(4):
                    pe.wait_ge(xwo["sem"], due(xwo))
                    step(bfree)
                    if some(bfree, 2):
                        pe.wait_ge(bfree["sem"], value(bfree, 2))
                    for k in range(2):
                        last = mul(acc[:, 2 + q % 2, k * R * SP_:(k + 1) * R * SP_], bn_s[j % 2][:, 2 * q + k],
                                   xwb[:, q % 2, k * R:(k + 1) * R])
                    last.then_inc(bst["sem"], step(bst))
            pe.wait_ge(bfree["sem"], value(bfree))
            pe.wait_ge(h0c["sem"], value(h0c))
            every = [(cin[0], 3), (cin[1], 3), (cbr, 2), (rise, 16), (e_ok, 16), (seg, 16), (m_ok, 16), (grp, 16),
                     (qok, 8), (car, 8), (quad, 8), (xd, 8), (hbin, 2)]
            with rounds(pe, 2, *every):
                for b in range(2):
                    scan_chunk(b, True)

            pe.wait_ge(s["chunk_ok"], 8)
            yt, yc = count(s["y_turned"]), count(s["y_ok"])
            for t in range(NT):
                for j in range(4):
                    step(yc)
                    if some(yc, 4):
                        pe.wait_ge(yc["sem"], value(yc, 4))
                    for n in range(4):
                        c = (4 * j + n) * P
                        src = yctx if t == 0 else ysb[(t - 1) % 2][:, (t - 1) // 2 * DI:]
                        last = pe.transpose(tp[:, j, n * P:(n + 1) * P], src[:, c:c + P], ident)
                    last.then_inc(yt["sem"], step(yt))
            pe.wait_ge(yc["sem"], value(yc))
            half = count(s["w_half"])
            with rounds(pe, 4, (lo, 2), (ready, 2), (free, 2), (half, 1)):
                pe.wait_ge(lo["sem"], due(lo))
                for sub in range(2):
                    step(free)
                    if some(free, 2):
                        pe.wait_ge(free["sem"], value(free, 2))
                    last = t_pass(0, sub, sub, yh, yl, 0, True, False)
                last.then_inc(half["sem"], step(half))
                pe.wait_ge(lo["sem"], due(lo))
                for sub in range(2):
                    t_pass(1, sub, sub, yh, yl, KT, False, True).then_inc(ready["sem"], step(ready))
            pe.wait_ge(s["merge_ok"], KT)
            for n, c in ((0, 2), (1, 5)):
                last = pe.transpose(tp[0:2 * KT, 2, n * P:(n + 1) * P],
                                    modc[:, c * KT:(c + 1) * KT].rearrange("p k c -> p (k c)"), ident)
            last.then_inc(s["gate_turned"], 1)
            n_stream(2, hh, hl)
            turn_x(xq, "x1_ok", NT)
            pe.wait_ge(s["h2_ok"], KT)
            ff = count(s["ff_ok"])
            with rounds(pe, 4, (lo, 8), (ready, KT + 4 * NT), (free, KT + 4 * NT), (ff, KT)):
                for n in range(KT):
                    if n % 2 == 0:
                        pe.wait_ge(lo["sem"], due(lo))
                    t_unit(n // 2 % 2, n % 2, n % 2, hh, hl)
                for n in range(KT):
                    pe.wait_ge(ff["sem"], due(ff))
                for b in range(4):
                    pe.wait_ge(lo["sem"], due(lo))
                    n_block(b % 2, fh, fl)

        @block.scalar
        def _(act):
            steps = count(s["act_step"])
            ready, free = count(s["acc_ready"]), count(s["acc_free"])
            hi, lo = count(s["hi_done"]), count(s["lo_done"])
            raws = pair("raw_in")

            def split_hi(slot):
                act.wait_ge(raws[slot]["sem"], due(raws[slot]))
                act.activation(whi[:, slot], raw[:, slot], ACT.Copy).then_inc(hi["sem"], step(hi))

            var, dev = count(s["var_ok"]), count(s["dev_ok"])

            def roots(ap):
                act.wait_ge(var["sem"], due(var))
                act.activation(ap, ap, ACT.Sqrt).then_inc(dev["sem"], step(dev))

            def out_of_acc(dst, src, func):
                act.wait_ge(ready["sem"], due(ready))
                act.activation(dst, src, func).then_inc(free["sem"], step(free))

            act.wait_ge(s["rows_turned"], 1)
            act.wait_ge(s["turned_free"], 1)
            act.activation(siluc[:], tp[:, 0, Q_C:Q_C + 2 * KT], ACT.Silu).then_inc(s["silu_ok"], 1)

            def modulated(ok, buf, hi_ok, lo_ok, sc, sh):
                h, l = count(s[hi_ok]), count(s[lo_ok])
                for k in range(KT):
                    u = k % 2
                    act.wait_ge(ready["sem"], due(ready))
                    step(l)
                    if some(l, 2):
                        act.wait_ge(l["sem"], value(l, 2))
                    for m, (dst, src) in enumerate(((buf[:, u, 0:CTX], acc[:, 2 * u + 1, 0:CTX]),
                                                    (buf[:, u, CTX + 2:NCONV], acc[:, 2 * u, 0:LAT]))):
                        last = act.activation(dst, src, ACT.Identity, bias=modc[:, sh * KT + k, m:m + 1],
                                              scale=modc[:, sc * KT + k, m:m + 1])
                    last.then_inc(free["sem"], step(free))
                    act.wait_ge(free["sem"], value(free))
                    act.activation(hh[:, k], buf[:, u], ACT.Copy).then_inc(h["sem"], step(h))

            roots(mv[:, :, 2])
            act.wait_ge(s["mod_copied"], 1)
            act.wait_ge(s["pad_ok"], 1)
            modulated(None, hf, "hi_of_h", "h_ok", 1, 0)
            for c in raws:
                step(c, 4)
            split_hi(0)
            split_hi(1)

            conv, silu = count(s["conv_ok"]), count(s["conv_silu"])
            turned, tfree = count(s["turned"]), count(s["turned_free"])
            nat_out, conv_out = pair("nat_out"), pair("conv_out")
            step(tfree)

            def evacuate(n):
                act.wait_ge(padded["sem"], due(padded))
                out_of_acc(xpad[:, n % 2, 2:2 + TP].rearrange("p (a b) -> p a b", a=2),
                           acc[:, 2 * (n % 2):2 * (n % 2) + 2, 0:HALF], ACT.Copy)

            def smooth(n, stored):
                act.wait_ge(conv["sem"], due(conv))
                if stored:
                    act.wait_ge(conv_out[n % 2]["sem"], value(conv_out[n % 2]))
                    step(conv_out[n % 2], 2)
                act.activation(cvs[:, n % 2], cvo[:, n % 2], ACT.Silu).then_inc(silu["sem"], step(silu))

            def turned_out(n):
                act.wait_ge(turned["sem"], due(turned))
                step(nat_out[n % 2])
                if some(nat_out[n % 2], 1):
                    act.wait_ge(nat_out[n % 2]["sem"], value(nat_out[n % 2], 1))
                act.activation(nst[:, n % 2, 0], tp[:, 1, 0:P], ACT.Copy)
                act.activation(nst[:, n % 2, 1:NT].rearrange("p t c -> p (t c)"), tp[:, 0], ACT.Copy).then_inc(tfree["sem"], step(tfree))

            def xbc_round(turning, stored):
                for n in range(4):
                    evacuate(n)
                    if n % 2 == 1:
                        split_hi(n // 2)
                    if turning and n:
                        turned_out(n - 1)
                    smooth(n, stored)
                if turning:
                    turned_out(3)

            padded = count(s["conv_ok"])
            step(conv, 2)
            act.wait_ge(s["h_ok"], KT)
            every = [(ready, 4), (free, 4), (hi, 2), (raws[0], 1), (raws[1], 1), (conv, 4), (padded, 4), (silu, 4)]
            turning = [(turned, 4), (tfree, 4), (nat_out[0], 2), (nat_out[1], 2)]
            storing = [(conv_out[0], 4), (conv_out[1], 4)]
            with rounds(act, RX, *every, *turning):
                xbc_round(True, False)
            with rounds(act, RB, *every, *turning, *storing):
                xbc_round(True, True)
            with rounds(act, RC, *every, *storing):
                xbc_round(False, True)

            act.wait_ge(s["dt_in"], 48)
            act.activation(wdh[:], wdt, ACT.Copy).then_inc(s["dt_hi"], 1)
            act.activation(alg, alg, ACT.Exp).then_inc(steps["sem"], step(steps))
            act.wait_ge(s["dt_abs"], 1)
            act.activation(dtu[:, 1], dtu[:, 0], ACT.Exp, scale=-1.0).then_inc(steps["sem"], step(steps))
            act.wait_ge(steps["sem"], value(steps))
            act.activation(dtu[:, 1], dtu[:, 1], ACT.Ln, bias=1.0).then_inc(s["dt_soft"], 1)
            act.wait_ge(s["dt_summed"], 1)
            act.activation(dec[:].rearrange("p t j h -> p j t h"),
                           tp[:, 1:4, 0:NT * 2 * NH].rearrange("p j (t h) -> p j t h", t=NT), ACT.Exp).then_inc(s["dt_exp"], 1)

            for c in nat_out + conv_out:
                act.wait_ge(c["sem"], value(c))
            act.wait_ge(s["dt_ok"], 1)
            rot = count(s["rot_ok"])

            def block_out(b, dst, func):
                for t in range(NT):
                    out_of_acc(dst[:, t], acc[:, 2 * ((NT * b + t) % 2), 0:BW], func)
                split_hi(b)

            for n in range(5):
                step(rot)
                if some(rot, 2):
                    act.wait_ge(rot["sem"], value(rot, 2))
                block_out(n % 2, q5[:, n % 2], ACT.Copy)
                roots(ms.rearrange("p t h -> p (t h)"))
            block_out(1, vn, ACT.Copy)

            act.wait_ge(s["rot_ok"], 5)
            act.wait_ge(s["out_kv"], 32)
            zo, go = pair("zst_out"), pair("gst_out")
            with rounds(act, 4, (ready, 2 * NT), (free, 2 * NT), (hi, 2), (raws[0], 1), (raws[1], 1), (zo[0], 1), (zo[1], 1)):
                for b in range(2):
                    step(zo[b])
                    if some(zo[b], 1):
                        act.wait_ge(zo[b]["sem"], value(zo[b], 1))
                    block_out(b, zst[:, b], ACT.Silu)
            with rounds(act, 4, (ready, 4), (free, 4), (hi, 2), (raws[0], 1), (raws[1], 1), (go[0], 2), (go[1], 2)):
                for n in range(4):
                    step(go[n % 2])
                    if some(go[n % 2], 1):
                        act.wait_ge(go[n % 2]["sem"], value(go[n % 2], 1))
                    out_of_acc(gst[:, n % 2].rearrange("p (a b) -> p a b", a=2),
                               acc[:, 2 * (n % 2):2 * (n % 2) + 2, 0:HALF], ACT.Sigmoid)
                    if n % 2 == 1:
                        split_hi(n // 2)
            for c in zo + go:
                act.wait_ge(c["sem"], value(c))

            qt, qc = count(s["qk_turned"]), count(s["qk_copied"])
            for h in range(HQ + HKV):
                act.wait_ge(qt["sem"], due(qt))
                act.activation(qT[:, h, LAT:], tp[:, 1, 0:P], ACT.Copy)
                act.activation(qT[:, h, 0:LAT], tp[:, 0], ACT.Copy).then_inc(qc["sem"], step(qc))
            act.wait_ge(qt["sem"], due(qt))
            act.activation(kcT.rearrange("p h t -> p (h t)"), tp[:, 0], ACT.Copy).then_inc(qc["sem"], step(qc))
            mx, ex = count(s["max_ok"]), count(s["exp_ok"])
            ptt, ptc, pv = count(s["p_turned"]), count(s["p_copied"]), count(s["pv_ready"])
            ahi = count(s["att_hi"])

            def exps(n):
                u = n % 2
                act.wait_ge(mx["sem"], due(mx))
                if n >= 2:
                    act.wait_ge(s["p_turned"], n - 1)
                if n < N_SCORE:
                    sc = acc[:, 2 * u:2 * u + 2].rearrange("p a b -> p (a b)")[:, 0:LAT + PAST]
                    act.activation(pr[:, u], sc, ACT.Exp, bias=sm[:, u, 0:1], scale=SCALE,
                                             accum_out=sm[:, u, 4:5]).then_inc(ex["sem"], step(ex))
                else:
                    for r in range(R):
                        last = act.activation(pr[:, u, r * P:(r + 1) * P], acc[:, 2 * u, r * P:(r + 1) * P], ACT.Exp,
                                              bias=sm[:, u, r:r + 1], scale=SCALE, accum_out=sm[:, u, 4 + r:5 + r])
                    last.then_inc(ex["sem"], step(ex))

            def probs_out(n):
                act.wait_ge(ptt["sem"], due(ptt))
                if n < N_SCORE:
                    h, t = n // 4, n % 4
                    if h >= 2:
                        act.wait_ge(s["pv_ready"], h - 1)
                    act.activation(pT[:, h % 2, :, t * P:(t + 1) * P],
                                              tp[:, 0:2].rearrange("p a b -> p (a b)")[:, 0:LAT + PAST]
                                              .rearrange("p (j q) -> p j q", q=P), ACT.Copy).then_inc(ptc["sem"], step(ptc))
                else:
                    h = HQ + n - N_SCORE
                    act.wait_ge(s["pv_ready"], h - 1)
                    act.activation(pT[:, h % 2, 0], tp[:, 0], ACT.Copy).then_inc(ptc["sem"], step(ptc))

            def att_out(h):
                act.wait_ge(pv["sem"], due(pv))
                if h < HQ:
                    act.activation(hh[:, h, CTX + 2:NCONV], tp[:, 2 + h % 2], ACT.Copy).then_inc(ahi["sem"], step(ahi))
                else:
                    g = h - HQ
                    act.activation(hh[:, R * g:R * g + R, 0:CTX],
                                              tp[:, 2 + h % 2].rearrange("p (r t) -> p r t", r=R), ACT.Copy).then_inc(ahi["sem"], step(ahi))

            exps(0)
            for n in range(N_SCORE + HKV):
                if n + 1 < N_SCORE + HKV:
                    exps(n + 1)
                if n == N_SCORE + 1:
                    att_out(HQ - 1)
                probs_out(n)
                if n % 4 == 1 and 4 < n < N_SCORE:
                    att_out(n // 4 - 1)
            att_out(HQ)
            att_out(HQ + 1)

            for b in range(2):
                step(ready, 2)
                act.wait_ge(ready["sem"], value(ready))
                split_hi(b)
            step(ready, 4)

            seg, e_ok, m_ok = count(s["seg_ready"]), count(s["e_ok"]), count(s["m_ok"])
            quad, stc, sqi, sqo = (count(s[n]) for n in ("states_ready", "st_copied", "sq_in", "sq_ok"))
            act.wait_ge(s["acc_free"], U_SO)
            for c in pair("ast_out"):
                step(c, KT // 2)
                act.wait_ge(c["sem"], value(c))
            flat = lambda t: t.rearrange("p h q -> p (h q)")

            def decays(g):
                act.wait_ge(seg["sem"], due(seg))
                step(m_ok)
                if some(m_ok, 2):
                    act.wait_ge(m_ok["sem"], value(m_ok, 2))
                act.activation(ee[:, g % 2].rearrange("p r t -> p (r t)"), acc[:, g % 2], ACT.Exp).then_inc(e_ok["sem"], step(e_ok))

            def states_out(q):
                act.wait_ge(quad["sem"], due(quad))
                for d, (buf, bank) in enumerate(((hF, acc[:, 3] if q % 2 == 0 else tp[:, 1]), (hB, tp[:, 2]))):
                    act.activation(flat(buf)[:, q * 512:(q + 1) * 512], bank, ACT.Copy).then_inc(stc["sem"], step(stc))

            def squares():
                act.wait_ge(sqi["sem"], due(sqi))
                act.activation(zc, flat(yy), ACT.Square, accum_out=mv[:, 0, 0:1]).then_inc(sqo["sem"], step(sqo))

            def rises(c, g):
                if some(seg_r, 1):
                    act.wait_ge(seg_r["sem"], value(seg_r, 1))
                step(seg_r)
                for j, m in enumerate((K_LE, K_GE)):
                    for r in range(R):
                        h = j * NH + R * g + r
                        last = act.activation(rr[:, g % 2, j, r], mask(m), ACT.Copy,
                                              scale=dta[:, bass.ds(c, 1), h:h + 1].rearrange("p o h -> p (o h)"))
                last.then_inc(rise["sem"], step(rise))

            rise, seg_r = count(s["rise_ok"]), count(s["seg_ready"])
            rises(0, 0)
            rises(0, 1)
            for g in range(NG):
                decays(g)
                if g + 2 < NG:
                    rises(0, g + 2)
                if g >= 2 and g % 2 == 0:
                    states_out(g // 2 - 1)
            states_out(3)
            squares()
            roots(mv[:, 0, 2:3])
            act.wait_ge(s["st_out"], 32)
            h0t, h0c = count(s["h0_turned"]), count(s["h0_ok"])
            for d, buf in enumerate((hF, hB)):
                for j in range(4):
                    act.wait_ge(h0t["sem"], due(h0t))
                    act.activation(flat(buf)[:, j * 512:(j + 1) * 512], tp[:, (4 * d + j) % 2], ACT.Copy).then_inc(h0c["sem"], step(h0c))
            with rounds(act, 2, (seg, 16), (seg_r, 16), (rise, 16), (e_ok, 16), (m_ok, 16), (sqi, 2), (sqo, 2),
                        (var, 2), (dev, 2)) as i:
                for b in range(2):
                    c = i * 2 + (1 + b)
                    rises(c, 0)
                    rises(c, 1)
                    for g in range(NG):
                        decays(g)
                        if g + 2 < NG:
                            rises(c, g + 2)
                    squares()
                    roots(mv[:, 0, 2:3])

            def split_hi_normed(slot):
                act.wait_ge(raws[slot]["sem"], due(raws[slot]))
                for k in range(KT):
                    n = Q_SN + slot * KT + k
                    last = act.activation(whi[:, slot, k], raw[:, slot, k], ACT.Copy, scale=colp[:, n:n + 1])
                last.then_inc(hi["sem"], step(hi))

            split_hi_normed(0)
            act.wait_ge(s["chunk_ok"], 8)
            yt, yhi, yok = count(s["y_turned"]), count(s["y_hi"]), count(s["y_ok"])
            for t in range(NT):
                for j in range(4):
                    act.wait_ge(yt["sem"], due(yt))
                    act.activation(yh[:, 4 * j:4 * j + 4, tok(t):tok(t) + P],
                                   tp[:, j].rearrange("p (n t) -> p n t", t=P), ACT.Copy).then_inc(yhi["sem"], step(yhi))
                if t == 0:
                    split_hi_normed(1)
            half, msum, mhi = count(s["w_half"]), count(s["merge_sum"]), count(s["merge_hi"])

            def merge_round(i, split):
                act.wait_ge(half["sem"], due(half))
                split(0)
                for b in range(2):
                    if b == 1:
                        step(ready, 2)
                        act.wait_ge(ready["sem"], value(ready))
                        split(1)
                    act.wait_ge(msum["sem"], due(msum))
                    act.activation(hh[:, bass.ds(i * 2 + b, 1)].rearrange("p o t -> p (o t)"), mrg,
                                   ACT.Copy).then_inc(mhi["sem"], step(mhi))

            with rounds(act, 3, (ready, 2), (hi, 2), (raws[0], 1), (raws[1], 1), (half, 1), (msum, 2), (mhi, 2)) as i:
                merge_round(i, split_hi_normed)
            merge_round(3, split_hi)

            with rounds(act, 2, (ready, 2 * NT), (hi, 2), (raws[0], 1), (raws[1], 1)):
                for b in range(2):
                    step(ready, NT)
                    act.wait_ge(ready["sem"], value(ready))
                    split_hi(b)
            roots(mv[:, :, 2])
            roots(mv[:, :, 2])
            jump(free, U_H2)
            act.wait_ge(s["pad_ok"], 2)
            modulated(None, hf2, "h2_hi", "h2_ok", 4, 3)

            relu, sq = count(s["relu_ok"]), count(s["square_ok"])

            def mlp_round(last_round):
                for n in range(KT):
                    act.wait_ge(relu["sem"], due(relu))
                    act.activation(fh[:, n], hf2[:, n % 2], ACT.Square).then_inc(sq["sem"], step(sq))
                    step(ready)
                    if n % 2 == 1:
                        act.wait_ge(ready["sem"], value(ready))
                        split_hi(n // 2 % 2)
                for b in range(4):
                    step(ready, NT)
                    if b < 2 or not last_round:
                        act.wait_ge(ready["sem"], value(ready))
                        split_hi(b % 2)

            with rounds(act, 3, (ready, KT + 4 * NT), (hi, 8), (raws[0], 4), (raws[1], 4), (relu, KT), (sq, KT)):
                mlp_round(False)
            mlp_round(True)
            roots(mv[:, :, 2])

        @block.vector
        def _(dve):
            dv = count(s["dve_step"])
            hi, lo = count(s["hi_done"]), count(s["lo_done"])
            ready, free = count(s["acc_ready"]), count(s["acc_free"])

            def do(ins):
                ins.then_inc(dv["sem"], step(dv))
                dve.wait_ge(dv["sem"], value(dv))

            def split_lo(slot):
                dve.wait_ge(hi["sem"], due(hi))
                dve.tensor_tensor(wlo[:, slot], raw[:, slot], whi[:, slot].bitcast(F32), ALU.subtract).then_inc(lo["sem"], step(lo))

            def over(ap, *shape):
                return ap.unsqueeze(len(ap.shape)).broadcast_to([P, *shape])

            for buf in (hf[:, :, CTX:CTX + 2], hf[:, :, NCONV:TP]):
                last = dve.memset(buf, 0.0)
            last.then_inc(s["pad_ok"], 1)
            dve.wait_ge(s["rows_turned"], 1)
            dve.tensor_copy(colp[:], tp[:, 0, 0:Q_ALL]).then_inc(s["turned_free"], 1)
            dve.wait_ge(s["turned_free"], 1)

            var, dev = count(s["var_ok"]), count(s["dev_ok"])

            def statistics(t, src):
                for j in range(2):
                    do(dve.bn_stats(st6[:, j], src[:, j * 512:(j + 1) * 512]))
                do(dve.bn_aggr(mv[:, t, 0:2], st6[:].rearrange("p a b -> p (a b)")))

            def deviations():
                dve.tensor_scalar(mv[:, :, 2], mv[:, :, 1], EPS, None, ALU.add).then_inc(var["sem"], step(var))
                dve.wait_ge(dev["sem"], due(dev))
                do(dve.reciprocal(mv[:, :, 2], mv[:, :, 2]))
                do(dve.scalar_tensor_tensor(mv[:, :, 3], mv[:, :, 0], -1.0, mv[:, :, 2], ALU.mult, ALU.mult))

            def normed(t, dst, src):
                return dve.tensor_scalar(dst, src, mv[:, t, 2:3], mv[:, t, 3:4], ALU.mult, ALU.add)

            dve.wait_ge(s["x_in"], 32)
            for t in range(NT):
                statistics(t, xin[:, t])
            deviations()
            for t in range(NT):
                normed(t, xin[:, t], xin[:, t]).then_inc(s["xn_ok"], 1)
            dve.wait_ge(s["mod_used"], 8)
            do(dve.tensor_tensor(modc[:, 0:2 * KT], modp, over(colp[:, Q_BM:Q_BM + 2 * KT], 2 * KT, 2), ALU.add))
            dve.tensor_scalar(modc[:, KT:2 * KT], modc[:, KT:2 * KT], 1.0, None, ALU.add).then_inc(s["mod_copied"], 1)

            def split_h(buf, hi_ok, lo_ok):
                h = count(s[hi_ok])
                for k in range(KT):
                    dve.wait_ge(h["sem"], due(h))
                    dve.tensor_tensor(hl[:, k], buf[:, k % 2], hh[:, k].bitcast(F32), ALU.subtract).then_inc(s[lo_ok], 1)

            split_h(hf, "hi_of_h", "h_ok")
            split_lo(0)
            split_lo(1)

            conv = count(s["conv_ok"])
            dve.wait_ge(s["acc_free"], KT)
            for u in range(2):
                dve.memset(xpad[:, u, 0:2], 0.0).then_inc(conv["sem"], step(conv))
            silu = count(s["conv_silu"])
            cmod, mru = count(s["mod_copied"]), count(s["mraw_used"])
            step(cmod)

            def convolve(n, ct):
                dve.wait_ge(free["sem"], due(free))
                w = lambda t: colp[:, bass.ds(ct + (Q_CONV + t * 32), 1)]
                o, x = cvo[:, n % 2], xpad[:, n % 2]
                step(silu)
                if some(silu, 2):
                    dve.wait_ge(silu["sem"], value(silu, 2))
                do(dve.tensor_scalar(o, x[:, 0:NCONV], w(0), colp[:, bass.ds(ct + Q_CB, 1)], ALU.mult, ALU.add))
                for t in range(1, TAPS):
                    ins = dve.scalar_tensor_tensor(o, x[:, t:t + NCONV], w(t), o, ALU.mult, ALU.add)
                    if t < TAPS - 1:
                        do(ins)
                ins.then_inc(conv["sem"], step(conv))

            step(free, KT)
            with rounds(dve, RX + RB + RC, (free, 4), (conv, 4), (hi, 2), (lo, 2), (dv, 16), (cmod, 1), (mru, 2)) as i:
                for n in range(4):
                    convolve(n, i * 4 + n)
                    if n % 2 == 1:
                        split_lo(n // 2)
                step(mru, 2)
                dve.wait_ge(mru["sem"], value(mru))
                dst = modc[:, bass.ds(i * 4 + 2 * KT, 4)].rearrange("p (a b) c -> p a b c", a=2)
                bias = colp[:, bass.ds(i * 4 + (Q_BM + 2 * KT), 4)].rearrange("p (a b) -> p a b", a=2)
                dve.tensor_tensor(dst, tp[:, 2:4, 0:4].rearrange("p a (b c) -> p a b c", c=2),
                                              bias.unsqueeze(3).broadcast_to([P, 2, 2, 2]), ALU.add).then_inc(cmod["sem"], step(cmod))
            dve.wait_ge(cmod["sem"], value(cmod))
            dve.tensor_scalar(modc[:, 4 * KT:5 * KT], modc[:, 4 * KT:5 * KT], 1.0, None, ALU.add).then_inc(s["modc_ok"], 1)

            dve.wait_ge(s["dt_in"], 48)
            dve.wait_ge(s["dt_hi"], 1)
            dve.tensor_tensor(wdl[:], wdt, wdh[:].bitcast(F32), ALU.subtract).then_inc(s["dt_split"], 1)
            dve.wait_ge(s["dt_mm"], 1)
            fl5 = lambda t: t.rearrange("p t h -> p (t h)")
            mid = lambda ap: ap.unsqueeze(1).broadcast_to([P, NT, 2 * NH])
            do(dve.tensor_tensor(dtu[:, 2], tp[:, 0, 0:NT * 2 * NH].rearrange("p (t h) -> p t h", t=NT), mid(dtb), ALU.add))
            do(dve.tensor_scalar(dtu[:, 0], dtu[:, 2], -1.0, None, ALU.mult))
            dve.tensor_tensor(dtu[:, 0], dtu[:, 0], dtu[:, 2], ALU.max).then_inc(s["dt_abs"], 1)
            do(dve.tensor_scalar(dtu[:, 2], dtu[:, 2], 0.0, None, ALU.max))
            dve.wait_ge(s["dt_soft"], 1)
            do(dve.tensor_tensor(dts[:], dtu[:, 2], dtu[:, 1], ALU.add))
            do(dve.tensor_tensor(dta[:], dts[:], mid(alg), ALU.mult))
            dve.tensor_scalar(dta[:], dta[:], -1.0, None, ALU.mult).then_inc(s["dt_sums"], 1)
            dve.wait_ge(s["dt_exp"], 1)
            dve.tensor_tensor(sdt[:], dts[:], dec[:, :, 1], ALU.mult).then_inc(s["dt_ok"], 1)

            for c in pair("nat_out"):
                step(c, 2 * (RX + RB))
                dve.wait_ge(c["sem"], value(c))
            for c in pair("conv_out"):
                step(c, 4 * (RB + RC))
                dve.wait_ge(c["sem"], value(c))
            dve.wait_ge(s["qkv_in"], 64)
            hd = lambda ap: ap.rearrange("p t (h d) -> p t h d", d=HD)
            th = lambda ap: ap.rearrange("p t (h d) -> p (t h) d", d=HD)
            for n in range(5):
                step(free, NT)
                dve.wait_ge(free["sem"], value(free))
                q = q5[:, n % 2]
                do(dve.tensor_tensor(t5, q, q, ALU.mult))
                msf = ms.rearrange("p t h -> p (t h)")
                do(dve.tensor_reduce(msf, th(t5), AX.X, ALU.add))
                dve.tensor_scalar(msf, msf, 1.0 / HD, EPS, ALU.mult, ALU.add).then_inc(var["sem"], step(var))
                dve.wait_ge(dev["sem"], due(dev))
                do(dve.reciprocal(msf, msf))
                do(dve.tensor_tensor(th(t5), th(q), over(msf, NT * 2, HD), ALU.mult))
                gain = nrow[:, n // 4].unsqueeze(1).broadcast_to([P, NT * 2, HD])
                do(dve.tensor_tensor(th(u5), th(t5), gain, ALU.mult))
                if n == 4:
                    dve.tensor_copy(kout, u5[:, 0]).then_inc(s["kout_ok"], 1)
                cols = slice(n * BW, (n + 1) * BW)
                dve.tensor_copy(rq[:, 0, cols], u5[:, 0])
                sine = cst[:, K_SIN:K_SIN + 4 * P].rearrange("p (t a b f) -> p t a b f", t=4, a=2, b=2)
                for h in range(2):
                    v = lambda ap: ap[:, 1:NT, h * HD:(h + 1) * HD].rearrange("p t (a b f) -> p t a b f", a=2, b=2)
                    for b in range(2):
                        last = dve.tensor_tensor(v(t5)[:, :, :, b], v(u5)[:, :, :, 1 - b], sine[:, :, :, b], ALU.mult)
                do(last)
                cosine = cst[:, K_COS:K_COS + 4 * P].rearrange("p (t d) -> p t d", t=4).unsqueeze(2).broadcast_to([P, 4, 2, HD])
                do(dve.tensor_tensor(hd(q[:, 1:NT]), hd(u5[:, 1:NT]), cosine, ALU.mult))
                dve.tensor_tensor(rq[:, 1:NT, cols], q[:, 1:NT], t5[:, 1:NT], ALU.add).then_inc(s["rot_ok"], 1)
                dve.wait_ge(s["rot_ok"], n + 1)
                split_lo(n % 2)
            step(free, NT)
            split_lo(1)
            with rounds(dve, 8, (hi, 2), (lo, 2)):
                for b in range(2):
                    split_lo(b)

            score, mx, ex, prob = (count(s[n]) for n in ("score_ready", "max_ok", "exp_ok", "prob_ok"))
            ahi, aok = count(s["att_hi"]), count(s["att_ok"])
            dve.wait_ge(s["qk_copied"], HQ + HKV + 1)

            def maxima(n):
                u = n % 2
                dve.wait_ge(score["sem"], due(score))
                if n < N_SCORE:
                    sc = acc[:, 2 * u:2 * u + 2].rearrange("p a b -> p (a b)")[:, 0:LAT + PAST]
                    do(dve.tensor_reduce(sm[:, u, 8:9], sc, AX.X, ALU.max))
                    dve.tensor_scalar(sm[:, u, 0:1], sm[:, u, 8:9], -SCALE, None, ALU.mult).then_inc(mx["sem"], step(mx))
                else:
                    sc = acc[:, 2 * u].rearrange("p (r t) -> p r t", r=R)
                    do(dve.tensor_reduce(sm[:, u, 8:12], sc, AX.X, ALU.max))
                    dve.tensor_scalar(sm[:, u, 0:4], sm[:, u, 8:12], -SCALE, None, ALU.mult).then_inc(mx["sem"], step(mx))

            def probabilities(n):
                u = n % 2
                dve.wait_ge(ex["sem"], due(ex))
                if n < N_SCORE:
                    do(dve.reciprocal(sm[:, u, 12:13], sm[:, u, 4:5]))
                    dve.tensor_scalar(pr[:, u], pr[:, u], sm[:, u, 12:13], None, ALU.mult).then_inc(prob["sem"], step(prob))
                else:
                    do(dve.reciprocal(sm[:, u, 12:16], sm[:, u, 4:8]))
                    p4 = pr[:, u, 0:R * P].rearrange("p (r t) -> p r t", r=R)
                    dve.tensor_tensor(p4, p4, over(sm[:, u, 12:16], R, P), ALU.mult).then_inc(prob["sem"], step(prob))

            def att_lower(h):
                dve.wait_ge(ahi["sem"], due(ahi))
                if h < HQ:
                    cols = (slice(h, h + 1), slice(CTX + 2, NCONV))
                    src = tp[:, 2 + h % 2].unsqueeze(1)
                else:
                    cols = (slice(R * (h - HQ), R * (h - HQ) + R), slice(0, CTX))
                    src = tp[:, 2 + h % 2].rearrange("p (r t) -> p r t", r=R)
                dve.tensor_tensor(hl[:, cols[0], cols[1]], src, hh[:, cols[0], cols[1]].bitcast(F32), ALU.subtract).then_inc(aok["sem"], step(aok))

            maxima(0)
            maxima(1)
            for n in range(N_SCORE + HKV):
                probabilities(n)
                if n + 2 < N_SCORE + HKV:
                    maxima(n + 2)
                if n % 4 == 1 and 4 < n < N_SCORE:
                    att_lower(n // 4 - 1)
            for h in range(HQ - 1, HQ + 2):
                att_lower(h)

            jump(ready, U_AO)
            jump(free, U_AO)
            gat_in, ao = pair("gat_in"), pair("ast_out")
            both = lambda ap: ap.rearrange("p (a b) -> p a b", a=2)
            for n in range(KT):
                dve.wait_ge(ready["sem"], due(ready))
                dve.wait_ge(gat_in[n % 2]["sem"], due(gat_in[n % 2]))
                step(ao[n % 2])
                if some(ao[n % 2], 1):
                    dve.wait_ge(ao[n % 2]["sem"], value(ao[n % 2], 1))
                dve.tensor_tensor(both(ast[:, n % 2]), acc[:, 2 * (n % 2):2 * (n % 2) + 2, 0:HALF],
                                              both(gat[:, n % 2]), ALU.mult).then_inc(free["sem"], step(free))
                if n in (1, 3):
                    split_lo(n // 2)
            for c in ao:
                dve.wait_ge(c["sem"], value(c))
            dve.wait_ge(free["sem"], value(free))

            cin = pair("chunk_in")
            cbr, cbo, rise, seg, e_ok = (count(s[n]) for n in ("cb_ready", "cb_ok", "rise_ok", "seg_ready", "e_ok"))
            m_ok, xd, grp, quad, qok = (count(s[n]) for n in ("m_ok", "xd_ok", "group_ready", "states_ready", "quad_ok"))
            car = count(s["carried_ok"])
            sqi, sqo, chunk = count(s["sq_in"]), count(s["sq_ok"]), count(s["chunk_ok"])
            zin = count(s["z_in"], 16)
            dve.wait_ge(s["dsk_in"], 16)
            flat = lambda t: t.rearrange("p h q -> p (h q)")
            le8, ge8 = (mask(k).unsqueeze(1).broadcast_to([P, NG, P]) for k in (K_LE, K_GE))

            def of_chunk(t, c):
                return t[:, bass.ds(c, 1)].rearrange("p o h -> p (o h)")

            def scan_chunk(slot, c, latent, out):
                x = xs_s[slot]
                step(cin[slot], 3)
                dve.wait_ge(cin[slot]["sem"], value(cin[slot]))
                f4 = lambda t, q: over(t[:, 8 * q:8 * q + 8], 8, SP_)
                DT, SD = (of_chunk(t, c) for t in (dts, sdt))
                to, whole = of_chunk(dec[:, :, 0], c), of_chunk(dec[:, :, 2], c)

                def scaled(q):
                    h = slice(8 * q, 8 * q + 8)
                    dve.tensor_tensor(xdf[:, q % 2], x[:, h], f4(DT, q), ALU.mult)
                    dve.tensor_tensor(xdb[:, q % 2], x[:, h], f4(DT[:, NH:], q), ALU.mult)
                    if not latent:
                        dve.tensor_tensor(xwb[:, q % 2], x[:, h], f4(SD[:, NH:], q), ALU.mult)
                    dve.tensor_tensor(xwf[:, q % 2], x[:, h], f4(SD, q), ALU.mult).then_inc(xd["sem"], step(xd))

                def weighted(g):
                    dve.wait_ge(e_ok["sem"], due(e_ok))
                    step(grp)
                    if some(grp, 2):
                        dve.wait_ge(grp["sem"], value(grp, 2))
                    for j in range(2):
                        last = dve.tensor_tensor(mm[:, g % 2, j], ee[:, g % 2],
                                                 cbm[:, j, g].unsqueeze(1).broadcast_to([P, R, P]), ALU.mult)
                    last.then_inc(m_ok["sem"], step(m_ok))

                v = lambda bank: bank.rearrange("p (h q) -> p h q", q=SP_)
                banks = lambda q: (acc[:, 2], acc[:, 3]) if q % 2 == 0 else (tp[:, 0], tp[:, 1])

                def carried(q):
                    h = slice(8 * q, 8 * q + 8)
                    dve.wait_ge(quad["sem"], due(quad))
                    dve.tensor_tensor(yy[:, h], v(tp[:, 2]), f4(to, q), ALU.mult)
                    do(dve.tensor_tensor(tq, v(tp[:, 3]), f4(to[:, NH:], q), ALU.mult))
                    dve.tensor_tensor(hF[:, h], hF[:, h], f4(whole, q), ALU.mult)
                    do(dve.tensor_tensor(yy[:, h], yy[:, h], tq, ALU.add))
                    dve.tensor_tensor(hF[:, h], hF[:, h], v(banks(q)[1]), ALU.add).then_inc(car["sem"], step(car))
                    do(dve.tensor_tensor(tq, x[:, h], f4(dsk[:], q), ALU.mult))
                    do(dve.tensor_tensor(yy[:, h], yy[:, h], tq, ALU.add))

                def combined(q):
                    h = slice(8 * q, 8 * q + 8)
                    if not latent:
                        dve.tensor_tensor(tq, x[:, h], f4(dsk[:], q), ALU.mult).then_inc(car["sem"], step(car))
                        dve.wait_ge(car["sem"], value(car))
                    step(grp_q, 2)
                    dve.wait_ge(grp_q["sem"], value(grp_q))
                    dve.tensor_tensor(yy[:, h], yy[:, h] if latent else tq, v(banks(q)[0]), ALU.add).then_inc(qok["sem"], step(qok))
                    if not latent:
                        dve.wait_ge(qok["sem"], value(qok))

                scaled(0)
                dve.wait_ge(cbr["sem"], due(cbr))
                tpv = tp[:, 0:2].rearrange("p a (g t) -> p (a g) t", t=P)
                dve.tensor_tensor(cbm[:, 0], tpv, le8, ALU.mult)
                dve.tensor_tensor(cbm[:, 1], tpv, ge8, ALU.mult).then_inc(cbo["sem"], step(cbo))
                dve.wait_ge(cbo["sem"], value(cbo))
                for g in range(NG):
                    weighted(g)
                    if g % 2 == 1 and g + 1 < NG:
                        scaled((g + 1) // 2)
                    if g % 2 == 1 and latent:
                        carried(g // 2)
                    if g % 2 == 1 and g > 1:
                        combined(g // 2 - 1)
                combined(3)
                dve.wait_ge(zin["sem"], due(zin))
                dve.wait_ge(qok["sem"], value(qok))
                dve.tensor_tensor(flat(yy), flat(yy), zc, ALU.mult).then_inc(sqi["sem"], step(sqi))
                dve.wait_ge(sqo["sem"], due(sqo))
                dve.tensor_scalar(mv[:, 0, 2:3], mv[:, 0, 0:1], 1.0 / DI, EPS, ALU.mult, ALU.add).then_inc(var["sem"], step(var))
                dve.wait_ge(dev["sem"], due(dev))
                do(dve.reciprocal(mv[:, 0, 3:4], mv[:, 0, 2:3]))
                dve.tensor_scalar(out, flat(yy), mv[:, 0, 3:4], None, ALU.mult).then_inc(chunk["sem"], step(chunk))
                dve.wait_ge(chunk["sem"], value(chunk))

            grp_q = count(s["group_ready"])
            scan_chunk(0, 0, False, yctx[:])
            step(quad, 4)
            back, bok, xwo = count(s["back_ready"]), count(s["back_ok"]), count(s["xwb_ok"])
            backr = count(s["back_ready"])
            dve.wait_ge(s["h0_ok"], 8)
            hbo = count(s["hb_out"], 16)
            for j in range(1, 4):
                c, x = ORDER_[j], xs_s[j % 2]
                step(cin[j % 2], 3)
                dve.wait_ge(cin[j % 2]["sem"], value(cin[j % 2]))
                f4 = lambda t, q: over(t[:, 8 * q:8 * q + 8], 8, SP_)

                def back_scaled(q):
                    step(back)
                    if some(back, 2):
                        dve.wait_ge(back["sem"], value(back, 2))
                    dve.tensor_tensor(xwb[:, q % 2], x[:, 8 * q:8 * q + 8], f4(sdt[:, c, NH:], q), ALU.mult).then_inc(xwo["sem"], step(xwo))

                dve.wait_ge(hbo["sem"], due(hbo))
                back_scaled(0)
                for q in range(4):
                    if q < 3:
                        back_scaled(q + 1)
                    h = slice(8 * q, 8 * q + 8)
                    do(dve.tensor_tensor(hB[:, h], hB[:, h], f4(dec[:, c, 2, NH:], q), ALU.mult))
                    dve.wait_ge(backr["sem"], due(backr))
                    ins = dve.tensor_tensor(hB[:, h], hB[:, h], acc[:, 2 + q % 2].rearrange("p (h q) -> p h q", q=SP_), ALU.add)
                    ins.then_inc(bok["sem"], step(bok))
                dve.wait_ge(bok["sem"], value(bok))
                dve.tensor_copy(mv[:, 1, 0:1], mv[:, 1, 1:2]).then_inc(chunk["sem"], step(chunk))
            every = [(cin[0], 3), (cin[1], 3), (cbr, 2), (cbo, 2), (e_ok, 16), (m_ok, 16), (grp, 16),
                     (xd, 8), (quad, 8), (grp_q, 16), (car, 8), (qok, 8), (sqi, 2), (sqo, 2), (chunk, 2), (zin, 2), (var, 2), (dev, 2), (dv, 2 * (4 * 4 + 1))]
            with rounds(dve, 2, *every) as i:
                for b in range(2):
                    scan_chunk(b, i * 2 + (1 + b), True, ysb[b][:, bass.ds(i * DI, DI)])

            def split_lo_normed(slot):
                dve.wait_ge(hi["sem"], due(hi))
                for k in range(KT):
                    n = Q_SN + slot * KT + k
                    last = dve.scalar_tensor_tensor(wlo[:, slot, k], raw[:, slot, k], colp[:, n:n + 1],
                                                    whi[:, slot, k].bitcast(F32), ALU.mult, ALU.subtract)
                last.then_inc(lo["sem"], step(lo))

            split_lo_normed(0)
            for y in (yh, yl):
                dve.memset(y[:, :, CTX:CTX + 2].bitcast(F32), 0.0)
                last = dve.memset(y[:, :, NCONV:TP].bitcast(F32), 0.0)
            yhi, yok = count(s["y_hi"]), count(s["y_ok"])
            for t in range(NT):
                for j in range(4):
                    dve.wait_ge(yhi["sem"], due(yhi))
                    part = (slice(4 * j, 4 * j + 4), slice(tok(t), tok(t) + P))
                    dve.tensor_tensor(yl[:, part[0], part[1]], tp[:, j].rearrange("p (n t) -> p n t", t=P),
                                      yh[:, part[0], part[1]].bitcast(F32), ALU.subtract).then_inc(yok["sem"], step(yok))
                if t == 0:
                    split_lo_normed(1)
            jump(ready, U_SO)
            jump(free, U_SO)
            gm, msum, mhi, mok = count(s["gm_in"], 16), count(s["merge_sum"]), count(s["merge_hi"]), count(s["merge_ok"])

            def merge_round(i, split):
                split(0)
                for b in range(2):
                    dve.wait_ge(ready["sem"], due(ready))
                    if b == 1:
                        split(1)
                    step(gm, 2)
                    dve.wait_ge(gm["sem"], value(gm))
                    dve.tensor_tensor(both(mrg), acc[:, 2 * b:2 * b + 2, 0:HALF], both(gbt), ALU.mult).then_inc(free["sem"], step(free))
                    dve.wait_ge(free["sem"], value(free))
                    dve.tensor_tensor(mrg, mrg, m1t, ALU.add).then_inc(msum["sem"], step(msum))
                    dve.wait_ge(mhi["sem"], due(mhi))
                    k = lambda t: t[:, bass.ds(i * 2 + b, 1)].rearrange("p o t -> p (o t)")
                    dve.tensor_tensor(k(hl), mrg, k(hh).bitcast(F32), ALU.subtract).then_inc(mok["sem"], step(mok))
                    dve.wait_ge(mok["sem"], value(mok))

            with rounds(dve, 3, (ready, 2), (free, 2), (hi, 2), (lo, 2), (gm, 4), (msum, 2), (mhi, 2), (mok, 2)) as i:
                merge_round(i, split_lo_normed)
            merge_round(3, split_lo)

            dve.wait_ge(s["gate_turned"], 1)
            for n in range(2):
                dve.tensor_copy(grow[:, n], tp[0:2 * KT, 2, n * P:(n + 1) * P]).then_inc(s["gate_copied"], 1)

            dve.wait_ge(s["rows2_in"], 16 * 7)
            do(dve.tensor_scalar(xo, xo, ALPHA, None, ALU.mult))
            with rounds(dve, 2, (ready, 2 * NT), (free, 2 * NT), (hi, 2), (lo, 2)) as i:
                for b in range(2):
                    cols = bass.ds(i * (2 * BW) + b * BW, BW)
                    for t in range(NT):
                        dve.wait_ge(ready["sem"], due(ready))
                        dve.tensor_tensor(x1[:, t, cols], acc[:, 2 * ((NT * b + t) % 2), 0:BW],
                                                      g1r[:, min(t, 1), cols], ALU.mult).then_inc(free["sem"], step(free))
                    split_lo(b)
            dve.wait_ge(free["sem"], value(free))
            for t in range(NT):
                do(dve.tensor_tensor(x1[:, t], x1[:, t], xo[:, t], ALU.add))
                statistics(t, x1[:, t])
            deviations()
            for t in range(NT):
                do(normed(t, x1[:, t], x1[:, t]))
                do(dve.tensor_tensor(x1[:, t], x1[:, t], lnr[:, 0], ALU.mult))
                do(dve.tensor_tensor(x1[:, t], x1[:, t], lnr[:, 1], ALU.add))
                statistics(t, x1[:, t])
            deviations()
            for t in range(NT):
                normed(t, xq[:, t], x1[:, t]).then_inc(s["x1_ok"], 1)
                do(dve.tensor_copy(xo[:, t], row))
            for buf in (hf2[:, :, CTX:CTX + 2], hf2[:, :, NCONV:TP]):
                last = dve.memset(buf, 0.0)
            last.then_inc(s["pad_ok"], 1)
            split_h(hf2, "h2_hi", "h2_ok")

            relu, sq, ff = count(s["relu_ok"]), count(s["square_ok"]), count(s["ff_ok"])
            jump(ready, U_MLP)
            jump(free, U_MLP)
            sqb = row[:, 0:TP]
            dve.wait_ge(s["h2_ok"], KT)
            dve.wait_ge(s["x1_ok"], NT)

            def mlp_round(i, last_round):
                for n in range(KT):
                    dve.wait_ge(ready["sem"], due(ready))
                    r = hf2[:, n % 2]
                    b1 = colp[:, bass.ds(i * KT + (Q_B1 + n), 1)]
                    dve.tensor_scalar(both(r), acc[:, 2 * (n % 2):2 * (n % 2) + 2, 0:HALF], b1, 0.0, ALU.add, ALU.max).then_inc(free["sem"], step(free))
                    dve.wait_ge(free["sem"], value(free))
                    dve.tensor_tensor(sqb, r, r, ALU.mult).then_inc(relu["sem"], step(relu))
                    dve.wait_ge(relu["sem"], value(relu))
                    dve.wait_ge(sq["sem"], due(sq))
                    dve.tensor_tensor(fl[:, n], sqb, fh[:, n].bitcast(F32), ALU.subtract).then_inc(ff["sem"], step(ff))
                    if n % 2 == 1:
                        split_lo(n // 2 % 2)
                for b in range(4):
                    cols = slice(b * BW, (b + 1) * BW)
                    for t in range(NT):
                        dve.wait_ge(ready["sem"], due(ready))
                        dve.tensor_tensor(xo[:, t, cols], xo[:, t, cols], acc[:, 2 * ((NT * b + t) % 2), 0:BW], ALU.add).then_inc(free["sem"], step(free))
                    if b < 2 or not last_round:
                        split_lo(b % 2)

            with rounds(dve, 3, (ready, KT + 4 * NT), (free, KT + 4 * NT), (hi, 8), (lo, 8), (relu, KT), (sq, KT), (ff, KT)) as i:
                mlp_round(i, False)
            mlp_round(3, True)
            dve.wait_ge(free["sem"], value(free))

            dve.wait_ge(s["rows2_in"], 16 * 11)
            for t in range(NT):
                do(dve.tensor_tensor(xo[:, t], xo[:, t], g1r[:, min(t, 1)], ALU.mult))
                do(dve.scalar_tensor_tensor(xo[:, t], x1[:, t], ALPHA, xo[:, t], ALU.mult, ALU.add))
                statistics(t, xo[:, t])
            deviations()
            for t in range(NT):
                do(normed(t, xo[:, t], xo[:, t]))
                do(dve.tensor_tensor(xo[:, t], xo[:, t], lnr[:, 0], ALU.mult))
                dve.tensor_tensor(xo[:, t], xo[:, t], lnr[:, 1], ALU.add).then_inc(s["final_ok"], 1)


_OUTS = [(1, CTX, D), (1, LAT, D), (1, 1, CTX, HKV, HD), (1, 1, CTX, HKV, HD), (1, 1, 2, NH, SP_, NS)]


def kernel(**inputs):
    import numpy as np
    import concourse.bacc as bacc
    from concourse.bass_utils import run_bass_kernel_spmd as run

    k, i = np.arange(P)[:, None], np.arange(P)[None, :]
    parts = [k == i, k <= i, k >= i, k > i, k < i, k >= 0 * i]
    t = np.arange(LAT)
    pos = np.stack([t // GRID_W, t % GRID_W], -1).astype(np.float32)
    inv = (np.float32(ROPE_THETA) ** (-np.arange(HD // 4, dtype=np.float32) / np.float32(HD // 4))).astype(np.float32)
    ang = pos[:, :, None] * inv
    cos, sin = np.cos(ang), np.sin(ang)
    table = lambda a, b: np.stack([a, b], 2).reshape(LAT // P, P, HD).transpose(1, 0, 2).reshape(P, -1)
    consts = np.concatenate([p.astype(np.float32) for p in parts] + [table(cos, cos), table(-sin, sin)], 1).astype(np.float32)

    nc = bacc.Bacc("TRN2", target_bir_lowering=False, num_devices=1)
    arrays, args = {}, {}
    for name, v in list(inputs.items()) + [("consts", consts)]:
        v = np.ascontiguousarray(v)
        arrays[f"in_{name}"] = v
        args[name] = nc.dram_tensor(f"in_{name}", v.shape, mybir.dt.from_np(v.dtype), kind="ExternalInput").ap()
    outs = [nc.dram_tensor(f"out_{n}", shape, F32, kind="ExternalOutput").ap() for n, shape in enumerate(_OUTS)]
    build(nc, args, outs)
    r = run(nc, [arrays], core_ids=[0])
    return tuple(r.results[0][f"out_{n}"] for n in range(len(_OUTS)))
```

```python
import math
from contextlib import ExitStack, contextmanager

import concourse.bass as bass
from concourse import mybir

F32 = mybir.dt.float32
F32R = mybir.dt.float32r
ACT = mybir.ActivationFunctionType
ALU = mybir.AluOpType
AX = mybir.AxisListType

P = 128
D = 1024
KT = D // P
CTX, LAT, PAST = 128, 512, 256
NT = (CTX + LAT) // P
HQ, HKV, HD = 8, 2, 128
DI = 2 * D
NH, SP_ = 32, 64
NG, NS = 8, 128
R = NH // NG
BC = NG * NS
XBC = DI + 2 * BC
TAPS = 5
ALPHA = 2.0 ** 0.25
EPS = 1e-6
SCALE = HD ** -0.5
C_Q = 0
C_Z = HQ * HD + 2 * HKV * HD
C_XBC = C_Z + DI
C_DT = C_XBC + XBC
C_G = C_DT + 2 * NH
TP = CTX + 2 + LAT + 2
HALF = TP // 2
NCONV = CTX + 2 + LAT
BW = 256
K_ID, K_LE, K_GE, K_GT, K_LT, K_ONE, K_COS, K_SIN = (P * n for n in (0, 1, 2, 3, 4, 5, 6, 10))
K_ALL = 14 * P
GRID_W, ROPE_THETA = 64, 10000.0
Q_CONV, Q_CB, Q_SN, Q_B1, Q_BM, Q_C = 0, 160, 192, 208, 240, 288
Q_ALL = 304


def tok(t):
    return 0 if t == 0 else 2 + t * P


def count(sem, step=1, start=0):
    return {"sem": sem, "step": step, "base": start, "k": 0, "round": None, "per": 0}


def value(c, back=0):
    v = c["step"] * (c["base"] + c["k"] - back)
    assert v > 0, "a wait stands where there is something to wait for"
    return v if c["round"] is None else c["round"] * (c["per"] * c["step"]) + v


def step(c, n=1):
    c["k"] += n
    return c["step"]


def due(c, back=0):
    step(c)
    return value(c, back)


def some(c, back=0):
    n = c["base"] + c["k"] - back
    assert c["round"] is None or n > 0, "in a loop every round waits"
    return n > 0


def jump(c, n):
    c["base"], c["k"] = n, 0


@contextmanager
def rounds(eng, n, *counts):
    with eng.Fori(0, n) as i:
        for c, per in counts:
            c["base"], c["k"], c["round"], c["per"] = c["base"] + c["k"], 0, i, per
        yield i
        for c, per in counts:
            assert c["k"] == per, f"{c['sem']}: {c['k']} signals in a round, not {per}"
    for c, per in counts:
        c["base"], c["k"], c["round"] = c["base"] + n * per, 0, None


def build(nc, a, outs):
    y_p, y_s, out_k, out_v, out_st = outs
    scratch = lambda n, shape: nc.dram_tensor(n, shape, F32, kind="Internal").ap()
    xs_d = scratch("xs_nat", (NT, P, DI))
    bn_d = scratch("b_nat", (NT, P, BC))
    bct_d = scratch("bc_t", (NT, P, 2 * NG, P))
    z_d = scratch("z_silu", (NT, P, DI))
    g_d = scratch("gates_t", (2 * KT, P, TP))
    hb_d = scratch("h_back", (NT, P, DI))
    m1_d = scratch("attention_branch", (KT, P, TP))
    gr_d = scratch("gate_rows", (2, KT, 2, P))

    with ExitStack() as ctx:
        def sb(n, shape, dt=F32):
            return ctx.enter_context(nc.sbuf_tensor(n, shape, dt))

        def sem(n):
            return ctx.enter_context(nc.semaphore(n))

        raw = sb("raw", [P, 2, KT, BW])
        whi = sb("whi", [P, 2, KT, BW], F32R)
        yctx = nc.alloc_sbuf_tensor_at("y_context", [P, DI], F32, offset=nc.sbuf_base - 4 * KT * BW)
        wlo = sb("wlo", [P, 2, KT, BW], F32R)
        hh = sb("hh", [P, KT, TP], F32R)
        y13 = nc.alloc_sbuf_tensor_at("y_tiles_1_3", [P, 2 * DI + 8 * SP_], F32, offset=nc.sbuf_base - 4 * KT * TP)
        hl = sb("hl", [P, KT, TP], F32R)
        y24 = nc.alloc_sbuf_tensor_at("y_tiles_2_4", [P, 2 * DI], F32, offset=nc.sbuf_base - 4 * KT * TP)
        cst = sb("cst", [P, K_ALL])
        colp = sb("colp", [P, Q_ALL])
        siluc = sb("siluc", [P, 2 * KT])
        ssplit = sb("ssplit", [P, KT, 4], F32R)
        modc = sb("modc", [P, 6 * KT, 2])
        dts = sb("dts", [P, NT, 2 * NH])
        dta = sb("dta", [P, NT, 2 * NH])
        dec = sb("dec", [P, NT, 3, 2 * NH])
        sdt = sb("sdt", [P, NT, 2 * NH])
        wdh = sb("wdh", [P, KT, 2 * NH], F32R)
        wdl = sb("wdl", [P, KT, 2 * NH], F32R)
        st6 = sb("st6", [P, NT, 4, 6])
        mv = sb("mv", [P, NT, 4])
        dsk = sb("dsk", [P, NH])
        opened = sb("opened", [1, 8])
        grow = sb("grow", [2 * KT, 2, P])
        A0 = -(-nc.sbuf_base // 64) * 64
        AR = (nc.sbuf_top - A0) // 4
        arena = nc.alloc_sbuf_tensor_at("arena", [P, AR], F32, offset=A0)
        ident = cst[:, K_ID:K_ID + P]
        mask = lambda k: cst[:, k:k + P]

        class Carve:

            def __init__(self, at=0):
                self.at = at

            def __call__(self, *shape):
                n = math.prod(shape)
                v = arena[:, self.at:self.at + n]
                self.at += n
                assert self.at <= AR, (self.at, AR)
                if len(shape) == 1:
                    return v
                names = "abcd"[:len(shape)]
                return v.rearrange(f"p ({' '.join(names)}) -> p {' '.join(names)}",
                                   **{x: y for x, y in zip(names[1:], shape[1:])})

        c0 = Carve()
        xin = c0(NT, D)
        prow = c0(4, P)
        hf = c0(2, TP)
        mod0 = c0(KT, KT, BW)
        mrow0 = mod0[0:4, 0].rearrange("p k n -> p (k n)")
        c1 = Carve()
        mraw = c1(2, KT, BW)
        xpad = c1(2, TP + 2)
        cvo = c1(2, NCONV)
        cvs = c1(2, NCONV)
        nst = c1(2, NT, P)
        base = Carve()
        rq = base(NT, (HQ + HKV) * HD)
        vn = base(NT, HKV * HD)
        vc = base(PAST // P, HKV * HD)
        kcr = base(PAST // P, HKV * HD)
        c2 = Carve(max(base.at, c1.at))
        q5 = c2(2, NT, BW)
        t5 = c2(NT, BW)
        u5 = c2(NT, BW)
        nrow = c2(2, HD)
        ms = c2(NT, 2)
        kout = c2(HKV * HD)
        wdt = c2(KT, 2 * NH)
        dtb = c2(2 * NH)
        alg = c2(2 * NH)
        dtu = c2(3, NT, 2 * NH)
        mrow = t5.rearrange("p t n -> p (t n)")[0:4, 0:2 * BW]
        c2.at = -(-c2.at // 8) * 8
        mwh = nc.alloc_sbuf_tensor_at("mod_hi", [P, 2, KT, BW], F32R, offset=A0 + 4 * c2.at)
        mwl = nc.alloc_sbuf_tensor_at("mod_lo", [P, 2, KT, BW], F32R, offset=A0 + 4 * (c2.at + 2 * KT * BW))
        assert c2.at + 4 * KT * BW <= AR
        c3 = Carve(base.at)
        zst = c3(2, NT, BW)
        gst = c3(2, TP)
        c4 = Carve(base.at)
        qT = c4(HQ + HKV, NT * P)
        kcT = c4(HKV, PAST)
        pr = c4(2, LAT + PAST)
        pT = c4(2, (LAT + PAST) // P, LAT)
        sm = c4(2, 16)
        c4b = Carve(base.at)
        gat = c4b(2, TP)
        ast = c4b(2, TP)
        c5 = Carve()
        xs0, bn0, bc0 = c5(NH, SP_), c5(NG, NS), c5(2 * NG, P)
        rawf = raw[:].rearrange("p s k n -> p (s k n)")
        xs1 = rawf[:, 0:DI].rearrange("p (h q) -> p h q", q=SP_)
        bc1 = rawf[:, DI:2 * DI].rearrange("p (g t) -> p g t", t=P)
        bn1 = c5(NG, NS)
        xs_s, bn_s, bc_s = (xs0, xs1), (bn0, bn1), (bc0, bc1)
        zc = c5(DI)
        ysb = (y13, y24)
        xdf, xdb, xwf = (c5(2, 8, SP_) for _ in range(3))
        xwb = cst[:, K_COS:K_COS + 8 * P].rearrange("p (s h q) -> p s h q", h=8, q=SP_)
        rr = c5(2, 2, R, P)
        ee = c5(2, R, P)
        mm = c5(2, 2, R, P)
        cbm = c5(2, NG, P)
        yy = c5(NH, SP_)
        hF = c5(NH, SP_)
        hB = c5(NH, SP_)
        backs = (hB, yy, zc.rearrange("p (h q) -> p h q", q=SP_), hB)
        h0raw = (y24[:, 0:DI], y24[:, DI:2 * DI])
        tq = y13[:, 2 * DI:].rearrange("p (h q) -> p h q", q=SP_)
        YW = 2 * KT * TP
        yh = nc.alloc_sbuf_tensor_at("yh", [P, 2 * KT, TP], F32R, offset=A0)
        yl = nc.alloc_sbuf_tensor_at("yl", [P, 2 * KT, TP], F32R, offset=A0 + 4 * YW)
        c6 = Carve(2 * YW)
        mrg = c6(TP)
        gbt = cst[:, P:P + TP]
        m1t = cst[:, P + TP:P + 2 * TP]
        c7 = Carve()
        fh = nc.alloc_sbuf_tensor_at("fh", [P, KT, TP], F32R, offset=A0)
        fl = nc.alloc_sbuf_tensor_at("fl", [P, KT, TP], F32R, offset=A0 + 2 * YW)
        c8 = Carve(YW)
        x1 = c8(NT, D)
        xo = c8(NT, D)
        c8.at = max(c8.at, c6.at)
        g1r = c8(2, D)
        row = c8(D)
        hf2 = cst[:, P:P + 2 * TP].rearrange("p (a b) -> p a b", a=2)
        lnr = c7(2, D)
        lnr2 = raw[:, 0].rearrange("p (a k) n -> p a (k n)", a=2)
        xq = c7(NT, D)
        acc = ctx.enter_context(nc.psum_tensor("acc", [P, 4, 512], F32))
        tp = ctx.enter_context(nc.psum_tensor("tp", [P, 4, 512], F32))
        modp = tp[:, 2, 0:8 * KT].rearrange("p (b c) -> p b c", c=4)
        names = """rows_in rows_turned silu_ok x_in xn_ok hi_of_h h_ok modc_ok mod_used mod_hi_done mod_lo_done
            mod_rows mod_cols cond_hi cond_lo raw_in0 raw_in1 mraw_in0 mraw_in1 hi_done lo_done w_half
            acc_ready acc_free dve_step act_step conv_ok conv_silu turned turned_free nat_out0 nat_out1
            conv_out0 conv_out1 dt_in dt_split dt_hi dt_mm dt_abs dt_soft dt_sums dt_exp dt_ok qkv_in rot_ok
            out_kv zst_out0 zst_out1 gst_out0 gst_out1 score_ready max_ok exp_ok prob_ok pv_ready att_hi att_ok
            gat_in0 gat_in1 ast_out0 ast_out1 chunk_in0 chunk_in1 z_in hb_in dsk_in h0_in h0_turned h0_ok
            cb_ready cb_ok rise_ok seg_ready e_ok m_ok xd_ok group_ready states_ready carried_ok quad_ok sq_in
            sq_ok chunk_ok hb_out st_copied st_out kout_ok qk_turned qk_copied p_turned p_copied back_ready
            back_ok xwb_ok mod_copied pad_ok dt_summed var_ok dev_ok y_turned y_hi y_ok gm_in merge_sum
            merge_hi merge_ok gate_turned gate_copied gate_out rows2_in x1_ok h2_hi h2_ok relu_ok square_ok
            ff_ok final_ok out_done norm_in g1_in hb_first_out""".split() + [f"mod_in{r}" for r in range(KT)]
        s = {n: ctx.enter_context(nc.semaphore(n)) for n in names}
        OPEN = ("nat_out", "conv_out", "zst_out", "gst_out")
        pair = lambda n: [count(s[n + b], 16, 1 if n in OPEN else 0) for b in "01"]
        W = lambda ap: ap.rearrange("(k p) n -> p k n", p=P)
        w_mod, w_in = W(a["w_mod"][0]), W(a["w_in"][0])
        w_ao, w_so, w_out = W(a["w_attn_o"][0]), W(a["w_ssd_o"][0]), W(a["w_out"][0])
        w_1, w_2 = W(a["w_mlp1"][0]), W(a["w_mlp2"][0])
        block = ctx.enter_context(nc.Block())
        U_XBC = KT
        U_QKV = U_XBC + 2 * XBC // BW
        U_Z = U_QKV + 6 * NT
        U_G = U_Z + DI // BW * NT
        U_AO = U_G + 2 * 2 * D // BW
        U_SO = U_AO + KT
        U_OUT = U_SO + KT
        U_H2 = U_OUT + 4 * NT
        U_MLP = U_H2 + KT
        B_QKV = XBC // BW
        B_AO = B_QKV + 6 + DI // BW + 2 * D // BW
        B_SO = B_AO + 4
        B_OUT = B_SO + 8
        B_MLP = B_OUT + 4
        N_SCORE = LAT // P * HQ
        CHUNKS = [0, 4, 3, 2, 1, 2, 3, 4]

        RX, RB, RC = DI // P // 4, BC // P // 4, BC // P // 4
        NKC = PAST // P

        @block.sync
        def _(sp):
            sp.dma_start(cst[:], a["consts"]).then_inc(s["rows_in"], 16)
            cw = a["conv_w"][0].rearrange("t (c p) -> (t c) p", p=P)
            rows = lambda ap: ap.rearrange("o (c p) -> (o c) p", p=P)
            sp.dma_start(prow[:, 0], cw[0:P]).then_inc(s["rows_in"], 16)
            sp.dma_start(prow[0:32, 1], cw[P:160]).then_inc(s["rows_in"], 16)
            sp.dma_start(prow[32:64, 1], rows(a["conv_b"])).then_inc(s["rows_in"], 16)
            sp.dma_start(prow[64:80, 1], rows(a["ssd_norm"])).then_inc(s["rows_in"], 16)
            sp.dma_start(prow[80:112, 1], rows(a["b_mlp1"])).then_inc(s["rows_in"], 16)
            sp.dma_start(prow[0:48, 2], rows(a["b_mod"])).then_inc(s["rows_in"], 16)
            sp.dma_start(prow[0:8, 3], a["c_ctx"].rearrange("(c p) -> c p", p=P)).then_inc(s["rows_in"], 16)
            sp.dma_start(prow[8:16, 3], rows(a["c"])).then_inc(s["rows_in"], 16)
            raws, mraws = pair("raw_in"), pair("mraw_in")
            lo, mlo = count(s["lo_done"]), count(s["mod_lo_done"])
            step(mlo, KT)

            def load(slot, src):
                sp.dma_start(raw[:, slot], src).then_inc(raws[slot]["sem"], step(raws[slot]))

            sp.dma_start(mod0[:, 0], w_mod[:, :, 0:BW]).then_inc(s["mod_in0"], 16)
            sp.dma_start(xin[:, 0], a["x_prompt"][0]).then_inc(s["x_in"], 16)
            sp.dma_start(xin[:, 1:NT], a["x_sample"][0].rearrange("(t p) d -> p t d", p=P)).then_inc(s["x_in"], 16)
            for r in range(1, KT):
                sp.dma_start(mod0[:, r], w_mod[:, :, r * BW:(r + 1) * BW]).then_inc(s[f"mod_in{r}"], 16)
            for b in range(2):
                load(b, w_in[:, :, C_XBC + b * BW:C_XBC + (b + 1) * BW])
                step(lo)
            sp.wait_ge(s["h_ok"], KT)
            for b in range(2):
                sp.dma_start(mraw[:, b], w_mod[:, :, (8 + b) * BW:(9 + b) * BW]).then_inc(mraws[b]["sem"], step(mraws[b]))
                step(mlo)
            sp.dma_start(wdt, w_in[:, :, C_DT:C_DT + 2 * NH]).then_inc(s["dt_in"], 16)
            sp.dma_start(dtb, a["dt_bias"].rearrange("o a h -> o (a h)")[0].partition_broadcast(P)).then_inc(s["dt_in"], 16)
            sp.dma_start(alg, a["a_log"].rearrange("o a h -> o (a h)")[0].partition_broadcast(P)).then_inc(s["dt_in"], 16)
            with rounds(sp, RX + RB + RC - 1, (raws[0], 1), (raws[1], 1), (mraws[0], 1), (mraws[1], 1),
                        (lo, 2), (mlo, 2)) as i:
                for b in range(2):
                    step(lo)
                    if some(lo, 2):
                        sp.wait_ge(lo["sem"], value(lo, 2))
                    load(b, w_in[:, :, bass.ds(i * (2 * BW) + (C_XBC + (b + 2) * BW), BW)])
                for b in range(2):
                    step(mlo)
                    sp.wait_ge(mlo["sem"], value(mlo, 2))
                    sp.dma_start(mraw[:, b], w_mod[:, :, bass.ds(i * (2 * BW) + (10 + b) * BW, BW)]).then_inc(mraws[b]["sem"], step(mraws[b]))

            def stream(n, src, col):
                with rounds(sp, n, (raws[0], 1), (raws[1], 1), (lo, 2)) as i:
                    for b in range(2):
                        step(lo)
                        if some(lo, 2):
                            sp.wait_ge(lo["sem"], value(lo, 2))
                        load(b, src[:, :, bass.ds(i * (2 * BW) + (col + b * BW), BW)])

            for b in range(2):
                step(lo)
                if some(lo, 2):
                    sp.wait_ge(lo["sem"], value(lo, 2))
                load(b, w_in[:, :, b * BW:(b + 1) * BW])
            sp.dma_start(nrow[:, 0], a["q_norm"][0].partition_broadcast(P)).then_inc(s["norm_in"], 16)
            sp.dma_start(nrow[:, 1], a["k_norm"][0].partition_broadcast(P)).then_inc(s["norm_in"], 16)
            for c in pair("nat_out"):
                step(c, 2 * (RX + RB))
                sp.wait_ge(c["sem"], value(c))
            for c in pair("conv_out"):
                step(c, 2 * 2 * (RB + RC))
                sp.wait_ge(c["sem"], value(c))
            hk = lambda ap: ap[0, 0].rearrange("(t p) h d -> p t (h d)", p=P)
            sp.dma_start(kcr, hk(a["cache_k"])).then_inc(s["qkv_in"], 16)
            sp.dma_start(vc, hk(a["cache_v"])).then_inc(s["qkv_in"], 16)
            stream(2, w_in, 2 * BW)
            stream(4, w_in, C_Z)
            stream(4, w_in, C_G)
            stream(2, w_ao, 0)
            sp.wait_ge(s["att_ok"], HQ + HKV)
            gat_in = pair("gat_in")
            for k in range(KT):
                if k >= 2:
                    sp.wait_ge(s["acc_free"], U_AO + k - 1)
                sp.dma_start(gat[:, k % 2], g_d[k]).then_inc(gat_in[k % 2]["sem"], step(gat_in[k % 2]))

            flat = lambda t: t.rearrange("p h q -> p (h q)")
            cin = pair("chunk_in")

            def chunk_in(j):
                slot, c = j % 2, CHUNKS[j]
                if j >= 2:
                    sp.wait_ge(s["chunk_ok"], j - 1)
                sp.dma_start(flat(xs_s[slot]), xs_d[c]).then_inc(cin[slot]["sem"], step(cin[slot]))
                sp.dma_start(flat(bn_s[slot]), bn_d[c]).then_inc(cin[slot]["sem"], step(cin[slot]))
                if j not in (1, 2, 3):
                    sp.dma_start(flat(bc_s[slot]), bct_d[c].rearrange("p g t -> p (g t)")).then_inc(cin[slot]["sem"], step(cin[slot]))

            sp.wait_ge(s["acc_free"], U_SO)
            for c in pair("ast_out"):
                step(c, KT // 2)
                sp.wait_ge(c["sem"], value(c))
            sp.wait_ge(s["lo_done"], B_SO)
            sp.dma_start(dsk[:], a["d_skip"][0].partition_broadcast(P)).then_inc(s["dsk_in"], 16)
            chunk_in(0)
            sp.dma_start(zc, z_d[0]).then_inc(s["z_in"], 16)
            chunk_in(1)
            for d, buf in enumerate(h0raw):
                h0 = a["state_ssd"][0, 0, d].rearrange("(j h) q n -> (h q) j n", h=2)
                sp.dma_start(buf.rearrange("p (j n) -> p j n", n=NS), h0).then_inc(s["h0_in"], 16)
            for j in range(2, 5):
                chunk_in(j)
            sp.wait_ge(s["h0_turned"], 8)
            for j in range(4, 8):
                sp.wait_ge(s["chunk_ok"], j)
                if j == 4:
                    sp.wait_ge(s["hb_first_out"], 16)
                    sp.wait_ge(s["hb_out"], 16 * 3)
                sp.dma_start(flat(hB), hb_d[j - 3]).then_inc(s["hb_in"], 16)
                sp.dma_start(zc, z_d[j - 3]).then_inc(s["z_in"], 16)
                if j < 7:
                    chunk_in(j + 1)

            sp.wait_ge(s["chunk_ok"], 8)
            jump(lo, B_SO)

            for b in range(2):
                step(lo)
                load(b, w_so[:, b * KT:(b + 1) * KT, 0:BW])
            sp.wait_ge(s["gate_out"], 32)
            for n in range(2):
                sp.dma_start(g1r[:, n].rearrange("p (k c) -> p k c", c=P), gr_d[0, :, n].partition_broadcast(P)).then_inc(s["g1_in"], 16)
            with rounds(sp, 3, (raws[0], 1), (raws[1], 1), (lo, 2)) as i:
                for b in range(2):
                    step(lo)
                    if some(lo, 2):
                        sp.wait_ge(lo["sem"], value(lo, 2))
                    load(b, w_so[:, b * KT:(b + 1) * KT, bass.ds(i * BW + BW, BW)])
            stream(2, w_out, 0)
            sp.wait_ge(s["merge_ok"], KT)
            sp.wait_ge(s["acc_ready"], U_OUT)
            sp.dma_start(xo[:, 0], a["x_prompt"][0]).then_inc(s["rows2_in"], 16)
            sp.dma_start(xo[:, 1:NT], a["x_sample"][0].rearrange("(t p) d -> p t d", p=P)).then_inc(s["rows2_in"], 16)
            sp.dma_start(lnr[:, 0], a["ln1_g"][0].partition_broadcast(P)).then_inc(s["rows2_in"], 16)
            sp.dma_start(lnr[:, 1], a["ln1_b"][0].partition_broadcast(P)).then_inc(s["rows2_in"], 16)
            sp.dma_start(row, a["b_mlp2"][0].partition_broadcast(P)).then_inc(s["rows2_in"], 16)

            for b in range(2):
                step(lo)
                if some(lo, 2):
                    sp.wait_ge(lo["sem"], value(lo, 2))
                load(b, w_1[:, :, b * BW:(b + 1) * BW])
            with rounds(sp, 3, (raws[0], 4), (raws[1], 4), (lo, 8)) as i:
                for b in range(2, 4):
                    step(lo)
                    if some(lo, 2):
                        sp.wait_ge(lo["sem"], value(lo, 2))
                    load(b % 2, w_1[:, :, bass.ds(i * D + b * BW, BW)])
                for b in range(4):
                    step(lo)
                    if some(lo, 2):
                        sp.wait_ge(lo["sem"], value(lo, 2))
                    load(b % 2, w_2[:, bass.ds(i * KT, KT), b * BW:(b + 1) * BW])
                for b in range(2):
                    step(lo)
                    if some(lo, 2):
                        sp.wait_ge(lo["sem"], value(lo, 2))
                    load(b, w_1[:, :, bass.ds(i * D + (D + b * BW), BW)])
            sp.wait_ge(s["h2_ok"], KT)
            for n in range(2):
                sp.dma_start(g1r[:, n].rearrange("p (k c) -> p k c", c=P), gr_d[1, :, n].partition_broadcast(P)).then_inc(s["rows2_in"], 16)
            for b in range(2, 4):
                step(lo)
                if some(lo, 2):
                    sp.wait_ge(lo["sem"], value(lo, 2))
                load(b % 2, w_1[:, :, 3 * D + b * BW:3 * D + (b + 1) * BW])
            for b in range(4):
                step(lo)
                if some(lo, 2):
                    sp.wait_ge(lo["sem"], value(lo, 2))
                load(b % 2, w_2[:, 3 * KT:4 * KT, b * BW:(b + 1) * BW])
            sp.wait_ge(lo["sem"], value(lo, 1))
            sp.dma_start(lnr2[:, 0], a["ln2_g"][0].partition_broadcast(P)).then_inc(s["rows2_in"], 16)
            sp.dma_start(lnr2[:, 1], a["ln2_b"][0].partition_broadcast(P)).then_inc(s["rows2_in"], 16)
            for t in range(NT):
                sp.wait_ge(s["final_ok"], t + 1)
                dst = y_p[0] if t == 0 else y_s[0, (t - 1) * P:t * P]
                sp.dma_start(dst, xo[:, t]).then_inc(s["out_done"], 16)
            sp.wait_ge(s["out_done"], 16 * NT)

        @block.gpsimd
        def _(po):
            for j, n in enumerate(n + b for n in OPEN for b in "01"):
                po.dma_start(opened[0:1, j:j + 1], a["d_skip"][0:1, 0:1]).then_inc(s[n], 16)
            nat_out, conv_out = pair("nat_out"), pair("conv_out")
            turned, silu = count(s["turned_free"]), count(s["conv_silu"])
            step(turned)

            def store_turned(u, dst):
                po.wait_ge(turned["sem"], due(turned))
                po.dma_start(dst, nst[:, u]).then_inc(nat_out[u]["sem"], step(nat_out[u]))

            def store_conv(u, g):
                po.wait_ge(silu["sem"], due(silu))
                to = bct_d[:, :, g]
                po.dma_start(to[0], cvs[:, u, 0:P]).then_inc(conv_out[u]["sem"], step(conv_out[u]))
                po.dma_start(to[1:NT].rearrange("c p o t -> p c (o t)"),
                                                cvs[:, u, 2 + P:NCONV].rearrange("p (c t) -> p c t", t=P)).then_inc(conv_out[u]["sem"], step(conv_out[u]))

            nat = lambda t, col: t.rearrange("t p c -> p t c")[:, :, bass.ds(col, P)]
            with rounds(po, RX, (turned, 4), (silu, 4), (nat_out[0], 2), (nat_out[1], 2)) as i:
                for n in range(4):
                    step(silu)
                    store_turned(n % 2, nat(xs_d, i * (4 * P) + n * P))
            with rounds(po, RB, (turned, 4), (silu, 4), (nat_out[0], 2), (nat_out[1], 2), (conv_out[0], 4), (conv_out[1], 4)) as i:
                for n in range(4):
                    store_conv(n % 2, bass.ds(i * 4 + n, 1))
                    store_turned(n % 2, nat(bn_d, i * (4 * P) + n * P))
            with rounds(po, RC, (silu, 4), (conv_out[0], 4), (conv_out[1], 4)) as i:
                for n in range(4):
                    store_conv(n % 2, bass.ds(i * 4 + (NG + n), 1))
            po.wait_ge(s["kout_ok"], 1)
            po.dma_start(out_k[0, 0].rearrange("t h d -> t (h d)"), kout).then_inc(s["out_kv"], 16)
            free = count(s["acc_free"])
            jump(free, U_Z)
            po.wait_ge(free["sem"], value(free))
            po.dma_start(out_v[0, 0].rearrange("t h d -> t (h d)"), vn[:, 0]).then_inc(s["out_kv"], 16)
            for n in range(2):
                po.wait_ge(s["gate_copied"], n + 1)
                po.dma_start(gr_d[n].rearrange("k c p -> (k c) p"), grow[:, n]).then_inc(s["gate_out"], 16)
            zo, go = pair("zst_out"), pair("gst_out")
            with rounds(po, 4, (free, 2 * NT), (zo[0], 1), (zo[1], 1)) as i:
                for b in range(2):
                    step(free, NT)
                    po.wait_ge(free["sem"], value(free))
                    po.dma_start(z_d.rearrange("t p c -> p t c")[:, :, bass.ds(i * (2 * BW) + b * BW, BW)], zst[:, b]).then_inc(zo[b]["sem"], step(zo[b]))
            with rounds(po, 4, (free, 4), (go[0], 2), (go[1], 2)) as i:
                for n in range(4):
                    po.wait_ge(free["sem"], due(free))
                    po.dma_start(g_d[bass.ds(i * 4 + n, 1)].rearrange("o p t -> p (o t)"), gst[:, n % 2]).then_inc(go[n % 2]["sem"], step(go[n % 2]))
            ao = pair("ast_out")
            with rounds(po, 2, (free, 4), (ao[0], 2), (ao[1], 2)) as i:
                for n in range(4):
                    po.wait_ge(free["sem"], due(free))
                    po.dma_start(m1_d[bass.ds(i * 4 + n, 1)].rearrange("o p t -> p (o t)"), ast[:, n % 2]).then_inc(ao[n % 2]["sem"], step(ao[n % 2]))
            flat = lambda t: t.rearrange("p h q -> p (h q)")
            po.wait_ge(s["st_copied"], 8)
            for d, buf in ((0, hF), (1, hB)):
                dst = out_st[0, 0, d].rearrange("(j h) q n -> (h q) j n", h=2)
                po.dma_start(dst, flat(buf).rearrange("p (j n) -> p j n", n=NS)).then_inc(s["st_out"], 16)
            po.wait_ge(s["h0_ok"], 8)
            po.dma_start(hb_d[NT - 1], flat(hB)).then_inc(s["hb_first_out"], 16)
            for j in range(1, 4):
                po.wait_ge(s["chunk_ok"], j + 1)
                po.dma_start(hb_d[NT - 1 - j], flat(backs[j])).then_inc(s["hb_out"], 16)
            po.wait_ge(s["chunk_ok"], 8)
            for k in range(KT):
                if k:
                    po.wait_ge(s["merge_sum"], k)
                po.dma_start(gbt, g_d[KT + k]).then_inc(s["gm_in"], 16)
                po.dma_start(m1t, m1_d[k]).then_inc(s["gm_in"], 16)
            po.wait_ge(s["out_kv"], 32)
            po.wait_ge(s["gate_out"], 32)

        @block.tensor
        def _(pe):
            lo, ready, free = count(s["lo_done"]), count(s["acc_ready"]), count(s["acc_free"])
            mlo, mod_used = count(s["mod_lo_done"]), count(s["mod_used"])
            turned, tfree, silu = count(s["turned"]), count(s["turned_free"]), count(s["conv_silu"])
            mcopied = count(s["mod_copied"])

            def mul(out, l, r, first=True, last=True):
                return pe.matmul(out, l, r, start=first, stop=last)

            pe.wait_ge(s["rows_in"], 16 * 9)
            for j, n, q in ((0, P, Q_CONV), (1, 112, P), (2, 48, Q_BM), (3, 16, Q_C)):
                last = pe.transpose(tp[:, 0, q:q + n], prow[0:n, j], ident[0:n, 0:n])
            last.then_inc(s["rows_turned"], 1)

            def mod_block(wh, wl, out):
                for k in range(KT):
                    last_k = k == KT - 1
                    if last_k:
                        mul(out[0:2], ssplit[:, k, 0:2], wl[:, k], False, False)
                    last = mul(out, ssplit[:, k], wh[:, k], k == 0, last_k)
                    if not last_k:
                        mul(out[0:2], ssplit[:, k, 0:2], wl[:, k], False, False)
                return last

            def mod_columns(out, rows, n):
                for j in range(n):
                    last = mul(out[:, j], rows[0:4, j * P:(j + 1) * P], ident[0:4, 0:4])
                return last

            pe.wait_ge(s["cond_lo"], 1)
            for r in range(KT):
                pe.wait_ge(mlo["sem"], due(mlo))
                mod_block(whi[:, r % 2], wlo[:, r % 2], acc[0:4, r // 2, r % 2 * BW:(r % 2 + 1) * BW]).then_inc(mod_used["sem"], step(mod_used))
            pe.wait_ge(s["mod_rows"], 1)
            mod_columns(modp, mrow0, 2 * KT).then_inc(s["mod_cols"], 1)

            def turn_x(src, ok, n):
                pe.wait_ge(s[ok], n)
                for k in range(KT):
                    step(free)
                    if some(free, 2):
                        pe.wait_ge(free["sem"], value(free, 2))
                    u = k % 2
                    for t in range(NT):
                        dst = acc[:, 2 * u + 1, 0:P] if t == 0 else acc[:, 2 * u, (t - 1) * P:t * P]
                        last = pe.transpose(dst, src[:, t, k * P:(k + 1) * P], ident)
                    last.then_inc(ready["sem"], step(ready))

            turn_x(xin, "xn_ok", NT)

            def t_pass(slot, sub, u, mh, ml, k0=0, first=True, end=True):
                for k in range(KT):
                    for w, m in ((whi, mh), (whi, ml), (wlo, mh)):
                        for half in range(2):
                            last = mul(acc[:, 2 * u + half, 0:HALF], w[:, slot, k, sub * P:(sub + 1) * P],
                                       m[:, k0 + k, half * HALF:(half + 1) * HALF],
                                       first and k == 0 and w is whi and m is mh, end and k == KT - 1 and w is wlo)
                return last

            def t_unit(slot, sub, u, mh, ml):
                step(free)
                if some(free, 2):
                    pe.wait_ge(free["sem"], value(free, 2))
                t_pass(slot, sub, u, mh, ml).then_inc(ready["sem"], step(ready))

            def n_block(slot, mh, ml):
                for t in range(NT):
                    u = (NT * slot + t) % 2
                    step(free)
                    if some(free, 2):
                        pe.wait_ge(free["sem"], value(free, 2))
                    for k in range(KT):
                        for m, w in ((mh, whi), (mh, wlo), (ml, whi)):
                            last = mul(acc[:, 2 * u, 0:BW], m[:, k, tok(t):tok(t) + P], w[:, slot, k],
                                       k == 0 and w is whi and m is mh, k == KT - 1 and m is ml)
                    last.then_inc(ready["sem"], step(ready))

            def turn_tile(n):
                pe.wait_ge(silu["sem"], due(silu))
                step(tfree)
                if some(tfree, 1):
                    pe.wait_ge(tfree["sem"], value(tfree, 1))
                for t in range(NT):
                    dst = tp[:, 1, 0:P] if t == 0 else tp[:, 0, (t - 1) * P:t * P]
                    last = pe.transpose(dst, cvs[:, n % 2, tok(t):tok(t) + P], ident)
                last.then_inc(turned["sem"], step(turned))

            def xbc_round(turning):
                for n in range(4):
                    if n % 2 == 0:
                        pe.wait_ge(lo["sem"], due(lo))
                    t_unit(n // 2, n % 2, n % 2, hh, hl)
                    if turning and n:
                        turn_tile(n - 1)
                for b in range(2):
                    pe.wait_ge(mlo["sem"], due(mlo))
                    mod_block(mwh[:, b], mwl[:, b], tp[0:4, 2, b * BW:(b + 1) * BW]).then_inc(mod_used["sem"], step(mod_used))
                if turning:
                    turn_tile(3)
                pe.wait_ge(mrows["sem"], due(mrows))
                step(mcopied)
                pe.wait_ge(mcopied["sem"], value(mcopied, 1))
                out = tp[:, 3, 0:16].rearrange("p (b c) -> p b c", c=4)
                mod_columns(out, mrow, 4).then_inc(mcols["sem"], step(mcols))

            mrows, mcols = count(s["mod_rows"], 1, 1), count(s["mod_cols"], 1, 1)
            pe.wait_ge(s["h_ok"], KT)
            step(tfree)
            step(mcopied)
            every = [(lo, 2), (ready, 4), (free, 4), (mlo, 2), (mod_used, 2), (mcopied, 1), (mrows, 1), (mcols, 1)]
            with rounds(pe, RX + RB, *every, (turned, 4), (tfree, 4), (silu, 4)):
                xbc_round(True)
            with rounds(pe, RC, *every):
                xbc_round(False)

            pe.wait_ge(s["dt_split"], 1)
            pe.wait_ge(mcopied["sem"], value(mcopied))
            pe.wait_ge(tfree["sem"], value(tfree))
            for t in range(NT):
                for k in range(KT):
                    for m, w in ((hh, wdh), (hh, wdl), (hl, wdh)):
                        last = mul(tp[:, 0, t * 2 * NH:(t + 1) * 2 * NH], m[:, k, tok(t):tok(t) + P], w[:, k],
                                   k == 0 and w is wdh and m is hh, k == KT - 1 and m is hl)
            last.then_inc(s["dt_mm"], 1)

            n_each = [(lo, 2), (ready, 2 * NT), (free, 2 * NT)]
            t_each = [(lo, 2), (ready, 4), (free, 4)]

            def n_stream(n, mh, ml):
                with rounds(pe, n, *n_each):
                    for b in range(2):
                        pe.wait_ge(lo["sem"], due(lo))
                        n_block(b, mh, ml)

            def t_stream(n, mh, ml):
                with rounds(pe, n, *t_each):
                    for u in range(4):
                        if u % 2 == 0:
                            pe.wait_ge(lo["sem"], due(lo))
                        t_unit(u // 2, u % 2, u % 2, mh, ml)

            n_stream(3, hh, hl)
            pe.wait_ge(s["dt_sums"], 1)
            for j, (f, b) in enumerate(((K_LE, K_GE), (K_GT, K_LT), (K_ONE, K_ONE))):
                o = tp[:, 1 + j, 0:NT * 2 * NH].rearrange("p (t h) -> p t h", t=NT)
                mul(o[:, :, 0:NH], mask(f), dta[:, :, 0:NH])
                last = mul(o[:, :, NH:], mask(b), dta[:, :, NH:])
            last.then_inc(s["dt_summed"], 1)
            pe.wait_ge(s["modc_ok"], 1)
            for n, c in ((0, 2), (1, 5)):
                last = pe.transpose(tp[0:2 * KT, 0, n * P:(n + 1) * P],
                                    modc[:, c * KT:(c + 1) * KT].rearrange("p k c -> p (k c)"), ident)
            last.then_inc(s["gate_turned"], 1)
            n_stream(4, hh, hl)
            t_stream(4, hh, hl)

            pe.wait_ge(s["dt_ok"], 1)
            pe.wait_ge(s["gate_copied"], 2)
            pe.wait_ge(s["rot_ok"], 5)
            pe.wait_ge(s["qkv_in"], 32)
            turned = count(s["qk_turned"])
            tfree = count(s["qk_copied"])

            def turn_qk(tiles):
                step(tfree)
                if some(tfree, 1):
                    pe.wait_ge(tfree["sem"], value(tfree, 1))
                tiles().then_inc(turned["sem"], step(turned))

            def q_tiles(h):
                for t in range(NT):
                    dst = tp[:, 1, 0:P] if t == 0 else tp[:, 0, (t - 1) * P:t * P]
                    last = pe.transpose(dst, rq[:, t, h * HD:(h + 1) * HD], ident)
                return last

            def cached_tiles():
                for h in range(HKV):
                    for t in range(NKC):
                        j = h * NKC + t
                        last = pe.transpose(tp[:, 0, j * P:(j + 1) * P], kcr[:, t, h * HD:(h + 1) * HD], ident)
                return last

            for h in range(HQ + HKV):
                turn_qk(lambda: q_tiles(h))
            turn_qk(cached_tiles)
            pe.wait_ge(free["sem"], value(free))
            score, prob = count(s["score_ready"]), count(s["prob_ok"])
            expd, pv, pvf = count(s["exp_ok"]), count(s["pv_ready"]), count(s["att_ok"])
            pt_turned, pt_free = count(s["p_turned"]), count(s["p_copied"])
            pe.wait_ge(tfree["sem"], value(tfree))

            def scores(n):
                u = n % 2
                if n < N_SCORE:
                    h, t = n // 4, n % 4
                    step(expd)
                    if some(expd, 2):
                        pe.wait_ge(expd["sem"], value(expd, 2))
                    q = qT[:, h, t * P:(t + 1) * P]
                    mul(acc[:, 2 * u, 0:LAT], q, qT[:, HQ + h // R, 0:LAT])
                    last = mul(acc[:, 2 * u + 1, 0:PAST], q, kcT[:, h // R])
                else:
                    g = n - N_SCORE
                    step(expd)
                    if some(expd, 2):
                        pe.wait_ge(expd["sem"], value(expd, 2))
                    for r in range(R):
                        last = mul(acc[:, 2 * u, r * P:(r + 1) * P], qT[:, R * g + r, LAT:], qT[:, HQ + g, LAT:])
                last.then_inc(score["sem"], step(score))

            def turn_p(n):
                u = n % 2
                pe.wait_ge(prob["sem"], due(prob))
                step(pt_free)
                if some(pt_free, 1):
                    pe.wait_ge(pt_free["sem"], value(pt_free, 1))
                for j in range(6 if n < N_SCORE else R):
                    last = pe.transpose(tp[:, j // 4, (j % 4) * P:(j % 4 + 1) * P], pr[:, u, j * P:(j + 1) * P], ident)
                last.then_inc(pt_turned["sem"], step(pt_turned))

            def values(h):
                step(pvf)
                if some(pvf, 2):
                    pe.wait_ge(pvf["sem"], value(pvf, 2))
                o = tp[:, 2 + h % 2]
                if h < HQ:
                    pe.wait_ge(s["p_copied"], 4 * (h + 1))
                    for j in range(6):
                        v = (vn[:, 1 + j] if j < 4 else vc[:, j - 4])[:, (h // R) * HD:(h // R + 1) * HD]
                        last = mul(o, v, pT[:, h % 2, j], j == 0, j == 5)
                else:
                    g = h - HQ
                    pe.wait_ge(s["p_copied"], N_SCORE + g + 1)
                    last = mul(o, vn[:, 0, g * HD:(g + 1) * HD], pT[:, h % 2, 0])
                last.then_inc(pv["sem"], step(pv))

            scores(0)
            scores(1)
            for n in range(N_SCORE + HKV):
                if n + 2 < N_SCORE + HKV:
                    scores(n + 2)
                turn_p(n)
                if n % 4 == 1 and 4 < n < N_SCORE:
                    values(n // 4 - 1)
            values(HQ - 1)
            values(HQ)
            values(HQ + 1)

            pe.wait_ge(pvf["sem"], value(pvf))
            t_stream(2, hh, hl)

            cin = pair("chunk_in")
            cbr, cbo, rise, seg, e_ok = (count(s[n]) for n in ("cb_ready", "cb_ok", "rise_ok", "seg_ready", "e_ok"))
            m_ok, xd, grp, quad, qok = (count(s[n]) for n in ("m_ok", "xd_ok", "group_ready", "states_ready", "quad_ok"))
            car = count(s["carried_ok"])
            hbin, stc = count(s["hb_in"], 16), count(s["st_copied"])

            def seg_group(g):
                pe.wait_ge(rise["sem"], due(rise))
                step(e_ok)
                if some(e_ok, 2):
                    pe.wait_ge(e_ok["sem"], value(e_ok, 2))
                mul(acc[:, g % 2], mask(K_GT), rr[:, g % 2, 0].rearrange("p r t -> p (r t)"), True, False)
                mul(acc[:, g % 2], mask(K_LT), rr[:, g % 2, 1].rearrange("p r t -> p (r t)"), False, True).then_inc(seg["sem"], step(seg))

            def scan_chunk(slot, latent):
                b, bc = bn_s[slot], bc_s[slot]
                step(cin[slot], 3)
                pe.wait_ge(cin[slot]["sem"], value(cin[slot]))
                if latent:
                    pe.wait_ge(qok["sem"], value(qok))
                for g in range(NG):
                    last = mul(tp[:, g // 4, (g % 4) * P:(g % 4 + 1) * P], bc[:, g], bc[:, NG + g])
                last.then_inc(cbr["sem"], step(cbr))
                seg_group(0)
                seg_group(1)
                if latent:
                    pe.wait_ge(hbin["sem"], due(hbin))
                for g in range(NG):
                    q, gg = g // 2, g % 2
                    if g + 2 < NG:
                        seg_group(g + 2)
                    yb, sbk = (acc[:, 2], acc[:, 3]) if q % 2 == 0 else (tp[:, 0], tp[:, 1])
                    if gg == 0:
                        pe.wait_ge(xd["sem"], due(xd))
                        states(q, sbk, b, bc, latent)
                    pe.wait_ge(m_ok["sem"], due(m_ok))
                    if gg == 0:
                        step(qok)
                        if some(qok, 2):
                            pe.wait_ge(qok["sem"], value(qok, 2))
                    for r in range(R):
                        j = gg * R + r
                        mul(yb[:, j * SP_:(j + 1) * SP_], mm[:, g % 2, 0, r], xdf[:, q % 2, j], True, False)
                        last = mul(yb[:, j * SP_:(j + 1) * SP_], mm[:, g % 2, 1, r], xdb[:, q % 2, j], False, True)
                    last.then_inc(grp["sem"], step(grp))

            def states(q, sbk, b, bc, latent):
                if latent:
                    step(car)
                    if some(car, 1):
                        pe.wait_ge(car["sem"], value(car, 1))
                else:
                    if some(stc):
                        pe.wait_ge(stc["sem"], value(stc))
                    step(stc, 2)
                for k in (0, 1):
                    w = slice(k * R * SP_, (k + 1) * R * SP_)
                    gk = 2 * q + k
                    heads = slice(gk * R, (gk + 1) * R)
                    if latent:
                        mul(tp[:, 2, w], bc[:, NG + gk], hF[:, heads])
                        mul(tp[:, 3, w], bc[:, NG + gk], hB[:, heads])
                        last = mul(sbk[:, w], b[:, gk], xwf[:, q % 2, k * R:(k + 1) * R])
                    else:
                        for h in (0, 2):
                            j = k * R + h
                            mul(sbk[:, j * SP_:j * SP_ + P], xwf[:, q % 2, j:j + 2], b[:, gk])
                            last = mul(tp[:, 2, j * SP_:j * SP_ + P], xwb[:, q % 2, j:j + 2], b[:, gk])
                last.then_inc(quad["sem"], step(quad))

            pe.wait_ge(s["acc_free"], U_SO)
            scan_chunk(0, False)
            step(car, 4)
            pe.wait_ge(s["h0_in"], 32)
            pe.wait_ge(qok["sem"], value(qok))
            pe.wait_ge(stc["sem"], value(stc))
            h0t, h0c = count(s["h0_turned"]), count(s["h0_ok"])
            for d, buf in enumerate(h0raw):
                for j in range(4):
                    u = (4 * d + j) % 2
                    step(h0c)
                    if some(h0c, 2):
                        pe.wait_ge(h0c["sem"], value(h0c, 2))
                    for n in range(4):
                        c = 4 * j + n
                        last = pe.transpose(tp[:, u, n * P:(n + 1) * P], buf[:, c * P:(c + 1) * P], ident)
                    last.then_inc(h0t["sem"], step(h0t))
            bst, bfree, xwo = count(s["back_ready"]), count(s["back_ok"]), count(s["xwb_ok"])
            for j in range(1, 4):
                step(cin[j % 2], 2)
                pe.wait_ge(cin[j % 2]["sem"], value(cin[j % 2]))
                for q in range(4):
                    pe.wait_ge(xwo["sem"], due(xwo))
                    step(bfree)
                    if some(bfree, 2):
                        pe.wait_ge(bfree["sem"], value(bfree, 2))
                    for k in range(2):
                        last = mul(acc[:, 2 + q % 2, k * R * SP_:(k + 1) * R * SP_], bn_s[j % 2][:, 2 * q + k],
                                   xwb[:, q % 2, k * R:(k + 1) * R])
                    last.then_inc(bst["sem"], step(bst))
            pe.wait_ge(bfree["sem"], value(bfree))
            pe.wait_ge(h0c["sem"], value(h0c))
            every = [(cin[0], 3), (cin[1], 3), (cbr, 2), (rise, 16), (e_ok, 16), (seg, 16), (m_ok, 16), (grp, 16),
                     (qok, 8), (car, 8), (quad, 8), (xd, 8), (hbin, 2)]
            with rounds(pe, 2, *every):
                for b in range(2):
                    scan_chunk(b, True)

            pe.wait_ge(s["chunk_ok"], 8)
            yt, yc = count(s["y_turned"]), count(s["y_ok"])
            for t in range(NT):
                for j in range(4):
                    step(yc)
                    if some(yc, 4):
                        pe.wait_ge(yc["sem"], value(yc, 4))
                    for n in range(4):
                        c = (4 * j + n) * P
                        src = yctx if t == 0 else ysb[(t - 1) % 2][:, (t - 1) // 2 * DI:]
                        last = pe.transpose(tp[:, j, n * P:(n + 1) * P], src[:, c:c + P], ident)
                    last.then_inc(yt["sem"], step(yt))
            pe.wait_ge(yc["sem"], value(yc))
            half = count(s["w_half"])
            with rounds(pe, 4, (lo, 2), (ready, 2), (free, 2), (half, 1)):
                pe.wait_ge(lo["sem"], due(lo))
                for sub in range(2):
                    step(free)
                    if some(free, 2):
                        pe.wait_ge(free["sem"], value(free, 2))
                    last = t_pass(0, sub, sub, yh, yl, 0, True, False)
                last.then_inc(half["sem"], step(half))
                pe.wait_ge(lo["sem"], due(lo))
                for sub in range(2):
                    t_pass(1, sub, sub, yh, yl, KT, False, True).then_inc(ready["sem"], step(ready))
            pe.wait_ge(s["merge_ok"], KT)
            n_stream(2, hh, hl)
            turn_x(xq, "x1_ok", NT)
            pe.wait_ge(s["h2_ok"], KT)
            ff = count(s["ff_ok"])
            with rounds(pe, 4, (lo, 8), (ready, KT + 4 * NT), (free, KT + 4 * NT), (ff, KT)):
                for n in range(KT):
                    if n % 2 == 0:
                        pe.wait_ge(lo["sem"], due(lo))
                    t_unit(n // 2 % 2, n % 2, n % 2, hh, hl)
                for n in range(KT):
                    pe.wait_ge(ff["sem"], due(ff))
                for b in range(4):
                    pe.wait_ge(lo["sem"], due(lo))
                    n_block(b % 2, fh, fl)

        @block.scalar
        def _(act):
            steps = count(s["act_step"])
            ready, free = count(s["acc_ready"]), count(s["acc_free"])
            hi, lo = count(s["hi_done"]), count(s["lo_done"])
            raws = pair("raw_in")

            def split_hi(slot):
                act.wait_ge(raws[slot]["sem"], due(raws[slot]))
                act.activation(whi[:, slot], raw[:, slot], ACT.Copy).then_inc(hi["sem"], step(hi))

            var, dev = count(s["var_ok"]), count(s["dev_ok"])

            def roots(ap):
                act.wait_ge(var["sem"], due(var))
                act.activation(ap, ap, ACT.Sqrt).then_inc(dev["sem"], step(dev))

            def out_of_acc(dst, src, func):
                act.wait_ge(ready["sem"], due(ready))
                act.activation(dst, src, func).then_inc(free["sem"], step(free))

            act.wait_ge(s["rows_turned"], 1)
            act.wait_ge(s["turned_free"], 1)
            act.activation(siluc[:], tp[:, 0, Q_C:Q_C + 2 * KT], ACT.Silu).then_inc(s["silu_ok"], 1)
            act.wait_ge(s["silu_ok"], 1)
            act.activation(ssplit[:, :, 0:2], siluc[:].rearrange("p (c k) -> p k c", k=KT), ACT.Copy).then_inc(s["cond_hi"], 1)
            mhi, mod_used = count(s["mod_hi_done"]), count(s["mod_used"])
            for r in range(KT):
                act.wait_ge(s[f"mod_in{r}"], 16)
                step(mod_used)
                if some(mod_used, 2):
                    act.wait_ge(mod_used["sem"], value(mod_used, 2))
                act.activation(whi[:, r % 2], mod0[:, r], ACT.Copy).then_inc(mhi["sem"], step(mhi))
                if r == NT:
                    roots(mv[:, :, 2])

            act.wait_ge(mod_used["sem"], value(mod_used))
            act.activation(mrow0, acc[0:4].rearrange("p a b -> p (a b)"), ACT.Copy).then_inc(s["mod_rows"], 1)

            def modulated(buf, hi_ok, lo_ok, sc, sh):
                h, l = count(s[hi_ok]), count(s[lo_ok])
                for k in range(KT):
                    u = k % 2
                    act.wait_ge(ready["sem"], due(ready))
                    step(l)
                    if some(l, 2):
                        act.wait_ge(l["sem"], value(l, 2))
                    for m, (dst, src) in enumerate(((buf[:, u, 0:CTX], acc[:, 2 * u + 1, 0:CTX]),
                                                    (buf[:, u, CTX + 2:NCONV], acc[:, 2 * u, 0:LAT]))):
                        last = act.activation(dst, src, ACT.Identity, bias=modc[:, sh * KT + k, m:m + 1],
                                              scale=modc[:, sc * KT + k, m:m + 1])
                    last.then_inc(free["sem"], step(free))
                    act.wait_ge(free["sem"], value(free))
                    act.activation(hh[:, k], buf[:, u], ACT.Copy).then_inc(h["sem"], step(h))

            act.wait_ge(s["mod_copied"], 1)
            act.wait_ge(s["pad_ok"], 1)
            modulated(hf, "hi_of_h", "h_ok", 1, 0)
            split_hi(0)
            split_hi(1)

            conv, silu = count(s["conv_ok"]), count(s["conv_silu"])
            turned, tfree = count(s["turned"]), count(s["turned_free"])
            nat_out, conv_out = pair("nat_out"), pair("conv_out")
            step(tfree)

            def evacuate(n):
                act.wait_ge(padded["sem"], due(padded))
                out_of_acc(xpad[:, n % 2, 2:2 + TP].rearrange("p (a b) -> p a b", a=2),
                           acc[:, 2 * (n % 2):2 * (n % 2) + 2, 0:HALF], ACT.Copy)

            def smooth(n, stored):
                act.wait_ge(conv["sem"], due(conv))
                if stored:
                    act.wait_ge(conv_out[n % 2]["sem"], value(conv_out[n % 2]))
                    step(conv_out[n % 2], 2)
                act.activation(cvs[:, n % 2], cvo[:, n % 2], ACT.Silu).then_inc(silu["sem"], step(silu))

            def turned_out(n):
                act.wait_ge(turned["sem"], due(turned))
                step(nat_out[n % 2])
                if some(nat_out[n % 2], 1):
                    act.wait_ge(nat_out[n % 2]["sem"], value(nat_out[n % 2], 1))
                act.activation(nst[:, n % 2, 0], tp[:, 1, 0:P], ACT.Copy)
                act.activation(nst[:, n % 2, 1:NT].rearrange("p t c -> p (t c)"), tp[:, 0], ACT.Copy).then_inc(tfree["sem"], step(tfree))

            mraws = pair("mraw_in")

            def split_mod_hi(b):
                act.wait_ge(mraws[b]["sem"], due(mraws[b]))
                step(mod_used)
                act.wait_ge(mod_used["sem"], value(mod_used, 2))
                act.activation(mwh[:, b], mraw[:, b], ACT.Copy).then_inc(mhi["sem"], step(mhi))

            mrows, mrow_used = count(s["mod_rows"], 1, 1), count(s["mod_cols"], 1, 1)

            def xbc_round(turning, stored):
                for n in range(4):
                    evacuate(n)
                    if n % 2 == 0:
                        split_mod_hi(n // 2)
                    else:
                        split_hi(n // 2)
                    if turning and n:
                        turned_out(n - 1)
                    smooth(n, stored)
                act.wait_ge(mod_used["sem"], value(mod_used))
                step(mrow_used)
                act.wait_ge(mrow_used["sem"], value(mrow_used, 1))
                act.activation(mrow, tp[0:4, 2], ACT.Copy).then_inc(mrows["sem"], step(mrows))
                if turning:
                    turned_out(3)

            padded = count(s["conv_ok"])
            step(conv, 2)
            act.wait_ge(s["h_ok"], KT)
            every = [(ready, 4), (free, 4), (hi, 2), (raws[0], 1), (raws[1], 1), (conv, 4), (padded, 4), (silu, 4),
                     (mraws[0], 1), (mraws[1], 1), (mhi, 2), (mod_used, 2), (mrows, 1), (mrow_used, 1)]
            turning = [(turned, 4), (tfree, 4), (nat_out[0], 2), (nat_out[1], 2)]
            storing = [(conv_out[0], 4), (conv_out[1], 4)]
            with rounds(act, RX, *every, *turning):
                xbc_round(True, False)
            with rounds(act, RB, *every, *turning, *storing):
                xbc_round(True, True)
            with rounds(act, RC, *every, *storing):
                xbc_round(False, True)

            act.wait_ge(s["dt_in"], 48)
            act.activation(wdh[:], wdt, ACT.Copy).then_inc(s["dt_hi"], 1)
            act.activation(alg, alg, ACT.Exp).then_inc(steps["sem"], step(steps))
            act.wait_ge(s["dt_abs"], 1)
            act.activation(dtu[:, 1], dtu[:, 0], ACT.Exp, scale=-1.0).then_inc(steps["sem"], step(steps))
            act.wait_ge(steps["sem"], value(steps))
            act.activation(dtu[:, 1], dtu[:, 1], ACT.Ln, bias=1.0).then_inc(s["dt_soft"], 1)

            rot = count(s["rot_ok"])

            def block_out(b, dst, func):
                for t in range(NT):
                    out_of_acc(dst[:, t], acc[:, 2 * ((NT * b + t) % 2), 0:BW], func)
                split_hi(b)

            for n in range(5):
                step(rot)
                if some(rot, 2):
                    act.wait_ge(rot["sem"], value(rot, 2))
                block_out(n % 2, q5[:, n % 2], ACT.Copy)
                roots(ms.rearrange("p t h -> p (t h)"))
            for c in nat_out + conv_out:
                act.wait_ge(c["sem"], value(c))
            block_out(1, vn, ACT.Copy)
            act.wait_ge(s["dt_summed"], 1)
            act.activation(dec[:].rearrange("p t j h -> p j t h"),
                           tp[:, 1:4, 0:NT * 2 * NH].rearrange("p j (t h) -> p j t h", t=NT), ACT.Exp).then_inc(s["dt_exp"], 1)

            act.wait_ge(s["rot_ok"], 5)
            act.wait_ge(s["out_kv"], 32)
            zo, go = pair("zst_out"), pair("gst_out")
            with rounds(act, 4, (ready, 2 * NT), (free, 2 * NT), (hi, 2), (raws[0], 1), (raws[1], 1), (zo[0], 1), (zo[1], 1)):
                for b in range(2):
                    step(zo[b])
                    if some(zo[b], 1):
                        act.wait_ge(zo[b]["sem"], value(zo[b], 1))
                    block_out(b, zst[:, b], ACT.Silu)
            with rounds(act, 4, (ready, 4), (free, 4), (hi, 2), (raws[0], 1), (raws[1], 1), (go[0], 2), (go[1], 2)):
                for n in range(4):
                    step(go[n % 2])
                    if some(go[n % 2], 1):
                        act.wait_ge(go[n % 2]["sem"], value(go[n % 2], 1))
                    out_of_acc(gst[:, n % 2].rearrange("p (a b) -> p a b", a=2),
                               acc[:, 2 * (n % 2):2 * (n % 2) + 2, 0:HALF], ACT.Sigmoid)
                    if n % 2 == 1:
                        split_hi(n // 2)
            for c in zo + go:
                act.wait_ge(c["sem"], value(c))

            qt, qc = count(s["qk_turned"]), count(s["qk_copied"])
            for h in range(HQ + HKV):
                act.wait_ge(qt["sem"], due(qt))
                act.activation(qT[:, h, LAT:], tp[:, 1, 0:P], ACT.Copy)
                act.activation(qT[:, h, 0:LAT], tp[:, 0], ACT.Copy).then_inc(qc["sem"], step(qc))
            act.wait_ge(qt["sem"], due(qt))
            act.activation(kcT.rearrange("p h t -> p (h t)"), tp[:, 0], ACT.Copy).then_inc(qc["sem"], step(qc))
            mx, ex = count(s["max_ok"]), count(s["exp_ok"])
            ptt, ptc, pv = count(s["p_turned"]), count(s["p_copied"]), count(s["pv_ready"])
            ahi = count(s["att_hi"])

            def exps(n):
                u = n % 2
                act.wait_ge(mx["sem"], due(mx))
                if n >= 2:
                    act.wait_ge(s["p_turned"], n - 1)
                if n < N_SCORE:
                    sc = acc[:, 2 * u:2 * u + 2].rearrange("p a b -> p (a b)")[:, 0:LAT + PAST]
                    act.activation(pr[:, u], sc, ACT.Exp, bias=sm[:, u, 0:1], scale=SCALE,
                                             accum_out=sm[:, u, 4:5]).then_inc(ex["sem"], step(ex))
                else:
                    for r in range(R):
                        last = act.activation(pr[:, u, r * P:(r + 1) * P], acc[:, 2 * u, r * P:(r + 1) * P], ACT.Exp,
                                              bias=sm[:, u, r:r + 1], scale=SCALE, accum_out=sm[:, u, 4 + r:5 + r])
                    last.then_inc(ex["sem"], step(ex))

            def probs_out(n):
                act.wait_ge(ptt["sem"], due(ptt))
                if n < N_SCORE:
                    h, t = n // 4, n % 4
                    if h >= 2:
                        act.wait_ge(s["pv_ready"], h - 1)
                    act.activation(pT[:, h % 2, :, t * P:(t + 1) * P],
                                              tp[:, 0:2].rearrange("p a b -> p (a b)")[:, 0:LAT + PAST]
                                              .rearrange("p (j q) -> p j q", q=P), ACT.Copy).then_inc(ptc["sem"], step(ptc))
                else:
                    h = HQ + n - N_SCORE
                    act.wait_ge(s["pv_ready"], h - 1)
                    act.activation(pT[:, h % 2, 0], tp[:, 0], ACT.Copy).then_inc(ptc["sem"], step(ptc))

            def att_out(h):
                act.wait_ge(pv["sem"], due(pv))
                if h < HQ:
                    act.activation(hh[:, h, CTX + 2:NCONV], tp[:, 2 + h % 2], ACT.Copy).then_inc(ahi["sem"], step(ahi))
                else:
                    g = h - HQ
                    act.activation(hh[:, R * g:R * g + R, 0:CTX],
                                              tp[:, 2 + h % 2].rearrange("p (r t) -> p r t", r=R), ACT.Copy).then_inc(ahi["sem"], step(ahi))

            exps(0)
            for n in range(N_SCORE + HKV):
                if n + 1 < N_SCORE + HKV:
                    exps(n + 1)
                if n == N_SCORE + 1:
                    att_out(HQ - 1)
                probs_out(n)
                if n % 4 == 1 and 4 < n < N_SCORE:
                    att_out(n // 4 - 1)
            att_out(HQ)
            att_out(HQ + 1)

            for b in range(2):
                step(ready, 2)
                act.wait_ge(ready["sem"], value(ready))
                split_hi(b)
            step(ready, 4)

            seg, e_ok, m_ok = count(s["seg_ready"]), count(s["e_ok"]), count(s["m_ok"])
            quad, stc, sqi, sqo = (count(s[n]) for n in ("states_ready", "st_copied", "sq_in", "sq_ok"))
            act.wait_ge(s["acc_free"], U_SO)
            for c in pair("ast_out"):
                step(c, KT // 2)
                act.wait_ge(c["sem"], value(c))
            flat = lambda t: t.rearrange("p h q -> p (h q)")

            def decays(g):
                act.wait_ge(seg["sem"], due(seg))
                step(m_ok)
                if some(m_ok, 2):
                    act.wait_ge(m_ok["sem"], value(m_ok, 2))
                act.activation(ee[:, g % 2].rearrange("p r t -> p (r t)"), acc[:, g % 2], ACT.Exp).then_inc(e_ok["sem"], step(e_ok))

            def states_out(q):
                act.wait_ge(quad["sem"], due(quad))
                for d, (buf, bank) in enumerate(((hF, acc[:, 3] if q % 2 == 0 else tp[:, 1]), (hB, tp[:, 2]))):
                    act.activation(flat(buf)[:, q * 512:(q + 1) * 512], bank, ACT.Copy).then_inc(stc["sem"], step(stc))

            def squares():
                act.wait_ge(sqi["sem"], due(sqi))
                act.activation(zc, flat(yy), ACT.Square, accum_out=mv[:, 0, 0:1]).then_inc(sqo["sem"], step(sqo))

            def rises(c, g):
                if some(seg_r, 1):
                    act.wait_ge(seg_r["sem"], value(seg_r, 1))
                step(seg_r)
                for j, m in enumerate((K_LE, K_GE)):
                    for r in range(R):
                        h = j * NH + R * g + r
                        last = act.activation(rr[:, g % 2, j, r], mask(m), ACT.Copy,
                                              scale=dta[:, bass.ds(c, 1), h:h + 1].rearrange("p o h -> p (o h)"))
                last.then_inc(rise["sem"], step(rise))

            rise, seg_r = count(s["rise_ok"]), count(s["seg_ready"])
            rises(0, 0)
            rises(0, 1)
            for g in range(NG):
                decays(g)
                if g + 2 < NG:
                    rises(0, g + 2)
                if g >= 2 and g % 2 == 0:
                    states_out(g // 2 - 1)
            states_out(3)
            squares()
            roots(mv[:, 0, 2:3])
            act.wait_ge(s["st_out"], 32)
            h0t, h0c = count(s["h0_turned"]), count(s["h0_ok"])
            for d, buf in enumerate((hF, hB)):
                for j in range(4):
                    act.wait_ge(h0t["sem"], due(h0t))
                    act.activation(flat(buf)[:, j * 512:(j + 1) * 512], tp[:, (4 * d + j) % 2], ACT.Copy).then_inc(h0c["sem"], step(h0c))
            with rounds(act, 2, (seg, 16), (seg_r, 16), (rise, 16), (e_ok, 16), (m_ok, 16), (sqi, 2), (sqo, 2),
                        (var, 2), (dev, 2)) as i:
                for b in range(2):
                    c = i * 2 + (1 + b)
                    rises(c, 0)
                    rises(c, 1)
                    for g in range(NG):
                        decays(g)
                        if g + 2 < NG:
                            rises(c, g + 2)
                    squares()
                    roots(mv[:, 0, 2:3])

            def split_hi_normed(slot):
                act.wait_ge(raws[slot]["sem"], due(raws[slot]))
                for k in range(KT):
                    n = Q_SN + slot * KT + k
                    last = act.activation(whi[:, slot, k], raw[:, slot, k], ACT.Copy, scale=colp[:, n:n + 1])
                last.then_inc(hi["sem"], step(hi))

            split_hi_normed(0)
            act.wait_ge(s["chunk_ok"], 8)
            yt, yhi, yok = count(s["y_turned"]), count(s["y_hi"]), count(s["y_ok"])
            for t in range(NT):
                for j in range(4):
                    act.wait_ge(yt["sem"], due(yt))
                    act.activation(yh[:, 4 * j:4 * j + 4, tok(t):tok(t) + P],
                                   tp[:, j].rearrange("p (n t) -> p n t", t=P), ACT.Copy).then_inc(yhi["sem"], step(yhi))
                if t == 0:
                    split_hi_normed(1)
            half, msum, mhi = count(s["w_half"]), count(s["merge_sum"]), count(s["merge_hi"])

            def merge_round(i, split):
                act.wait_ge(half["sem"], due(half))
                split(0)
                for b in range(2):
                    if b == 1:
                        step(ready, 2)
                        act.wait_ge(ready["sem"], value(ready))
                        split(1)
                    act.wait_ge(msum["sem"], due(msum))
                    act.activation(hh[:, bass.ds(i * 2 + b, 1)].rearrange("p o t -> p (o t)"), mrg,
                                   ACT.Copy).then_inc(mhi["sem"], step(mhi))

            with rounds(act, 3, (ready, 2), (hi, 2), (raws[0], 1), (raws[1], 1), (half, 1), (msum, 2), (mhi, 2)) as i:
                merge_round(i, split_hi_normed)
            merge_round(3, split_hi)

            with rounds(act, 2, (ready, 2 * NT), (hi, 2), (raws[0], 1), (raws[1], 1)):
                for b in range(2):
                    step(ready, NT)
                    act.wait_ge(ready["sem"], value(ready))
                    split_hi(b)
            roots(mv[:, :, 2])
            roots(mv[:, :, 2])
            jump(free, U_H2)
            act.wait_ge(s["pad_ok"], 2)
            modulated(hf2, "h2_hi", "h2_ok", 4, 3)

            relu, sq = count(s["relu_ok"]), count(s["square_ok"])

            def mlp_round(last_round):
                for n in range(KT):
                    act.wait_ge(relu["sem"], due(relu))
                    act.activation(fh[:, n], hf2[:, n % 2], ACT.Square).then_inc(sq["sem"], step(sq))
                    step(ready)
                    if n % 2 == 1:
                        act.wait_ge(ready["sem"], value(ready))
                        split_hi(n // 2 % 2)
                for b in range(4):
                    step(ready, NT)
                    if b < 2 or not last_round:
                        act.wait_ge(ready["sem"], value(ready))
                        split_hi(b % 2)

            with rounds(act, 3, (ready, KT + 4 * NT), (hi, 8), (raws[0], 4), (raws[1], 4), (relu, KT), (sq, KT)):
                mlp_round(False)
            mlp_round(True)
            roots(mv[:, :, 2])

        @block.vector
        def _(dve):
            dv = count(s["dve_step"])
            hi, lo = count(s["hi_done"]), count(s["lo_done"])
            ready, free = count(s["acc_ready"]), count(s["acc_free"])

            def do(ins):
                ins.then_inc(dv["sem"], step(dv))
                dve.wait_ge(dv["sem"], value(dv))

            def split_lo(slot):
                dve.wait_ge(hi["sem"], due(hi))
                dve.tensor_tensor(wlo[:, slot], raw[:, slot], whi[:, slot].bitcast(F32), ALU.subtract).then_inc(lo["sem"], step(lo))

            def over(ap, *shape):
                return ap.unsqueeze(len(ap.shape)).broadcast_to([P, *shape])

            for buf in (hf[:, :, CTX:CTX + 2], hf[:, :, NCONV:TP]):
                last = dve.memset(buf, 0.0)
            last.then_inc(s["pad_ok"], 1)
            dve.wait_ge(s["rows_turned"], 1)
            dve.tensor_copy(colp[:], tp[:, 0, 0:Q_ALL]).then_inc(s["turned_free"], 1)
            dve.wait_ge(s["turned_free"], 1)

            var, dev = count(s["var_ok"]), count(s["dev_ok"])

            def statistics(t, src):
                for j in range(2):
                    last = dve.bn_stats(st6[:, t, j], src[:, j * 512:(j + 1) * 512])
                do(last)
                do(dve.bn_aggr(mv[:, t, 0:2], st6[:, t, 0:2].rearrange("p a b -> p (a b)")))

            def gathered(t):
                do(dve.bn_aggr(mv[:, t, 0:2], st6[:, t].rearrange("p a b -> p (a b)")))

            def deviations():
                dve.tensor_scalar(mv[:, :, 2], mv[:, :, 1], EPS, None, ALU.add).then_inc(var["sem"], step(var))
                inverses()

            def inverses():
                dve.wait_ge(dev["sem"], due(dev))
                do(dve.reciprocal(mv[:, :, 2], mv[:, :, 2]))
                do(dve.scalar_tensor_tensor(mv[:, :, 3], mv[:, :, 0], -1.0, mv[:, :, 2], ALU.mult, ALU.mult))

            def weighed(t, x, rows):
                do(dve.scalar_tensor_tensor(x, x, mv[:, t, 0:1], rows[:, 0], ALU.subtract, ALU.mult))
                return dve.scalar_tensor_tensor(x, x, mv[:, t, 2:3], rows[:, 1], ALU.mult, ALU.add)

            def normed(t, dst, src):
                return dve.tensor_scalar(dst, src, mv[:, t, 2:3], mv[:, t, 3:4], ALU.mult, ALU.add)

            dve.wait_ge(s["cond_hi"], 1)
            dve.tensor_tensor(ssplit[:, :, 2:4], siluc[:].rearrange("p (c k) -> p k c", k=KT),
                              ssplit[:, :, 0:2].bitcast(F32), ALU.subtract).then_inc(s["cond_lo"], 1)
            mhi, mlo = count(s["mod_hi_done"]), count(s["mod_lo_done"])

            def split_mod_lo(dst, src, upper):
                dve.wait_ge(mhi["sem"], due(mhi))
                dve.tensor_tensor(dst, src, upper.bitcast(F32), ALU.subtract).then_inc(mlo["sem"], step(mlo))

            for r in range(KT):
                split_mod_lo(wlo[:, r % 2], mod0[:, r], whi[:, r % 2])
                if r == 0:
                    dve.wait_ge(s["x_in"], 32)
                if r < NT:
                    statistics(r, xin[:, r])
                if r == NT - 1:
                    dve.tensor_scalar(mv[:, :, 2], mv[:, :, 1], EPS, None, ALU.add).then_inc(var["sem"], step(var))
                if r == NT:
                    inverses()
            for t in range(NT):
                normed(t, xin[:, t], xin[:, t]).then_inc(s["xn_ok"], 1)
            dve.wait_ge(s["mod_cols"], 1)
            shift = modc[:, 0:2 * KT]
            do(dve.tensor_tensor(shift, modp[:, :, 0:2], over(colp[:, Q_BM:Q_BM + 2 * KT], 2 * KT, 2), ALU.add))
            do(dve.tensor_tensor(shift, shift, modp[:, :, 2:4], ALU.add))
            dve.tensor_scalar(modc[:, KT:2 * KT], modc[:, KT:2 * KT], 1.0, None, ALU.add).then_inc(s["mod_copied"], 1)

            def split_h(buf, hi_ok, lo_ok):
                h = count(s[hi_ok])
                for k in range(KT):
                    dve.wait_ge(h["sem"], due(h))
                    dve.tensor_tensor(hl[:, k], buf[:, k % 2], hh[:, k].bitcast(F32), ALU.subtract).then_inc(s[lo_ok], 1)

            split_h(hf, "hi_of_h", "h_ok")
            split_lo(0)
            split_lo(1)

            conv = count(s["conv_ok"])
            dve.wait_ge(s["acc_free"], KT)
            for u in range(2):
                dve.memset(xpad[:, u, 0:2], 0.0).then_inc(conv["sem"], step(conv))
            silu = count(s["conv_silu"])
            cmod, mcols = count(s["mod_copied"]), count(s["mod_cols"], 1, 1)
            step(cmod)

            def convolve(n, ct):
                dve.wait_ge(free["sem"], due(free))
                w = lambda t: colp[:, bass.ds(ct + (Q_CONV + t * 32), 1)]
                o, x = cvo[:, n % 2], xpad[:, n % 2]
                step(silu)
                if some(silu, 2):
                    dve.wait_ge(silu["sem"], value(silu, 2))
                do(dve.tensor_scalar(o, x[:, 0:NCONV], w(0), colp[:, bass.ds(ct + Q_CB, 1)], ALU.mult, ALU.add))
                for t in range(1, TAPS):
                    ins = dve.scalar_tensor_tensor(o, x[:, t:t + NCONV], w(t), o, ALU.mult, ALU.add)
                    if t < TAPS - 1:
                        do(ins)
                ins.then_inc(conv["sem"], step(conv))

            step(free, KT)
            with rounds(dve, RX + RB + RC, (free, 4), (conv, 4), (hi, 2), (lo, 2), (dv, 17), (cmod, 1),
                        (mcols, 1), (mhi, 2), (mlo, 2)) as i:
                for n in range(4):
                    convolve(n, i * 4 + n)
                    if n % 2 == 1:
                        split_lo(n // 2)
                    else:
                        split_mod_lo(mwl[:, n // 2], mraw[:, n // 2], mwh[:, n // 2])
                dve.wait_ge(mcols["sem"], due(mcols))
                dst = modc[:, bass.ds(i * 4 + 2 * KT, 4)]
                bias = colp[:, bass.ds(i * 4 + (Q_BM + 2 * KT), 4)]
                parts = tp[:, 3, 0:16].rearrange("p (b c) -> p b c", c=4)
                do(dve.tensor_tensor(dst, parts[:, :, 0:2], over(bias, 4, 2), ALU.add))
                dve.tensor_tensor(dst, dst, parts[:, :, 2:4], ALU.add).then_inc(cmod["sem"], step(cmod))
            dve.wait_ge(cmod["sem"], value(cmod))
            dve.tensor_scalar(modc[:, 4 * KT:5 * KT], modc[:, 4 * KT:5 * KT], 1.0, None, ALU.add).then_inc(s["modc_ok"], 1)

            dve.wait_ge(s["dt_in"], 48)
            dve.wait_ge(s["dt_hi"], 1)
            dve.tensor_tensor(wdl[:], wdt, wdh[:].bitcast(F32), ALU.subtract).then_inc(s["dt_split"], 1)
            dve.wait_ge(s["dt_mm"], 1)
            mid = lambda ap: ap.unsqueeze(1).broadcast_to([P, NT, 2 * NH])
            do(dve.tensor_tensor(dtu[:, 2], tp[:, 0, 0:NT * 2 * NH].rearrange("p (t h) -> p t h", t=NT), mid(dtb), ALU.add))
            do(dve.tensor_scalar(dtu[:, 0], dtu[:, 2], -1.0, None, ALU.mult))
            dve.tensor_tensor(dtu[:, 0], dtu[:, 0], dtu[:, 2], ALU.max).then_inc(s["dt_abs"], 1)
            do(dve.tensor_scalar(dtu[:, 2], dtu[:, 2], 0.0, None, ALU.max))
            dve.wait_ge(s["dt_soft"], 1)
            do(dve.tensor_tensor(dts[:], dtu[:, 2], dtu[:, 1], ALU.add))
            do(dve.tensor_tensor(dta[:], dts[:], mid(alg), ALU.mult))
            dve.tensor_scalar(dta[:], dta[:], -1.0, None, ALU.mult).then_inc(s["dt_sums"], 1)

            for c in pair("nat_out"):
                step(c, 2 * (RX + RB))
                dve.wait_ge(c["sem"], value(c))
            for c in pair("conv_out"):
                step(c, 4 * (RB + RC))
                dve.wait_ge(c["sem"], value(c))
            dve.wait_ge(s["norm_in"], 32)
            hd = lambda ap: ap.rearrange("p t (h d) -> p t h d", d=HD)
            th = lambda ap: ap.rearrange("p t (h d) -> p (t h) d", d=HD)
            for n in range(5):
                step(free, NT)
                dve.wait_ge(free["sem"], value(free))
                q = q5[:, n % 2]
                do(dve.tensor_tensor(t5, q, q, ALU.mult))
                msf = ms.rearrange("p t h -> p (t h)")
                do(dve.tensor_reduce(msf, th(t5), AX.X, ALU.add))
                dve.tensor_scalar(msf, msf, 1.0 / HD, EPS, ALU.mult, ALU.add).then_inc(var["sem"], step(var))
                dve.wait_ge(dev["sem"], due(dev))
                do(dve.reciprocal(msf, msf))
                do(dve.tensor_tensor(th(t5), th(q), over(msf, NT * 2, HD), ALU.mult))
                gain = nrow[:, n // 4].unsqueeze(1).broadcast_to([P, NT * 2, HD])
                do(dve.tensor_tensor(th(u5), th(t5), gain, ALU.mult))
                if n == 4:
                    dve.tensor_copy(kout, u5[:, 0]).then_inc(s["kout_ok"], 1)
                cols = slice(n * BW, (n + 1) * BW)
                dve.tensor_copy(rq[:, 0, cols], u5[:, 0])
                sine = cst[:, K_SIN:K_SIN + 4 * P].rearrange("p (t a b f) -> p t a b f", t=4, a=2, b=2)
                for h in range(2):
                    v = lambda ap: ap[:, 1:NT, h * HD:(h + 1) * HD].rearrange("p t (a b f) -> p t a b f", a=2, b=2)
                    for b in range(2):
                        last = dve.tensor_tensor(v(t5)[:, :, :, b], v(u5)[:, :, :, 1 - b], sine[:, :, :, b], ALU.mult)
                do(last)
                cosine = cst[:, K_COS:K_COS + 4 * P].rearrange("p (t d) -> p t d", t=4).unsqueeze(2).broadcast_to([P, 4, 2, HD])
                do(dve.tensor_tensor(hd(q[:, 1:NT]), hd(u5[:, 1:NT]), cosine, ALU.mult))
                dve.tensor_tensor(rq[:, 1:NT, cols], q[:, 1:NT], t5[:, 1:NT], ALU.add).then_inc(s["rot_ok"], 1)
                dve.wait_ge(s["rot_ok"], n + 1)
                split_lo(n % 2)
            step(free, NT)
            split_lo(1)
            dve.wait_ge(s["dt_exp"], 1)
            dve.tensor_tensor(sdt[:], dts[:], dec[:, :, 1], ALU.mult).then_inc(s["dt_ok"], 1)
            dve.wait_ge(s["gate_turned"], 1)
            for n in range(2):
                dve.tensor_copy(grow[:, n], tp[0:2 * KT, 0, n * P:(n + 1) * P]).then_inc(s["gate_copied"], 1)
            with rounds(dve, 8, (hi, 2), (lo, 2)):
                for b in range(2):
                    split_lo(b)

            score, mx, ex, prob = (count(s[n]) for n in ("score_ready", "max_ok", "exp_ok", "prob_ok"))
            ahi, aok = count(s["att_hi"]), count(s["att_ok"])
            dve.wait_ge(s["qk_copied"], HQ + HKV + 1)

            def maxima(n):
                u = n % 2
                dve.wait_ge(score["sem"], due(score))
                if n < N_SCORE:
                    sc = acc[:, 2 * u:2 * u + 2].rearrange("p a b -> p (a b)")[:, 0:LAT + PAST]
                    do(dve.tensor_reduce(sm[:, u, 8:9], sc, AX.X, ALU.max))
                    dve.tensor_scalar(sm[:, u, 0:1], sm[:, u, 8:9], -SCALE, None, ALU.mult).then_inc(mx["sem"], step(mx))
                else:
                    sc = acc[:, 2 * u].rearrange("p (r t) -> p r t", r=R)
                    do(dve.tensor_reduce(sm[:, u, 8:12], sc, AX.X, ALU.max))
                    dve.tensor_scalar(sm[:, u, 0:4], sm[:, u, 8:12], -SCALE, None, ALU.mult).then_inc(mx["sem"], step(mx))

            def probabilities(n):
                u = n % 2
                dve.wait_ge(ex["sem"], due(ex))
                if n < N_SCORE:
                    do(dve.reciprocal(sm[:, u, 12:13], sm[:, u, 4:5]))
                    dve.tensor_scalar(pr[:, u], pr[:, u], sm[:, u, 12:13], None, ALU.mult).then_inc(prob["sem"], step(prob))
                else:
                    do(dve.reciprocal(sm[:, u, 12:16], sm[:, u, 4:8]))
                    p4 = pr[:, u, 0:R * P].rearrange("p (r t) -> p r t", r=R)
                    dve.tensor_tensor(p4, p4, over(sm[:, u, 12:16], R, P), ALU.mult).then_inc(prob["sem"], step(prob))

            def att_lower(h):
                dve.wait_ge(ahi["sem"], due(ahi))
                if h < HQ:
                    cols = (slice(h, h + 1), slice(CTX + 2, NCONV))
                    src = tp[:, 2 + h % 2].unsqueeze(1)
                else:
                    cols = (slice(R * (h - HQ), R * (h - HQ) + R), slice(0, CTX))
                    src = tp[:, 2 + h % 2].rearrange("p (r t) -> p r t", r=R)
                dve.tensor_tensor(hl[:, cols[0], cols[1]], src, hh[:, cols[0], cols[1]].bitcast(F32), ALU.subtract).then_inc(aok["sem"], step(aok))

            maxima(0)
            maxima(1)
            for n in range(N_SCORE + HKV):
                probabilities(n)
                if n + 2 < N_SCORE + HKV:
                    maxima(n + 2)
                if n % 4 == 1 and 4 < n < N_SCORE:
                    att_lower(n // 4 - 1)
            for h in range(HQ - 1, HQ + 2):
                att_lower(h)

            jump(ready, U_AO)
            jump(free, U_AO)
            gat_in, ao = pair("gat_in"), pair("ast_out")
            both = lambda ap: ap.rearrange("p (a b) -> p a b", a=2)
            for n in range(KT):
                dve.wait_ge(ready["sem"], due(ready))
                dve.wait_ge(gat_in[n % 2]["sem"], due(gat_in[n % 2]))
                step(ao[n % 2])
                if some(ao[n % 2], 1):
                    dve.wait_ge(ao[n % 2]["sem"], value(ao[n % 2], 1))
                dve.tensor_tensor(both(ast[:, n % 2]), acc[:, 2 * (n % 2):2 * (n % 2) + 2, 0:HALF],
                                              both(gat[:, n % 2]), ALU.mult).then_inc(free["sem"], step(free))
                if n in (1, 3):
                    split_lo(n // 2)
            for c in ao:
                dve.wait_ge(c["sem"], value(c))
            dve.wait_ge(free["sem"], value(free))

            cin = pair("chunk_in")
            cbr, cbo, rise, seg, e_ok = (count(s[n]) for n in ("cb_ready", "cb_ok", "rise_ok", "seg_ready", "e_ok"))
            m_ok, xd, grp, quad, qok = (count(s[n]) for n in ("m_ok", "xd_ok", "group_ready", "states_ready", "quad_ok"))
            car = count(s["carried_ok"])
            sqi, sqo, chunk = count(s["sq_in"]), count(s["sq_ok"]), count(s["chunk_ok"])
            zin = count(s["z_in"], 16)
            dve.wait_ge(s["dsk_in"], 16)
            flat = lambda t: t.rearrange("p h q -> p (h q)")
            le8, ge8 = (mask(k).unsqueeze(1).broadcast_to([P, NG, P]) for k in (K_LE, K_GE))

            def of_chunk(t, c):
                return t[:, bass.ds(c, 1)].rearrange("p o h -> p (o h)")

            def scan_chunk(slot, c, latent, out):
                x = xs_s[slot]
                step(cin[slot], 3)
                dve.wait_ge(cin[slot]["sem"], value(cin[slot]))
                f4 = lambda t, q: over(t[:, 8 * q:8 * q + 8], 8, SP_)
                DT, SD = (of_chunk(t, c) for t in (dts, sdt))
                to, whole = of_chunk(dec[:, :, 0], c), of_chunk(dec[:, :, 2], c)

                def scaled(q):
                    h = slice(8 * q, 8 * q + 8)
                    dve.tensor_tensor(xdf[:, q % 2], x[:, h], f4(DT, q), ALU.mult)
                    dve.tensor_tensor(xdb[:, q % 2], x[:, h], f4(DT[:, NH:], q), ALU.mult)
                    if not latent:
                        dve.tensor_tensor(xwb[:, q % 2], x[:, h], f4(SD[:, NH:], q), ALU.mult)
                    dve.tensor_tensor(xwf[:, q % 2], x[:, h], f4(SD, q), ALU.mult).then_inc(xd["sem"], step(xd))

                def weighted(g):
                    dve.wait_ge(e_ok["sem"], due(e_ok))
                    step(grp)
                    if some(grp, 2):
                        dve.wait_ge(grp["sem"], value(grp, 2))
                    for j in range(2):
                        last = dve.tensor_tensor(mm[:, g % 2, j], ee[:, g % 2],
                                                 cbm[:, j, g].unsqueeze(1).broadcast_to([P, R, P]), ALU.mult)
                    last.then_inc(m_ok["sem"], step(m_ok))

                v = lambda bank: bank.rearrange("p (h q) -> p h q", q=SP_)
                banks = lambda q: (acc[:, 2], acc[:, 3]) if q % 2 == 0 else (tp[:, 0], tp[:, 1])

                def carried(q):
                    h = slice(8 * q, 8 * q + 8)
                    dve.wait_ge(quad["sem"], due(quad))
                    dve.tensor_tensor(yy[:, h], v(tp[:, 2]), f4(to, q), ALU.mult)
                    do(dve.tensor_tensor(tq, v(tp[:, 3]), f4(to[:, NH:], q), ALU.mult))
                    dve.tensor_tensor(hF[:, h], hF[:, h], f4(whole, q), ALU.mult)
                    do(dve.tensor_tensor(yy[:, h], yy[:, h], tq, ALU.add))
                    dve.tensor_tensor(hF[:, h], hF[:, h], v(banks(q)[1]), ALU.add).then_inc(car["sem"], step(car))
                    do(dve.tensor_tensor(tq, x[:, h], f4(dsk[:], q), ALU.mult))
                    do(dve.tensor_tensor(yy[:, h], yy[:, h], tq, ALU.add))

                def combined(q):
                    h = slice(8 * q, 8 * q + 8)
                    if not latent:
                        dve.tensor_tensor(tq, x[:, h], f4(dsk[:], q), ALU.mult).then_inc(car["sem"], step(car))
                        dve.wait_ge(car["sem"], value(car))
                    step(grp_q, 2)
                    dve.wait_ge(grp_q["sem"], value(grp_q))
                    dve.tensor_tensor(yy[:, h], yy[:, h] if latent else tq, v(banks(q)[0]), ALU.add).then_inc(qok["sem"], step(qok))
                    if not latent:
                        dve.wait_ge(qok["sem"], value(qok))

                scaled(0)
                dve.wait_ge(cbr["sem"], due(cbr))
                tpv = tp[:, 0:2].rearrange("p a (g t) -> p (a g) t", t=P)
                dve.tensor_tensor(cbm[:, 0], tpv, le8, ALU.mult)
                dve.tensor_tensor(cbm[:, 1], tpv, ge8, ALU.mult).then_inc(cbo["sem"], step(cbo))
                dve.wait_ge(cbo["sem"], value(cbo))
                for g in range(NG):
                    weighted(g)
                    if g % 2 == 1 and g + 1 < NG:
                        scaled((g + 1) // 2)
                    if g % 2 == 1 and latent:
                        carried(g // 2)
                    if g % 2 == 1 and g > 1:
                        combined(g // 2 - 1)
                combined(3)
                dve.wait_ge(zin["sem"], due(zin))
                dve.wait_ge(qok["sem"], value(qok))
                dve.tensor_tensor(flat(yy), flat(yy), zc, ALU.mult).then_inc(sqi["sem"], step(sqi))
                dve.wait_ge(sqo["sem"], due(sqo))
                dve.tensor_scalar(mv[:, 0, 2:3], mv[:, 0, 0:1], 1.0 / DI, EPS, ALU.mult, ALU.add).then_inc(var["sem"], step(var))
                dve.wait_ge(dev["sem"], due(dev))
                do(dve.reciprocal(mv[:, 0, 3:4], mv[:, 0, 2:3]))
                dve.tensor_scalar(out, flat(yy), mv[:, 0, 3:4], None, ALU.mult).then_inc(chunk["sem"], step(chunk))
                dve.wait_ge(chunk["sem"], value(chunk))

            grp_q = count(s["group_ready"])
            scan_chunk(0, 0, False, yctx[:])
            step(quad, 4)
            back, bok, xwo = count(s["back_ready"]), count(s["back_ok"]), count(s["xwb_ok"])
            backr = count(s["back_ready"])
            dve.wait_ge(s["h0_ok"], 8)
            for j in range(1, 4):
                c, x = CHUNKS[j], xs_s[j % 2]
                step(cin[j % 2], 2)
                dve.wait_ge(cin[j % 2]["sem"], value(cin[j % 2]))
                f4 = lambda t, q: over(t[:, 8 * q:8 * q + 8], 8, SP_)

                def back_scaled(q):
                    step(back)
                    if some(back, 2):
                        dve.wait_ge(back["sem"], value(back, 2))
                    dve.tensor_tensor(xwb[:, q % 2], x[:, 8 * q:8 * q + 8], f4(sdt[:, c, NH:], q), ALU.mult).then_inc(xwo["sem"], step(xwo))

                if j == 3:
                    dve.wait_ge(s["hb_first_out"], 16)
                back_scaled(0)
                for q in range(4):
                    if q < 3:
                        back_scaled(q + 1)
                    h = slice(8 * q, 8 * q + 8)
                    do(dve.tensor_tensor(backs[j][:, h], backs[j - 1][:, h], f4(dec[:, c, 2, NH:], q), ALU.mult))
                    dve.wait_ge(backr["sem"], due(backr))
                    ins = dve.tensor_tensor(backs[j][:, h], backs[j][:, h], acc[:, 2 + q % 2].rearrange("p (h q) -> p h q", q=SP_), ALU.add)
                    ins.then_inc(bok["sem"], step(bok))
                dve.wait_ge(bok["sem"], value(bok))
                dve.tensor_copy(mv[:, 1, 0:1], mv[:, 1, 1:2]).then_inc(chunk["sem"], step(chunk))
            every = [(cin[0], 3), (cin[1], 3), (cbr, 2), (cbo, 2), (e_ok, 16), (m_ok, 16), (grp, 16),
                     (xd, 8), (quad, 8), (grp_q, 16), (car, 8), (qok, 8), (sqi, 2), (sqo, 2), (chunk, 2), (zin, 2), (var, 2), (dev, 2), (dv, 2 * (4 * 4 + 1))]
            with rounds(dve, 2, *every) as i:
                for b in range(2):
                    scan_chunk(b, i * 2 + (1 + b), True, ysb[b][:, bass.ds(i * DI, DI)])

            def split_lo_normed(slot):
                dve.wait_ge(hi["sem"], due(hi))
                for k in range(KT):
                    n = Q_SN + slot * KT + k
                    last = dve.scalar_tensor_tensor(wlo[:, slot, k], raw[:, slot, k], colp[:, n:n + 1],
                                                    whi[:, slot, k].bitcast(F32), ALU.mult, ALU.subtract)
                last.then_inc(lo["sem"], step(lo))

            split_lo_normed(0)
            for y in (yh, yl):
                dve.memset(y[:, :, CTX:CTX + 2].bitcast(F32), 0.0)
                last = dve.memset(y[:, :, NCONV:TP].bitcast(F32), 0.0)
            yhi, yok = count(s["y_hi"]), count(s["y_ok"])
            for t in range(NT):
                for j in range(4):
                    dve.wait_ge(yhi["sem"], due(yhi))
                    part = (slice(4 * j, 4 * j + 4), slice(tok(t), tok(t) + P))
                    dve.tensor_tensor(yl[:, part[0], part[1]], tp[:, j].rearrange("p (n t) -> p n t", t=P),
                                      yh[:, part[0], part[1]].bitcast(F32), ALU.subtract).then_inc(yok["sem"], step(yok))
                if t == 0:
                    split_lo_normed(1)
            jump(ready, U_SO)
            jump(free, U_SO)
            gm, msum, mhi, mok = count(s["gm_in"], 16), count(s["merge_sum"]), count(s["merge_hi"]), count(s["merge_ok"])

            def merge_round(i, split):
                split(0)
                for b in range(2):
                    dve.wait_ge(ready["sem"], due(ready))
                    if b == 1:
                        split(1)
                    step(gm, 2)
                    dve.wait_ge(gm["sem"], value(gm))
                    dve.tensor_tensor(both(mrg), acc[:, 2 * b:2 * b + 2, 0:HALF], both(gbt), ALU.mult).then_inc(free["sem"], step(free))
                    dve.wait_ge(free["sem"], value(free))
                    dve.tensor_tensor(mrg, mrg, m1t, ALU.add).then_inc(msum["sem"], step(msum))
                    dve.wait_ge(mhi["sem"], due(mhi))
                    k = lambda t: t[:, bass.ds(i * 2 + b, 1)].rearrange("p o t -> p (o t)")
                    dve.tensor_tensor(k(hl), mrg, k(hh).bitcast(F32), ALU.subtract).then_inc(mok["sem"], step(mok))
                    dve.wait_ge(mok["sem"], value(mok))

            with rounds(dve, 3, (ready, 2), (free, 2), (hi, 2), (lo, 2), (gm, 4), (msum, 2), (mhi, 2), (mok, 2)) as i:
                merge_round(i, split_lo_normed)
            merge_round(3, split_lo)

            dve.wait_ge(s["g1_in"], 32)

            def with_x(t, b):
                cols = slice(b * BW, (b + 1) * BW)
                do(dve.scalar_tensor_tensor(x1[:, t, cols], xo[:, t, cols], ALPHA, x1[:, t, cols], ALU.mult, ALU.add))
                dve.bn_stats(st6[:, t, b], x1[:, t, cols])

            for b in range(4):
                cols = slice(b * BW, (b + 1) * BW)
                if b == 2:
                    dve.wait_ge(s["rows2_in"], 16 * 5)
                for t in range(NT):
                    dve.wait_ge(ready["sem"], due(ready))
                    dve.tensor_tensor(x1[:, t, cols], acc[:, 2 * ((NT * b + t) % 2), 0:BW],
                                      g1r[:, min(t, 1), cols], ALU.mult).then_inc(free["sem"], step(free))
                    if b >= 2:
                        dve.wait_ge(free["sem"], value(free))
                        with_x(t, b - 2)
                        with_x(t, b)
                split_lo(b % 2)
            for buf in (hf2[:, :, CTX:CTX + 2], hf2[:, :, NCONV:TP]):
                last = dve.memset(buf, 0.0)
            last.then_inc(s["pad_ok"], 1)
            for t in range(NT):
                gathered(t)
            deviations()
            for t in range(NT):
                do(weighed(t, x1[:, t], lnr))
                statistics(t, x1[:, t])
            deviations()
            for t in range(NT):
                normed(t, xq[:, t], x1[:, t]).then_inc(s["x1_ok"], 1)
            for t in range(NT):
                do(dve.tensor_copy(xo[:, t], row))
            split_h(hf2, "h2_hi", "h2_ok")

            relu, sq, ff = count(s["relu_ok"]), count(s["square_ok"]), count(s["ff_ok"])
            jump(ready, U_MLP)
            jump(free, U_MLP)
            sqb = row[:, 0:TP]
            dve.wait_ge(s["h2_ok"], KT)
            dve.wait_ge(s["x1_ok"], NT)

            def mlp_round(i, last_round):
                for n in range(KT):
                    dve.wait_ge(ready["sem"], due(ready))
                    r = hf2[:, n % 2]
                    b1 = colp[:, bass.ds(i * KT + (Q_B1 + n), 1)]
                    dve.tensor_scalar(both(r), acc[:, 2 * (n % 2):2 * (n % 2) + 2, 0:HALF], b1, 0.0, ALU.add, ALU.max).then_inc(free["sem"], step(free))
                    dve.wait_ge(free["sem"], value(free))
                    dve.tensor_tensor(sqb, r, r, ALU.mult).then_inc(relu["sem"], step(relu))
                    dve.wait_ge(relu["sem"], value(relu))
                    dve.wait_ge(sq["sem"], due(sq))
                    dve.tensor_tensor(fl[:, n], sqb, fh[:, n].bitcast(F32), ALU.subtract).then_inc(ff["sem"], step(ff))
                    if n % 2 == 1:
                        split_lo(n // 2 % 2)
                for b in range(4):
                    cols = slice(b * BW, (b + 1) * BW)
                    for t in range(NT):
                        dve.wait_ge(ready["sem"], due(ready))
                        dve.tensor_tensor(xo[:, t, cols], xo[:, t, cols], acc[:, 2 * ((NT * b + t) % 2), 0:BW],
                                          ALU.add).then_inc(free["sem"], step(free))
                        if last_round:
                            dve.wait_ge(free["sem"], value(free))
                            do(dve.tensor_tensor(xo[:, t, cols], xo[:, t, cols], g1r[:, min(t, 1), cols], ALU.mult))
                            do(dve.scalar_tensor_tensor(xo[:, t, cols], x1[:, t, cols], ALPHA, xo[:, t, cols],
                                                        ALU.mult, ALU.add))
                            dve.bn_stats(st6[:, t, b], xo[:, t, cols])
                    if b < 2 or not last_round:
                        split_lo(b % 2)

            with rounds(dve, 3, (ready, KT + 4 * NT), (free, KT + 4 * NT), (hi, 8), (lo, 8), (relu, KT), (sq, KT), (ff, KT)) as i:
                mlp_round(i, False)
            dve.wait_ge(s["rows2_in"], 16 * 7)
            mlp_round(3, True)

            dve.wait_ge(s["rows2_in"], 16 * 9)
            for t in range(NT):
                gathered(t)
            deviations()
            for t in range(NT):
                weighed(t, xo[:, t], lnr2).then_inc(s["final_ok"], 1)


_OUTS = [(1, CTX, D), (1, LAT, D), (1, 1, CTX, HKV, HD), (1, 1, CTX, HKV, HD), (1, 1, 2, NH, SP_, NS)]


def kernel(**inputs):
    import numpy as np
    import concourse.bacc as bacc
    from concourse.bass_utils import run_bass_kernel_spmd as run

    k, i = np.arange(P)[:, None], np.arange(P)[None, :]
    parts = [k == i, k <= i, k >= i, k > i, k < i, k >= 0 * i]
    t = np.arange(LAT)
    pos = np.stack([t // GRID_W, t % GRID_W], -1).astype(np.float32)
    inv = (np.float32(ROPE_THETA) ** (-np.arange(HD // 4, dtype=np.float32) / np.float32(HD // 4))).astype(np.float32)
    ang = pos[:, :, None] * inv
    cos, sin = np.cos(ang), np.sin(ang)
    table = lambda a, b: np.stack([a, b], 2).reshape(LAT // P, P, HD).transpose(1, 0, 2).reshape(P, -1)
    consts = np.concatenate([p.astype(np.float32) for p in parts] + [table(cos, cos), table(-sin, sin)], 1).astype(np.float32)

    nc = bacc.Bacc("TRN2", target_bir_lowering=False, num_devices=1)
    arrays, args = {}, {}
    for name, v in list(inputs.items()) + [("consts", consts)]:
        v = np.ascontiguousarray(v)
        arrays[f"in_{name}"] = v
        args[name] = nc.dram_tensor(f"in_{name}", v.shape, mybir.dt.from_np(v.dtype), kind="ExternalInput").ap()
    outs = [nc.dram_tensor(f"out_{n}", shape, F32, kind="ExternalOutput").ap() for n, shape in enumerate(_OUTS)]
    build(nc, args, outs)
    r = run(nc, [arrays], core_ids=[0])
    return tuple(r.results[0][f"out_{n}"] for n in range(len(_OUTS)))
```
